# Optimizing a Trainium2 kernel written in Bass

```python
import math
import jax, jax.numpy as jnp
from jax import lax
import numpy as np

D_MODEL = 1024
BATCH = 1
SEQ = 1024
DEPTH = 1

N_META = 16
NORM_EPS = 1e-6

RWKV_HEADS = 16
RWKV_HEAD_DIM = 64
RWKV_WIDTH = RWKV_HEADS * RWKV_HEAD_DIM
DECAY_LORA = 64
AAA_LORA = 64
GATE_LORA = 128
RWKV_GN_EPS = 64e-5
RWKV_COLS = 3 * RWKV_WIDTH + DECAY_LORA + AAA_LORA + GATE_LORA

DIFF_HEADS = 8
DIFF_HEAD_DIM = 64
DIFF_V_DIM = 2 * DIFF_HEAD_DIM
DIFF_QK_WIDTH = DIFF_HEADS * 2 * DIFF_HEAD_DIM
DIFF_V_WIDTH = DIFF_HEADS * DIFF_V_DIM
DIFF_COLS = 2 * DIFF_QK_WIDTH + DIFF_V_WIDTH
ROPE_THETA = 500000.0
ROPE_DIM = DIFF_HEAD_DIM // 4
Q_BLOCK = 128

GATE_COLS = 2 * D_MODEL
IN_COLS = RWKV_COLS + DIFF_COLS + GATE_COLS

N_GROUPS = 4
EXPERTS_PER_GROUP = 8
N_EXPERTS = N_GROUPS * EXPERTS_PER_GROUP
TOP_K = 2
EXPERT_FF = 512
MOE_BLOCK = 128

kernel_name = 'hybrid_rwkv7_diffattn_hmoe'

def rms_norm(x, w, eps=NORM_EPS):
    xf = x.astype(jnp.float32)
    y = xf * lax.rsqrt(jnp.mean(xf * xf, axis=-1, keepdims=True) + eps)
    return (y * w.astype(jnp.float32)).astype(x.dtype)

def token_shift(p):
    return jnp.pad(p, ((0, 0), (1, 0), (0, 0)))[:, :-1]

def partial_rope(t, pos):
    half = ROPE_DIM // 2
    inv_freq = jnp.exp(-math.log(ROPE_THETA) * jnp.arange(half, dtype=jnp.float32) * 2.0 / ROPE_DIM)
    ang = pos.astype(jnp.float32)[:, None] * inv_freq[None, :]
    cos = jnp.cos(ang)[None, :, None, None, :]
    sin = jnp.sin(ang)[None, :, None, None, :]
    tf = t.astype(jnp.float32)
    x1 = tf[..., :half]
    x2 = tf[..., half:ROPE_DIM]
    out = jnp.concatenate([x1 * cos - x2 * sin, x2 * cos + x1 * sin, tf[..., ROPE_DIM:]], axis=-1)
    return out.astype(t.dtype)

def rwkv7_time_mix(p, mu, w0, w2, a0, a2, g2, k_k, k_a, r_k, ln_w, ln_b):
    bsz, length, _ = p.shape
    f32 = jnp.float32
    p = p + (token_shift(p) - p) * mu
    c0 = RWKV_WIDTH
    c1 = 2 * RWKV_WIDTH
    c2 = 3 * RWKV_WIDTH
    c3 = c2 + DECAY_LORA
    c4 = c3 + AAA_LORA
    r, k, v = p[..., :c0], p[..., c0:c1], p[..., c1:c2]
    xw, xa, xg = p[..., c2:c3], p[..., c3:c4], p[..., c4:]
    w_log = -jax.nn.softplus(-(w0 + jnp.tanh(xw) @ w2).astype(f32)) - 0.5
    decay = jnp.exp(-jnp.exp(w_log))
    a = jax.nn.sigmoid((a0 + xa @ a2).astype(f32))
    g = jax.nn.sigmoid(xg) @ g2
    heads = lambda t: t.astype(f32).reshape(bsz, length, RWKV_HEADS, RWKV_HEAD_DIM)
    kk = heads(k * k_k)
    kk = kk / jnp.maximum(jnp.sqrt(jnp.sum(kk * kk, axis=-1, keepdims=True)), 1e-12)
    k = k.astype(f32) * (1.0 + (a - 1.0) * k_a.astype(f32))
    r, k, v, a, decay = heads(r), heads(k), heads(v), heads(a), heads(decay)

    def step(state, inp):
        r_t, w_t, k_t, v_t, kk_t, a_t = inp
        sa = jnp.einsum('bhvk,bhk->bhv', state, -kk_t)
        state = (state * w_t[:, :, None, :]
                 + sa[..., None] * (kk_t * a_t)[:, :, None, :]
                 + v_t[..., None] * k_t[:, :, None, :])
        return state, jnp.einsum('bhvk,bhk->bhv', state, r_t)

    seq_first = lambda t: jnp.moveaxis(t, 1, 0)
    s0 = jnp.zeros((bsz, RWKV_HEADS, RWKV_HEAD_DIM, RWKV_HEAD_DIM), f32)
    _, y = lax.scan(step, s0, tuple(map(seq_first, (r, decay, k, v, kk, a))))
    y = jnp.moveaxis(y, 0, 1)
    mean = jnp.mean(y, axis=-1, keepdims=True)
    var = jnp.mean(jnp.square(y - mean), axis=-1, keepdims=True)
    yn = ((y - mean) * lax.rsqrt(var + RWKV_GN_EPS)).reshape(bsz, length, RWKV_WIDTH)
    yn = yn * ln_w.astype(f32) + ln_b.astype(f32)
    bonus = (jnp.sum(r * k * r_k.astype(f32), axis=-1, keepdims=True) * v).reshape(bsz, length, RWKV_WIDTH)
    return ((yn + bonus) * g.astype(f32)).astype(p.dtype)

def diff_attention(p, pos, q_norm_w, k_norm_w, lq1, lk1, lq2, lk2, subln_w, lambda_init):
    bsz, length, _ = p.shape
    f32 = jnp.float32
    q = p[..., :DIFF_QK_WIDTH].reshape(bsz, length, DIFF_HEADS, 2, DIFF_HEAD_DIM)
    k = p[..., DIFF_QK_WIDTH:2 * DIFF_QK_WIDTH].reshape(bsz, length, DIFF_HEADS, 2, DIFF_HEAD_DIM)
    v = p[..., 2 * DIFF_QK_WIDTH:].reshape(bsz, length, DIFF_HEADS, DIFF_V_DIM)
    q = partial_rope(rms_norm(q, q_norm_w), pos)
    k = partial_rope(rms_norm(k, k_norm_w), pos)
    lam = (jnp.exp(jnp.sum(lq1.astype(f32) * lk1.astype(f32)))
           - jnp.exp(jnp.sum(lq2.astype(f32) * lk2.astype(f32))) + lambda_init)
    scale = DIFF_HEAD_DIM ** -0.5
    bounds = [(0, N_META)] + [(s, min(s + Q_BLOCK, length)) for s in range(N_META, length, Q_BLOCK)]
    outs = []
    for s, e in bounds:
        qb = q[:, s:e]
        kb = k[:, :e]
        vb = v[:, :e]
        sc = jnp.einsum('bqhcd,bkhcd->bhcqk', qb, kb, preferred_element_type=f32) * scale
        mask = jnp.arange(e)[None, :] <= jnp.arange(s, e)[:, None]
        pr = jax.nn.softmax(jnp.where(mask, sc, -jnp.inf), axis=-1)
        att = pr[:, :, 0] - lam * pr[:, :, 1]
        outs.append(jnp.einsum('bhqk,bkhe->bqhe', att.astype(vb.dtype), vb))
    o = jnp.concatenate(outs, axis=1)
    o = rms_norm(o, subln_w) * (1.0 - lambda_init)
    return o.reshape(bsz, length, DIFF_V_WIDTH)

def hierarchical_moe(x, wg, bg, we, be, w_gate, w_up, w_down):
    n_tok, d = x.shape
    f32 = jnp.float32
    g_prob = jax.nn.softmax((x @ wg).astype(f32) + bg.astype(f32), axis=-1)
    g_val, g_idx = lax.top_k(g_prob, 1)
    e_logits = ((x @ we).astype(f32) + be.astype(f32)).reshape(n_tok, N_GROUPS, EXPERTS_PER_GROUP)
    e_logits = jnp.take_along_axis(e_logits, g_idx[:, :, None], axis=1)[:, 0]
    e_prob = jax.nn.softmax(e_logits, axis=-1)
    e_val, e_idx = lax.top_k(e_prob, TOP_K)
    gate = g_val * e_val / jnp.sum(e_val, axis=-1, keepdims=True)
    expert_id = g_idx * EXPERTS_PER_GROUP + e_idx
    n_assign = n_tok * TOP_K
    flat_e = expert_id.reshape(n_assign)
    flat_t = jnp.repeat(jnp.arange(n_tok, dtype=jnp.int32), TOP_K)
    flat_g = gate.reshape(n_assign)
    order = jnp.argsort(flat_e)
    se = flat_e[order]
    counts = jnp.bincount(flat_e, length=N_EXPERTS)
    padded = (counts + MOE_BLOCK - 1) // MOE_BLOCK * MOE_BLOCK
    pad_end = jnp.cumsum(padded)
    pad_start = pad_end - padded
    start = jnp.cumsum(counts) - counts
    dest = pad_start[se] + jnp.arange(n_assign) - start[se]
    n_blocks = -(-n_assign // MOE_BLOCK) + N_EXPERTS
    cap = n_blocks * MOE_BLOCK
    buf_t = jnp.full((cap,), n_tok, jnp.int32).at[dest].set(flat_t[order])
    buf_g = jnp.zeros((cap,), f32).at[dest].set(flat_g[order])
    block_e = jnp.minimum(jnp.searchsorted(pad_end, jnp.arange(n_blocks) * MOE_BLOCK, side='right'),
                          N_EXPERTS - 1)
    xp = jnp.concatenate([x, jnp.zeros((1, d), x.dtype)], axis=0)
    xb = xp[buf_t].reshape(n_blocks, MOE_BLOCK, d)

    def expert_block(args):
        xblk, e = args
        hid = jax.nn.silu(xblk @ w_gate[e]) * (xblk @ w_up[e])
        return hid @ w_down[e]

    yb = lax.map(expert_block, (xb, block_e))
    y = jnp.zeros((n_tok + 1, d), f32).at[buf_t].add(yb.reshape(cap, d).astype(f32) * buf_g[:, None])
    return y[:n_tok].astype(x.dtype)

def setup_inputs(seed: int = 0) -> dict:
    key = jax.random.key(seed)
    ks = iter(jax.random.split(key, 40))
    f32 = jnp.float32

    def nrm(shape, scale):
        return jax.random.normal(next(ks), shape, f32) * scale

    def gain(shape):
        return 1.0 + nrm(shape, 0.02)

    return {
        'x': nrm((BATCH, SEQ, D_MODEL), 1.0),
        'meta_tokens': nrm((N_META, D_MODEL), 1.0),
        'norm1_w': gain((DEPTH, D_MODEL)),
        'w_in': nrm((DEPTH, D_MODEL, IN_COLS), D_MODEL ** -0.5),
        'rwkv_mu': jax.random.uniform(next(ks), (DEPTH, RWKV_COLS), f32),
        'rwkv_w0': -1.5 + nrm((DEPTH, RWKV_WIDTH), 1.0),
        'rwkv_w2': nrm((DEPTH, DECAY_LORA, RWKV_WIDTH), 0.1 * DECAY_LORA ** -0.5),
        'rwkv_a0': nrm((DEPTH, RWKV_WIDTH), 0.5),
        'rwkv_a2': nrm((DEPTH, AAA_LORA, RWKV_WIDTH), 0.5 * AAA_LORA ** -0.5),
        'rwkv_g2': nrm((DEPTH, GATE_LORA, RWKV_WIDTH), GATE_LORA ** -0.5),
        'rwkv_k_k': 0.85 + nrm((DEPTH, RWKV_WIDTH), 0.05),
        'rwkv_k_a': 1.0 + nrm((DEPTH, RWKV_WIDTH), 0.05),
        'rwkv_r_k': nrm((DEPTH, RWKV_HEADS, RWKV_HEAD_DIM), 0.1),
        'rwkv_ln_w': gain((DEPTH, RWKV_WIDTH)),
        'rwkv_ln_b': nrm((DEPTH, RWKV_WIDTH), 0.02),
        'q_norm_w': gain((DEPTH, DIFF_HEAD_DIM)),
        'k_norm_w': gain((DEPTH, DIFF_HEAD_DIM)),
        'lambda_q1': nrm((DEPTH, DIFF_HEAD_DIM), 0.1),
        'lambda_k1': nrm((DEPTH, DIFF_HEAD_DIM), 0.1),
        'lambda_q2': nrm((DEPTH, DIFF_HEAD_DIM), 0.1),
        'lambda_k2': nrm((DEPTH, DIFF_HEAD_DIM), 0.1),
        'diff_subln_w': gain((DEPTH, DIFF_V_DIM)),
        'w_branch_rwkv': nrm((DEPTH, RWKV_WIDTH, D_MODEL), RWKV_WIDTH ** -0.5),
        'w_branch_diff': nrm((DEPTH, DIFF_V_WIDTH, D_MODEL), DIFF_V_WIDTH ** -0.5),
        'w_out': nrm((DEPTH, D_MODEL, D_MODEL), D_MODEL ** -0.5),
        'norm2_w': gain((DEPTH, D_MODEL)),
        'router_group_w': nrm((DEPTH, D_MODEL, N_GROUPS), D_MODEL ** -0.5),
        'router_group_b': nrm((DEPTH, N_GROUPS), 0.01),
        'router_expert_w': nrm((DEPTH, D_MODEL, N_EXPERTS), D_MODEL ** -0.5),
        'router_expert_b': nrm((DEPTH, N_EXPERTS), 0.01),
        'expert_w_gate': nrm((DEPTH, N_EXPERTS, D_MODEL, EXPERT_FF), D_MODEL ** -0.5),
        'expert_w_up': nrm((DEPTH, N_EXPERTS, D_MODEL, EXPERT_FF), D_MODEL ** -0.5),
        'expert_w_down': nrm((DEPTH, N_EXPERTS, EXPERT_FF, D_MODEL), EXPERT_FF ** -0.5),
    }

def reference(x, meta_tokens, norm1_w, w_in, rwkv_mu, rwkv_w0, rwkv_w2, rwkv_a0, rwkv_a2, rwkv_g2,
              rwkv_k_k, rwkv_k_a, rwkv_r_k, rwkv_ln_w, rwkv_ln_b, q_norm_w, k_norm_w,
              lambda_q1, lambda_k1, lambda_q2, lambda_k2, diff_subln_w, w_branch_rwkv, w_branch_diff,
              w_out, norm2_w, router_group_w, router_group_b, router_expert_w, router_expert_b,
              expert_w_gate, expert_w_up, expert_w_down):
    bsz = x.shape[0]
    meta = jnp.broadcast_to(meta_tokens[None].astype(x.dtype), (bsz, N_META, D_MODEL))
    h = jnp.concatenate([meta, x], axis=1)
    length = h.shape[1]
    pos = jnp.arange(length)
    for l in range(DEPTH):
        lambda_init = 0.8 - 0.6 * math.exp(-0.3 * l)
        u = rms_norm(h, norm1_w[l])
        proj = u @ w_in[l]
        p_rwkv = proj[..., :RWKV_COLS]
        p_diff = proj[..., RWKV_COLS:RWKV_COLS + DIFF_COLS]
        gates = jax.nn.sigmoid(proj[..., RWKV_COLS + DIFF_COLS:])
        y_rwkv = rwkv7_time_mix(p_rwkv, rwkv_mu[l], rwkv_w0[l], rwkv_w2[l], rwkv_a0[l], rwkv_a2[l],
                                rwkv_g2[l], rwkv_k_k[l], rwkv_k_a[l], rwkv_r_k[l],
                                rwkv_ln_w[l], rwkv_ln_b[l]) @ w_branch_rwkv[l]
        y_diff = diff_attention(p_diff, pos, q_norm_w[l], k_norm_w[l], lambda_q1[l], lambda_k1[l],
                                lambda_q2[l], lambda_k2[l], diff_subln_w[l], lambda_init) @ w_branch_diff[l]
        merged = gates[..., :D_MODEL] * y_rwkv + gates[..., D_MODEL:] * y_diff
        h = h + merged @ w_out[l]
        u2 = rms_norm(h, norm2_w[l]).reshape(-1, D_MODEL)
        h = h + hierarchical_moe(u2, router_group_w[l], router_group_b[l], router_expert_w[l],
                                 router_expert_b[l], expert_w_gate[l], expert_w_up[l],
                                 expert_w_down[l]).reshape(h.shape)
    return h[:, N_META:]


_drawn_inputs = setup_inputs


def setup_inputs(seed=0):
    import zlib

    import numpy as np

    out = dict(_drawn_inputs(seed))
    spreads = {}
    factors = {'rwkv_w2': 4.118,
     'rwkv_k_k': 12.218,
     'rwkv_ln_w': 12.777,
     'rwkv_ln_b': 13.079,
     'k_norm_w': 2.696,
     'lambda_k1': 3.036,
     'lambda_q2': 3.13,
     'lambda_k2': 3.5,
     'diff_subln_w': 9.53,
     'router_group_b': 19.109,
     'router_expert_b': 12.827,
     'norm2_w': 3.403}
    for name, (base, spread) in spreads.items():
        noise = np.random.default_rng([zlib.crc32(name.encode()), seed]).standard_normal(out[name].shape)
        drawn = base * np.exp(spread * noise) if base else spread * noise
        out[name] = __import__('jax').numpy.asarray(drawn.astype(out[name].dtype))
    for name, factor in factors.items():
        out[name] = (out[name] * factor).astype(out[name].dtype)
    return out
```

```python
import math
from contextlib import ExitStack

import numpy as np
import concourse.bass as bass
from concourse import mybir

F32 = mybir.dt.float32
I32 = mybir.dt.int32
U32 = mybir.dt.uint32
ALU = mybir.AluOpType
ACT = mybir.ActivationFunctionType
AX = mybir.AxisListType

META, SEQ, D = 16, 1024, 1024
T = META + SEQ
TT = 104
NT = T // TT
KD = D // 128
EPS = 1e-6
RH, RD = 16, 64
LW, LA, LG = 64, 64, 128
RWKV_COLS = 3 * D + LW + LA + LG
RT = RWKV_COLS // 128
GT = 2 * D // 128
DH, DD = 8, 64
DIFF_COL = RWKV_COLS
GATE_COL = RWKV_COLS + 3 * D
ROPE, THETA = DD // 4, 500000.0
OPEN = 16
NCOL = 4
CW = T // NCOL


class Shared:
    pass


class Chain:

    def __init__(self, eng, sem, start=0):
        self.eng, self.sem, self.n = eng, sem, start

    def __call__(self, ins):
        self.n += 1
        ins.then_inc(self.sem, 1)
        self.eng.wait_ge(self.sem, self.n + OPEN)


def scope(nc, st):
    def sb(name, shape, dt=F32):
        return st.enter_context(nc.sbuf_tensor(name, shape, dt))

    def ps(name, shape):
        return st.enter_context(nc.psum_tensor(name, shape, F32))

    sems = []

    def sem(name, first=OPEN):
        sems.append((nc.alloc_semaphore(name), first))
        return sems[-1][0]

    def begin():
        for x, first in sems:
            if first:
                nc.gpsimd.sem_inc(x, first)
        nc.all_engine_barrier()
        return st.enter_context(nc.Block())

    st.callback(lambda: nc.clear_and_free_semaphores([x for x, _ in sems]))
    return sb, ps, sem, begin


def constants(nc, c):
    with ExitStack() as st:
        sb, ps, sem, begin = scope(nc, st)
        zeroed = sem("ident_zeroed")
        block = begin()

        @block.gpsimd
        def _(pool):
            nc.gpsimd.memset(c.eps[:], EPS).then_inc(zeroed, 1)
            nc.gpsimd.memset(c.ident[:], 0.0).then_inc(zeroed, 1)
            pool.wait_ge(zeroed, 2 + OPEN)
            nc.gpsimd.affine_select(out=c.ident[:], in_=c.ident[:], compare_op=ALU.not_equal, fill=1.0,
                                    base=0, pattern=[[-1, 128]], channel_multiplier=1).then_inc(zeroed, 1)
            pool.wait_ge(zeroed, 3 + OPEN)


def norm1(nc, c):
    with ExitStack() as st:
        sb, ps, sem, begin = scope(nc, st)
        h = sb("n1_h", [TT, 2, D])
        sq = sb("n1_sq", [TT, D])
        ms = sb("n1_ms", [TT, 2])
        rs = sb("n1_rs", [TT, 2])
        ri = sb("n1_ri", [TT, 2])
        u = sb("n1_u", [TT, 2, D])
        w = sb("n1_w", [128, KD])
        pt = ps("n1_pt", [128, 2, 2, 512])
        w_in = sem("n1_w_in")
        h_in = [sem(f"n1_h_in{s}") for s in range(2)]
        h_used = sem("n1_h_used")
        sq_done = sem("n1_sq_done")
        u_done = sem("n1_u_done")
        t_done = sem("n1_t_done")
        uT_done = sem("n1_uT_done")
        rs_done = sem("n1_rs_done")
        vec = sem("n1_vec")
        block = begin()

        @block.sync
        def _(sp):
            sp.dma_start(w[:], c.norm1_w.rearrange("o (p k) -> p (o k)", k=KD)).then_inc(w_in, 16)
            sp.dma_start(h[0:META, 0, :], c.meta_tokens).then_inc(h_in[0], 16)
            sp.dma_start(h[META:TT, 0, :], c.x[0, 0:TT - META, :]).then_inc(h_in[0], 16)
            sp.dma_start(h[:, 1, :], c.x[0, TT - META:2 * TT - META, :]).then_inc(h_in[1], 16)
            with sp.Fori(1, NT // 2) as i:
                for s in range(2):
                    sp.wait_ge(h_used, 2 * i + s - 1 + OPEN)
                    sp.dma_start(h[:, s, :], c.x[0, bass.ds((2 * i + s) * TT - META, TT), :]).then_inc(h_in[s], 16)

        @block.scalar
        def _(act):
            with act.Fori(0, NT // 2) as i:
                for s in range(2):
                    act.wait_ge(h_in[s], 16 * i + (32 if s == 0 else 16) + OPEN)
                    nc.scalar.activation(sq[:], h[:, s, :], ACT.Square,
                                         accum_out=ms[:, s:s + 1]).then_inc(sq_done, 1)
                    act.wait_ge(sq_done, 2 * i + s + 1 + OPEN)
                    nc.scalar.activation(rs[:, s:s + 1], ms[:, s:s + 1], ACT.Sqrt, bias=c.eps[0:TT, :],
                                         scale=1.0 / D).then_inc(rs_done, 1)

        @block.vector
        def _(dve):
            dve.wait_ge(w_in, 16 + OPEN)
            with dve.Fori(0, NT // 2) as i:
                for s in range(2):
                    dve.wait_ge(rs_done, 2 * i + s + 1 + OPEN)
                    nc.vector.reciprocal(ri[:, s:s + 1], rs[:, s:s + 1]).then_inc(vec, 1)
                    dve.wait_ge(vec, 2 * i + s + 1 + OPEN)
                    dve.wait_ge(t_done, 2 * i + s + OPEN)
                    nc.vector.tensor_scalar(u[:, s, :], h[:, s, :], ri[:, s:s + 1], None, ALU.mult).then_inc(u_done, 1)
                    dve.wait_ge(u_done, 2 * i + s + 1 + OPEN)
                    dve.sem_inc(h_used, 1)
                    dve.wait_ge(t_done, 2 * i + s + 1 + OPEN)
                    for b in range(2):
                        ins = nc.vector.tensor_tensor(
                            c.uT[:, 4 * b:4 * b + 4, bass.ds((2 * i + s) * TT, TT)],
                            pt[:, s, b, 0:4 * TT].rearrange("p (k t) -> p k t", k=4),
                            w[:, 4 * b:4 * b + 4].unsqueeze(2).to_broadcast([128, 4, TT]), ALU.mult)
                        ins.then_inc(uT_done, 1)
            dve.wait_ge(uT_done, 2 * NT + OPEN)

        @block.tensor
        def _(pe):
            with pe.Fori(0, NT // 2) as i:
                for s in range(2):
                    pe.wait_ge(u_done, 2 * i + s + 1 + OPEN)
                    if s == 1:
                        pe.wait_ge(uT_done, 4 * i + OPEN)
                    else:
                        pe.wait_ge(uT_done, 4 * i + OPEN)
                    for k in range(KD):
                        last = nc.tensor.transpose(pt[:, s, k // 4, (k % 4) * TT:(k % 4 + 1) * TT],
                                                   u[:, s, k::KD], c.ident[0:TT, 0:TT])
                    last.then_inc(t_done, 1)


def project_features(nc, c):
    with ExitStack() as st:
        sb, ps, sem, begin = scope(nc, st)
        w = sb("pf_w", [128, 2, KD, 128])
        ev = sb("pf_ev", [128, 2, T])
        acc = ps("pf_acc", [128, 2, NCOL, 512])
        w_ready = [sem(f"pf_w_ready{s}") for s in range(2)]
        product = [sem(f"pf_product{s}") for s in range(2)]
        copied = [sem(f"pf_copied{s}") for s in range(2)]
        stored = [sem(f"pf_stored{s}") for s in range(2)]
        zero = sb("pf_zero", [SLOTS, D])
        zeroed = sem("pf_zeroed")
        cleared = sem("pf_cleared")
        w_v = c.w_in.rearrange("o (p k) f -> p (o k) f", k=KD)
        block = begin()
        RI, GI = RT // 2, GT // 2

        @block.gpsimd
        def _(pool):
            nc.gpsimd.memset(zero[:], 0.0).then_inc(zeroed, 1)

        @block.sync
        def _(sp):
            for s in range(2):
                sp.dma_start(w[:, s], w_v[:, :, s * 128:s * 128 + 128]).then_inc(w_ready[s], 16)
            sp.wait_ge(zeroed, 1 + OPEN)
            with sp.Fori(NE, NBLK) as n:
                sp.dma_start(c.yD[bass.ds(n * SLOTS, SLOTS), :], zero[:]).then_inc(cleared, 16)
            for lo, hi, shift in ((1, RI, 0), (RI, RI + GI, GATE_COL - RWKV_COLS)):
                with sp.Fori(lo, hi) as i:
                    for s in range(2):
                        sp.wait_ge(product[s], i + OPEN)
                        sp.dma_start(w[:, s], w_v[:, :, bass.ds((2 * i + s) * 128 + shift, 128)]).then_inc(w_ready[s], 16)
            sp.wait_ge(cleared, 16 * OVER + OPEN)

        @block.tensor
        def _(pe):
            with pe.Fori(0, RI + GI) as i:
                for s in range(2):
                    pe.wait_ge(w_ready[s], 16 * i + 16 + OPEN)
                    pe.wait_ge(copied[s], i + OPEN)
                    for k in range(KD):
                        for n in range(NCOL):
                            last = nc.tensor.matmul(acc[:, s, n, 0:CW], w[:, s, k, :],
                                                    c.uT[:, k, n * CW:(n + 1) * CW],
                                                    start=(k == 0), stop=(k == KD - 1))
                    last.then_inc(product[s], 1)

        def read_out(eng, s, i):
            eng.wait_ge(product[s], i + 1 + OPEN)
            eng.wait_ge(stored[s], 16 * i + OPEN)

        @block.scalar
        def _(act):
            with act.Fori(0, RI + GI) as i:
                read_out(act, 0, i)
                nc.scalar.copy(ev[:, 0, :].rearrange("p (n t) -> p n t", n=NCOL),
                               acc[:, 0, :, 0:CW]).then_inc(copied[0], 1)
                for s in range(2):
                    act.wait_ge(copied[s], i + 1 + OPEN)
                    act.dma_start(c.pT[bass.ds(2 * i + s, 1)].rearrange("o p t -> (o p) t"),
                                  ev[:, s, :]).then_inc(stored[s], 16)
            for s in range(2):
                act.wait_ge(stored[s], 16 * (RI + GI) + OPEN)

        @block.vector
        def _(dve):
            with dve.Fori(0, RI + GI) as i:
                read_out(dve, 1, i)
                nc.vector.tensor_copy(ev[:, 1, :].rearrange("p (n t) -> p n t", n=NCOL),
                                      acc[:, 1, :, 0:CW]).then_inc(copied[1], 1)


def project_heads(nc, c):
    NB = 2 * D // 512
    G = 512 // DD
    with ExitStack() as st:
        sb, ps, sem, begin = scope(nc, st)
        w = sb("ph_w", [128, 2, KD, 512])
        nw = sb("ph_norm_w", [TT, 2, DD])
        cos = sb("ph_cos", [TT, NT, ROPE])
        sin = sb("ph_sin", [TT, NT, ROPE])
        sq = sb("ph_sq", [TT, 2, 512])
        ms = sb("ph_ms", [TT, 2, G])
        rs = sb("ph_rs", [TT, 2, G])
        ri = sb("ph_ri", [TT, 2, G])
        qn = sb("ph_qn", [TT, 2, 512])
        ra = sb("ph_ra", [TT, G, ROPE])
        rb = sb("ph_rb", [TT, G, ROPE])
        stg = sb("ph_stg", [128, 2, 4, T])
        vst = sb("ph_vst", [TT, 2, 512])
        acc = ps("ph_acc", [TT, 2, 512])
        tp = ps("ph_tp", [128, 2, 512])
        tables = sem("ph_tables")
        scaled = sem("ph_scaled")
        w_ready = [sem(f"ph_w_ready{s}") for s in range(2)]
        w_used = [sem(f"ph_w_used{s}") for s in range(2)]
        product = sem("ph_product")
        sq_done = sem("ph_sq_done")
        ms_done = sem("ph_ms_done")
        rs_done = sem("ph_rs_done")
        vec = sem("ph_vec")
        normed = sem("ph_normed")
        roped = sem("ph_roped")
        rope_step = sem("ph_rope_step")
        turned = sem("ph_turned")
        staged = sem("ph_staged")
        stored = [sem(f"ph_stored{s}") for s in range(2)]
        v_copied = sem("ph_v_copied")
        v_stored = [sem(f"ph_v_stored{s}") for s in range(2)]
        block = begin()
        w_v = c.w_in.rearrange("o (p k) f -> p (o k) f", k=KD)
        U = 2 * NT
        NI = NB // 2
        QK = NI * U

        @block.sync
        def _(sp):
            for j, src in enumerate((c.q_norm_w, c.k_norm_w)):
                sp.dma_start(nw[:, j, :], src.to_broadcast([TT, DD])).then_inc(tables, 16)
            sp.dma_start(cos[:], c.rope_cos).then_inc(tables, 16)
            sp.dma_start(sin[:], c.rope_sin).then_inc(tables, 16)
            for b in range(2):
                sp.dma_start(w[:, b], w_v[:, :, DIFF_COL + b * 512:DIFF_COL + (b + 1) * 512]).then_inc(w_ready[b], 16)
            with sp.Fori(1, NB // 2 + 1) as i:
                for b in range(2):
                    sp.wait_ge(w_used[b], i + OPEN)
                    sp.dma_start(w[:, b], w_v[:, :, bass.ds((2 * i + b) * 512 + DIFF_COL, 512)]).then_inc(w_ready[b], 16)

        def multiply(pe, b, t, slot):
            for k in range(KD):
                last = nc.tensor.matmul(acc[:, slot, :], c.uT[:, k, t * TT:(t + 1) * TT], w[:, b, k, :],
                                        start=(k == 0), stop=(k == KD - 1))
            last.then_inc(product, 1)

        @block.tensor
        def _(pe):
            def turn(i, u):
                pe.wait_ge(roped, U * i + u + 1 + OPEN)
                pe.wait_ge(staged, (U * i + u) // 1 - 1 + OPEN) if u >= 2 else pe.wait_ge(staged, U * i + OPEN)
                for k in range(4):
                    last = nc.tensor.transpose(tp[:, u % 2, k * TT:(k + 1) * TT],
                                               qn[:, u % 2, k * 128:(k + 1) * 128], c.ident[0:TT, 0:TT])
                last.then_inc(turned, 1)

            with pe.Fori(0, NI) as i:
                for u in range(U):
                    b, t = divmod(u, NT)
                    if t == 0:
                        pe.wait_ge(w_ready[b], 16 * i + 16 + OPEN)
                    pe.wait_ge(normed, U * i + u - 1 + OPEN) if u >= 2 else pe.wait_ge(normed, U * i + OPEN)
                    multiply(pe, b, t, u % 2)
                    if t == NT - 1:
                        pe.wait_ge(product, U * i + u + 1 + OPEN)
                        pe.sem_inc(w_used[b], 1)
                    if u >= 1:
                        turn(i, u - 1)
                turn(i, U - 1)
            pe.wait_ge(normed, QK + OPEN)
            for u in range(U):
                b, t = divmod(u, NT)
                if t == 0:
                    pe.wait_ge(w_ready[b], 16 * NI + 16 + OPEN)
                if u >= 2:
                    pe.wait_ge(v_copied, u - 1 + OPEN)
                multiply(pe, b, t, u % 2)

        @block.scalar
        def _(act):
            def stage(i, u):
                b, t = divmod(u, NT)
                act.wait_ge(turned, U * i + u + 1 + OPEN)
                if t == 0:
                    act.wait_ge(stored[b], 16 * i + OPEN)
                nc.scalar.copy(stg[:, b, :, t * TT:(t + 1) * TT],
                               tp[:, u % 2, 0:4 * TT].rearrange("p (k t) -> p k t", k=4)).then_inc(staged, 1)
                if t == NT - 1:
                    act.wait_ge(staged, U * i + u + 1 + OPEN)
                    act.dma_start(c.qkT[bass.ds(8 * i + 4 * b, 4)].rearrange("k p t -> p k t"),
                                  stg[:, b]).then_inc(stored[b], 16)

            with act.Fori(0, NI) as i:
                for u in range(U):
                    s = u % 2
                    act.wait_ge(product, U * i + u + 1 + OPEN)
                    nc.scalar.activation(sq[:, s, :], acc[:, s, :], ACT.Square).then_inc(sq_done, 1)
                    act.wait_ge(ms_done, U * i + u + 1 + OPEN)
                    nc.scalar.activation(rs[:, s, :], ms[:, s, :], ACT.Sqrt, bias=c.eps[0:TT, :],
                                         scale=1.0 / DD).then_inc(rs_done, 1)
                    if u >= 1:
                        stage(i, u - 1)
                stage(i, U - 1)
            for s in range(2):
                act.wait_ge(stored[s], 16 * NI + OPEN)
            for u in range(U):
                b, t = divmod(u, NT)
                act.wait_ge(product, QK + u + 1 + OPEN)
                if u >= 2:
                    act.wait_ge(v_stored[u % 2], 16 * (u // 2) + OPEN)
                nc.scalar.copy(vst[:, u % 2, :], acc[:, u % 2, :]).then_inc(v_copied, 1)
                act.wait_ge(v_copied, u + 1 + OPEN)
                act.dma_start(c.vD[t, :, b * 512:(b + 1) * 512], vst[:, u % 2, :]).then_inc(v_stored[u % 2], 16)
            for s in range(2):
                act.wait_ge(v_stored[s], 16 * (U // 2) + OPEN)

        @block.vector
        def _(dve):
            dve.wait_ge(tables, 64 + OPEN)
            nc.vector.tensor_scalar(nw[:, 0, :], nw[:, 0, :], DD ** -0.5, None, ALU.mult).then_inc(scaled, 1)
            dve.wait_ge(scaled, 1 + OPEN)
            for part in range(2):
                with dve.Fori(part * (NI // 2), (part + 1) * (NI // 2)) as i:
                    ch = Chain(dve, vec, 2 * U * i)
                    for u in range(U):
                        s = u % 2
                        dve.wait_ge(sq_done, U * i + u + 1 + OPEN)
                        nc.vector.tensor_reduce(ms[:, s, :], sq[:, s, :].rearrange("p (g d) -> p g d", g=G),
                                                AX.X, ALU.add).then_inc(ms_done, 1)
                        dve.wait_ge(rs_done, U * i + u + 1 + OPEN)
                        ch(nc.vector.reciprocal(ri[:, s, :], rs[:, s, :]))
                        if u >= 2:
                            dve.wait_ge(turned, U * i + u - 1 + OPEN)
                        else:
                            dve.wait_ge(turned, U * i + OPEN)
                        q3 = qn[:, s, :].rearrange("p (g d) -> p g d", g=G)
                        ch(nc.vector.tensor_tensor(q3, acc[:, s, :].rearrange("p (g d) -> p g d", g=G),
                                                   ri[:, s, :].unsqueeze(2).to_broadcast([TT, G, DD]), ALU.mult))
                        nc.vector.tensor_tensor(q3, q3, nw[:, part, :].unsqueeze(1).to_broadcast([TT, G, DD]),
                                                ALU.mult).then_inc(normed, 1)

        @block.gpsimd
        def _(pool):
            pool.wait_ge(tables, 64 + OPEN)
            with pool.Fori(0, NI) as i:
                ch = Chain(pool, rope_step, 3 * U * i)
                for u in range(U):
                    b, t = divmod(u, NT)
                    pool.wait_ge(normed, U * i + u + 1 + OPEN)
                    q3 = qn[:, u % 2, :].rearrange("p (g d) -> p g d", g=G)
                    h = ROPE // 2
                    cs = cos[:, t, :].unsqueeze(1).to_broadcast([TT, G, ROPE])
                    sn = sin[:, t, :].unsqueeze(1).to_broadcast([TT, G, ROPE])
                    ch(nc.gpsimd.tensor_tensor(ra[:], q3[:, :, 0:ROPE], cs, ALU.mult))
                    ch(nc.gpsimd.tensor_tensor(rb[:, :, 0:h], q3[:, :, h:ROPE], sn[:, :, 0:h], ALU.mult))
                    ch(nc.gpsimd.tensor_tensor(rb[:, :, h:ROPE], q3[:, :, 0:h], sn[:, :, h:ROPE], ALU.mult))
                    nc.gpsimd.tensor_tensor(q3[:, :, 0:ROPE], ra[:], rb[:], ALU.add).then_inc(roped, 1)
                    pool.wait_ge(roped, U * i + u + 1 + OPEN)


def attention(nc, c):
    with ExitStack() as st:
        sb, ps, sem, begin = scope(nc, st)
        q = sb("at_q", [128, 2, T])
        k = sb("at_k", [128, 2, T])
        v = sb("at_v", [TT, 2, NT, 128])
        mask = sb("at_mask", [TT, TT])
        lams = sb("at_lams", [TT, 4, DD])
        lj = sb("at_lj", [TT, 2, DD])
        ls = sb("at_ls", [TT, 2])
        le = sb("at_le", [TT, 2])
        nlam = sb("at_nlam", [TT, 1])
        nmx = sb("at_nmx", [TT, 2, 2])
        den = sb("at_den", [TT, 2, 2])
        rden = sb("at_rden", [TT, 2, 2])
        rel = sb("at_rel", [TT, 2])
        e = sb("at_e", [TT, 2, T])
        a = sb("at_a", [TT, 2, T])
        aT = sb("at_aT", [TT, 2, 4 * TT])
        o = sb("at_o", [TT, 2, 128])
        osq = sb("at_osq", [TT, 128])
        S = [ps(f"at_S{n}", [TT, 1536]) for n in range(2)]
        tp = ps("at_tp", [TT, 512])
        pv = ps("at_pv", [TT, 512])
        tables = sem("at_tables")
        lam_sum = sem("at_lam_sum")
        lam_exp = sem("at_lam_exp")
        vec = sem("at_vec")
        mask_made = sem("at_mask_made")
        loaded = [sem(f"at_loaded{s}") for s in range(2)]
        head_done = [sem(f"at_head_done{s}") for s in range(2)]
        scored = [sem(f"at_scored{n}") for n in range(2)]
        maxed = [sem(f"at_maxed{n}") for n in range(2)]
        exped = [sem(f"at_exped{n}") for n in range(2)]
        mixed = sem("at_mixed")
        turned = sem("at_turned")
        moved = sem("at_moved")
        pv_done = sem("at_pv_done")
        o_done = sem("at_o_done")
        squared = sem("at_squared")
        stored = [sem(f"at_stored{s}") for s in range(2)]
        block = begin()
        NI = DH // 2
        U = 2 * NT
        GR = [-(-(t + 1) // 4) for t in range(NT)]
        BEFORE = [sum(GR[u2 % NT] for u2 in range(u)) for u in range(U + 1)]
        NG = BEFORE[U]

        @block.sync
        def _(sp):
            for j, src in enumerate((c.lambda_q1, c.lambda_k1, c.lambda_q2, c.lambda_k2)):
                sp.dma_start(lams[:, j, :], src.to_broadcast([TT, DD])).then_inc(tables, 16)
            with sp.Fori(0, NI) as i:
                for s in range(2):
                    sp.wait_ge(head_done[s], i + OPEN)
                    sp.dma_start(q[:, s, :], c.qkT[bass.ds(2 * i + s, 1)].rearrange("o p t -> (o p) t")).then_inc(loaded[s], 16)
                    sp.dma_start(k[:, s, :], c.qkT[bass.ds(2 * i + s + DH, 1)].rearrange("o p t -> (o p) t")).then_inc(loaded[s], 16)
                    sp.dma_start(v[:, s], c.vD[:, :, bass.ds((2 * i + s) * 128, 128)].rearrange("n p d -> p n d")).then_inc(loaded[s], 16)

        @block.gpsimd
        def _(pool):
            nc.gpsimd.memset(mask[:], 0.0).then_inc(mask_made, 1)
            pool.wait_ge(mask_made, 1 + OPEN)
            nc.gpsimd.affine_select(out=mask[:], in_=mask[:], compare_op=ALU.is_ge, fill=-3.0e38,
                                    base=0, pattern=[[-1, TT]], channel_multiplier=1).then_inc(mask_made, 1)

        @block.tensor
        def _(pe):
            def scores(i, u):
                s, t = divmod(u, NT)
                if t == 0:
                    pe.wait_ge(loaded[s], 48 * i + 48 + OPEN)
                for n in range(2):
                    pe.wait_ge(exped[n], U * i + u + OPEN)
                    keys = (t + 1) * TT
                    for lo in range(0, keys, 512):
                        hi = min(lo + 512, keys)
                        last = nc.tensor.matmul(S[n][:, lo:hi], q[64 * n:64 * n + 64, s, t * TT:(t + 1) * TT],
                                                k[64 * n:64 * n + 64, s, lo:hi], start=True, stop=True)
                    last.then_inc(scored[n], 1)

            def values(i, u):
                s, t = divmod(u, NT)
                pe.wait_ge(mixed, U * i + u + 1 + OPEN)

                def turn(g):
                    pe.wait_ge(moved, NG * i + BEFORE[u] + g + OPEN)
                    for j in range(4 * g, min(4 * g + 4, t + 1)):
                        last = nc.tensor.transpose(tp[:, (j % 4) * TT:(j % 4 + 1) * TT],
                                                   a[:, u % 2, j * TT:(j + 1) * TT], c.ident[0:TT, 0:TT])
                    last.then_inc(turned, 1)

                def times(g):
                    pe.wait_ge(moved, NG * i + BEFORE[u] + g + 1 + OPEN)
                    if g == 0:
                        pe.wait_ge(squared, U * i + u + OPEN)
                    for j in range(4 * g, min(4 * g + 4, t + 1)):
                        last = nc.tensor.matmul(pv[:, 0:128], aT[:, (BEFORE[u] + g) % 2, (j % 4) * TT:(j % 4 + 1) * TT],
                                                v[:, s, j, :], start=(j == 0), stop=(j == t))
                    if g == GR[t] - 1:
                        last.then_inc(pv_done, 1)

                for g in range(GR[t]):
                    turn(g)
                    times(g)
                if t == NT - 1:
                    pe.wait_ge(pv_done, U * i + u + 1 + OPEN)
                    pe.sem_inc(head_done[s], 1)

            with pe.Fori(0, NI) as i:
                for u in range(U):
                    scores(i, u)
                    if u >= 1:
                        values(i, u - 1)
                values(i, U - 1)

        @block.vector
        def _(dve):
            dve.wait_ge(tables, 64 + OPEN)
            for j in range(2):
                nc.vector.tensor_tensor_reduce(out=lj[:, j, :], in0=lams[:, 2 * j, :], in1=lams[:, 2 * j + 1, :],
                                               scale=1.0, scalar=0.0, op0=ALU.mult, op1=ALU.add,
                                               accum_out=ls[:, j:j + 1]).then_inc(lam_sum, 1)
            dve.wait_ge(lam_exp, 1 + OPEN)
            LAMBDA0 = 0.8 - 0.6
            ch = Chain(dve, vec)
            ch(nc.vector.tensor_tensor(nlam[:], le[:, 1:2], le[:, 0:1], ALU.subtract))
            ch(nc.vector.tensor_scalar(nlam[:], nlam[:], -LAMBDA0, None, ALU.add))
            dve.wait_ge(mask_made, 2 + OPEN)

            def maxima(i, u, ch):
                t = u % NT
                for n in range(2):
                    dve.wait_ge(scored[n], U * i + u + 1 + OPEN)
                    ch(nc.vector.tensor_tensor(S[n][:, t * TT:(t + 1) * TT], S[n][:, t * TT:(t + 1) * TT],
                                               mask[:], ALU.add))
                    nc.vector.tensor_reduce(nmx[:, u % 2, n:n + 1], S[n][:, 0:(t + 1) * TT], AX.X, ALU.max,
                                            negate=True).then_inc(maxed[n], 1)

            def mix(i, u, ch):
                t, s = u % NT, u % 2
                for n in range(2):
                    dve.wait_ge(exped[n], U * i + u + 1 + OPEN)
                ch(nc.vector.reciprocal(rden[:, s, :], den[:, s, :]))
                ch(nc.vector.tensor_scalar(rel[:, s:s + 1], rden[:, s, 1:2], den[:, s, 0:1], nlam[:], ALU.mult, ALU.mult))
                nc.vector.scalar_tensor_tensor(out=a[:, s, 0:(t + 1) * TT], in0=e[:, 1, 0:(t + 1) * TT],
                                               scalar=rel[:, s:s + 1], in1=e[:, 0, 0:(t + 1) * TT],
                                               op0=ALU.mult, op1=ALU.add).then_inc(mixed, 1)

            def outs(i, u):
                s = u % 2
                dve.wait_ge(pv_done, U * i + u + 1 + OPEN)
                dve.wait_ge(stored[s], 16 * (U // 2 * i + u // 2) + OPEN)
                nc.vector.tensor_scalar(o[:, s, :], pv[:, 0:128], rden[:, s, 0:1], None, ALU.mult).then_inc(o_done, 1)

            with dve.Fori(0, NI) as i:
                ch = Chain(dve, vec, 4 * U * i + 2)
                for u in range(U):
                    maxima(i, u, ch)
                    if u >= 1:
                        outs(i, u - 1)
                    mix(i, u, ch)
                outs(i, U - 1)

        @block.scalar
        def _(act):
            act.wait_ge(lam_sum, 2 + OPEN)
            nc.scalar.activation(le[:], ls[:], ACT.Exp).then_inc(lam_exp, 1)

            def move(i, u):
                t = u % NT
                for g in range(GR[t]):
                    n = min(4, t + 1 - 4 * g) * TT
                    act.wait_ge(turned, NG * i + BEFORE[u] + g + 1 + OPEN)
                    nc.scalar.copy(aT[:, (BEFORE[u] + g) % 2, 0:n], tp[:, 0:n]).then_inc(moved, 1)

            def square(i, u):
                t = u % NT
                act.wait_ge(o_done, U * i + u + 1 + OPEN)
                act.dma_start(c.oD[t, :, bass.ds((2 * i + u // NT) * 128, 128)], o[:, u % 2, :]).then_inc(stored[u % 2], 16)
                nc.scalar.activation(osq[:], o[:, u % 2, :], ACT.Square,
                                     accum_out=c.o_ms[:, t, bass.ds(2 * i + u // NT, 1)]).then_inc(squared, 1)

            with act.Fori(0, NI) as i:
                for u in range(U):
                    t = u % NT
                    for n in range(2):
                        act.wait_ge(maxed[n], U * i + u + 1 + OPEN)
                        act.wait_ge(mixed, U * i + u + OPEN)
                        nc.scalar.activation(e[:, n, 0:(t + 1) * TT], S[n][:, 0:(t + 1) * TT], ACT.Exp,
                                             bias=nmx[:, u % 2, n:n + 1],
                                             accum_out=den[:, u % 2, n:n + 1]).then_inc(exped[n], 1)
                    if u >= 1:
                        move(i, u - 1)
                        square(i, u - 1)
                move(i, U - 1)
                square(i, U - 1)
            act.wait_ge(squared, NI * U + OPEN)
            for s in range(2):
                act.wait_ge(stored[s], 16 * NI * U // 2 + OPEN)


SUB = 13
DECAY = math.exp(-0.5)
GN_EPS = 64e-5


def rwkv(nc, c):
    with ExitStack() as st:
        sb, ps, sem, begin = scope(nc, st)
        x3 = sb("rw_x3", [128, 3, T + 1])
        d3 = sb("rw_d3", [128, 3, T])
        m3 = sb("rw_m3", [128, 3, T])
        lo = sb("rw_lo", [128, 2, T])
        NP = 10
        MU_R, MU_K, MU_V, W0, A0, K_K, K_A, R_K, LN_W, LN_B = range(NP)
        NR = NP * RH // 2 + 2
        rows_ = sb("rw_rows", [NR, 128])
        par_ = sb("rw_par", [128, NR])
        par = par_[:, 0:NP * RH // 2].rearrange("p (n f) -> p n f", n=NP)
        lmu = par_[:, NP * RH // 2:NR]
        pf = sb("rw_pf", [128, NP])
        wa = sb("rw_wa", [128, 128])
        g2 = sb("rw_g2", [128, 128])
        reset = sb("rw_reset", [128, T])
        ones = sb("rw_ones", [128, 128])
        mask4 = sb("rw_mask4", [TT, 4, TT])
        maskn = sb("rw_maskn", [TT, 2, TT])
        geps = sb("rw_geps", [128, 1])
        sw = sb("rw_sw", [128, T])
        a = sb("rw_a", [128, T])
        g = sb("rw_g", [128, T])
        run = sb("rw_run", [128, T])
        lpr = sb("rw_lpr", [128, T])
        P = sb("rw_P", [128, T])
        Pi = sb("rw_Pi", [128, T])
        Pp = sb("rw_Pp", [128, T])
        kk = sb("rw_kk", [128, T])
        kk2 = sb("rw_kk2", [128, T])
        kn = sb("rw_kn", [128, T])
        kr = sb("rw_kr", [128, 2, T])
        bk = sb("rw_bk", [128, 2, T])
        bon = sb("rw_bon", [128, T])
        M4 = sb("rw_M4", [TT, 2, 4, 4, TT])
        Nn = sb("rw_Nn", [TT, 2, 4, TT])
        X2 = sb("rw_X2", [TT, 2, 4, TT])
        X4 = sb("rw_X4", [TT, 2, 4, TT])
        N8 = sb("rw_N8", [TT, 4, TT])
        Q = sb("rw_Q", [TT, 2, 4, TT])
        Y1 = sb("rw_Y1", [TT, 2, 4, TT])
        Y2 = sb("rw_Y2", [TT, 2, 4, TT])
        Y4 = sb("rw_Y4", [TT, 4, TT])
        G = sb("rw_G", [TT, 2, 4, TT])
        MT = sb("rw_MT", [TT, 2, 4, TT])
        tok = sb("rw_tok", [TT, 2, 2, 3, 128])
        R = sb("rw_R", [TT, 128])
        Uu = sb("rw_U", [TT, 128])
        S = sb("rw_S", [128, 2, RD])
        St = sb("rw_St", [128, RD])
        Y = sb("rw_Y", [TT, NT * 2, RD])
        Yq = sb("rw_Yq", [TT, NT * 2, RD])
        gs = sb("rw_gs", [TT, 4, NT * 2])
        yw = sb("rw_yw", [128, T])
        bank = ps("rw_bank", [128, 8, 512])
        region = bank[:, 2:5, :].rearrange("p b n -> p (b n)")
        consts = sem("rw_consts")
        x_in = sem("rw_x_in")
        lora_in = sem("rw_lora_in")
        pre = sem("rw_pre")
        made = sem("rw_made")
        par_turned = sem("rw_par_turned")
        lora = sem("rw_lora")
        pfc = sem("rw_pf_copied")
        prep_dve, prep_act, prep_pe = sem("rw_prep_dve"), sem("rw_prep_act"), sem("rw_prep_pe")
        solve_dve, solve_act, solve_pe = sem("rw_solve_dve"), sem("rw_solve_act"), sem("rw_solve_pe")
        seq_dve, seq_act, seq_pe = sem("rw_seq_dve"), sem("rw_seq_act"), sem("rw_seq_pe")
        seq_add = sem("rw_seq_add")
        gn_dve, gn_act, gn_pe = sem("rw_gn_dve"), sem("rw_gn_act"), sem("rw_gn_pe")
        y_out = sem("rw_y_out")
        block = begin()
        NF = RH // 2
        NB = NT // 2

        DV = ["diff", "mr", "mk", "mv", "kk", "run", "lpr", "kmax", "krec", "kkn", "kap", "ta", "kp", "b", "bh", "kh", "rh", "rk", "bon"]
        AC = ["sw", "a", "g", "kk2", "P", "Pi", "Pp", "kn"]
        PR = ["w", "a", "g", "ss", "bs"]

        def dv(i, name):
            return len(DV) * i + DV.index(name) + 1

        def ac(i, name):
            return len(AC) * i + AC.index(name) + 1

        def pr(i, name):
            return len(PR) * i + PR.index(name) + 1

        @block.sync
        def _(sp):
            row = lambda ap: ap.rearrange("o (f p) -> (o f) p", p=128)
            mu = c.rwkv_mu
            for j, src in enumerate((mu[:, 0:D], mu[:, D:2 * D], mu[:, 2 * D:3 * D], c.rwkv_w0, c.rwkv_a0,
                                     c.rwkv_k_k, c.rwkv_k_a, c.rwkv_r_k.rearrange("o h d -> o (h d)"),
                                     c.rwkv_ln_w, c.rwkv_ln_b)):
                sp.dma_start(rows_[8 * j:8 * j + 8, :], row(src)).then_inc(consts, 16)
            sp.dma_start(rows_[8 * NP:8 * NP + 2, :], row(mu[:, 3 * D:RWKV_COLS])).then_inc(consts, 16)
            sp.dma_start(mask4[:], c.mask4).then_inc(consts, 16)
            sp.dma_start(maskn[:], c.maskn).then_inc(consts, 16)
            for j in range(2):
                sp.dma_start(x3[:, j, 1:T + 1], c.pT[24 + j]).then_inc(lora_in, 16)
            with sp.Fori(0, NF) as i:
                sp.wait_ge(pre, 3 + OPEN)
                sp.wait_ge(prep_dve, len(DV) * i + OPEN)
                for j in range(3):
                    sp.dma_start(x3[:, j, 1:T + 1], c.pT[bass.ds(i + 8 * j, 1)].rearrange("o p t -> (o p) t")).then_inc(x_in, 16)
                sp.wait_ge(prep_pe, len(PR) * i + OPEN)
                fs = bass.ds(i * 128, 128)
                sp.dma_start(wa[0:64, :], c.rwkv_w2[0, :, fs]).then_inc(x_in, 16)
                sp.dma_start(wa[64:128, :], c.rwkv_a2[0, :, fs]).then_inc(x_in, 16)
                sp.dma_start(g2[:], c.rwkv_g2[0, :, fs]).then_inc(x_in, 16)
                sp.wait_ge(gn_dve, 8 * i + 8 + OPEN)
                sp.dma_start(c.yrT[bass.ds(i, 1)].rearrange("o p t -> (o p) t"), yw[:]).then_inc(y_out, 16)
            sp.wait_ge(y_out, 16 * NF + OPEN)

        def order(b):
            early, late = [1, 2, 3, 4, 5, 6], [7, 8, 9, 10, 11, 12, 13, 14]
            pieces = [[(0, 1)], [(0, 2)], [(0, 3), (0, 4)], [(1, 1)], [(1, 2)], [(1, 3), (1, 4)], [], []]
            out = []
            if b < NB:
                out += [("solve", b, n) for n in early]
            for n, ps_ in zip(late, pieces):
                if b > 0:
                    out += [("seq", b - 1, q) for q in ps_]
                if b < NB:
                    out.append(("solve", b, n))
            return out

        ORDER = [x for b in range(NB + 1) for x in order(b)]
        ND, NA_, NPE = 11, 9, 14

        @block.tensor
        def _(pe):
            units = [(cc, h) for cc in range(2) for h in range(2)]

            def rows(h):
                return slice(64 * h, 64 * h + 64)

            def solve(i, b, n):
                B = NB * i + b
                sd, sa = lambda k: pe.wait_ge(solve_dve, ND * B + k + OPEN), lambda k: pe.wait_ge(solve_act, NA_ * B + k + OPEN)
                s = b % 2
                mm, tr = nc.tensor.matmul, nc.tensor.transpose
                bq = lambda bb, u: bank[0:TT, bb, u * TT:(u + 1) * TT]
                ch = lambda cc: slice((2 * b + cc) * TT, (2 * b + cc + 1) * TT)
                last = None
                if n in (1, 4):
                    cc = n // 4
                    if n == 4:
                        sd(1)
                    elif b > 0:
                        pe.wait_ge(solve_dve, ND * (B - 1) + 3 + OPEN)
                    else:
                        pe.wait_ge(solve_dve, ND * B + OPEN)
                        pe.wait_ge(prep_dve, dv(i, "bon") + OPEN)
                    for h in range(2):
                        for j in range(2):
                            last = mm(bank[0:TT, h, 2 * j * TT:(2 * j + 2) * TT].rearrange("p (a t) -> p a t", a=2),
                                      bk[rows(h), j, ch(cc)], kr[rows(h), :, ch(cc)], start=True, stop=True)
                elif n == 2:
                    pe.wait_ge(solve_act, NA_ * B + OPEN)
                    for cc, h in units:
                        last = mm(bq(3 + h, cc), kr[rows(h), 0, ch(cc)], bk[rows(h), 0, ch(cc)], start=True, stop=True)
                elif n in (3, 5):
                    cc = (n - 3) // 2
                    if n == 5:
                        sa(1)
                    elif b > 1:
                        pe.wait_ge(seq_dve, (NT - 1) * i + 2 * (b - 1) + OPEN)
                    for j, src in enumerate((bk[:, 0, ch(cc)], bk[:, 1, ch(cc)], m3[:, 2, ch(cc)])):
                        last = tr(bank[0:TT, 5, j * 128:(j + 1) * 128], src, c.ident[:])
                elif n == 6:
                    sd(3)
                    for u in range(4):
                        mm(bq(2, u), Nn[:, 0, u, :], M4[:, s, u, 0, :], start=True, stop=True)
                        last = mm(bq(3, u), M4[:, s, u, 0, :], Nn[:, 0, u, :], start=True, stop=True)
                elif n == 7:
                    sa(3)
                    sd(4)
                    for u in range(4):
                        mm(bq(2, u), X2[:, 1, u, :], X2[:, 0, u, :], start=True, stop=True)
                        mm(bq(3, u), X2[:, 0, u, :], X2[:, 1, u, :], start=True, stop=True)
                        last = mm(bq(4, u), X2[:, 1, u, :], Q[:, 0, u, :], start=True, stop=True)
                elif n == 8:
                    sa(4)
                    sd(5)
                    for u in range(4):
                        mm(bq(3, u), X4[:, 0, u, :], X4[:, 1, u, :], start=True, stop=True)
                        last = mm(bq(4, u), X4[:, 1, u, :], Q[:, 1, u, :], start=True, stop=True)
                elif n == 9:
                    sa(5)
                    sd(6)
                    for u in range(4):
                        last = mm(bq(4, u), N8[:, u, :], Q[:, 0, u, :], start=True, stop=True)
                elif n == 10:
                    sd(7)
                    for u in range(4):
                        mm(bq(2, u), Nn[:, 1, u, :], Q[:, 1, u, :], start=True, stop=True)
                        mm(bq(3, u), Q[:, 1, u, :], Nn[:, 1, u, :], start=True, stop=True)
                        last = tr(bq(4, u), Q[:, 1, u, :], c.ident[0:TT, 0:TT])
                elif n == 11:
                    sa(6)
                    sd(8)
                    for u in range(4):
                        mm(bq(2, u), Y1[:, 1, u, :], Y1[:, 0, u, :], start=True, stop=True)
                        mm(bq(3, u), Y1[:, 0, u, :], Y1[:, 1, u, :], start=True, stop=True)
                        last = mm(bq(4, u), Y1[:, 0, u, :], G[:, 0, u, :], start=True, stop=True)
                elif n == 12:
                    sa(7)
                    sd(9)
                    for u in range(4):
                        mm(bq(2, u), Y2[:, 1, u, :], Y2[:, 0, u, :], start=True, stop=True)
                        last = mm(bq(4, u), Y2[:, 0, u, :], G[:, 1, u, :], start=True, stop=True)
                elif n == 13:
                    sa(8)
                    sd(10)
                    for u in range(4):
                        last = mm(bq(4, u), Y4[:, u, :], G[:, 0, u, :], start=True, stop=True)
                elif n == 14:
                    sd(11)
                    for u in range(4):
                        last = tr(bq(4, u), G[:, 1, u, :], c.ident[0:TT, 0:TT])
                last.then_inc(solve_pe, 1)

            def seq(i, b, cc, q):
                t = 2 * b + cc
                C = NT * i + t
                s = b % 2
                ch = slice(t * TT, (t + 1) * TT)
                mm = nc.tensor.matmul
                vv = lambda h: tok[:, s, cc, 2, 64 * h:64 * h + 64]
                last = None
                if q == 1:
                    if t > 0:
                        pe.wait_ge(seq_dve, (NT - 1) * i + t + OPEN)
                    pe.wait_ge(solve_act, NA_ * (NB * i + b) + 9 + OPEN)
                    pe.wait_ge(seq_act, 3 * C + OPEN)
                    for h in range(2):
                        o = bank[0:TT, 6 + h, 0:64]
                        if t > 0:
                            mm(o, kr[rows(h), 0, ch], S[rows(h), t % 2, :], start=True, stop=False)
                        last = mm(o, M4[:, s, 2 * cc + h, 2, :], vv(h), start=(t == 0), stop=True)
                elif q == 2:
                    pe.wait_ge(seq_act, 3 * C + 1 + OPEN)
                    for h in range(2):
                        last = mm(bank[0:TT, 6 + h, 64:128], MT[:, s, 2 * cc + h, :],
                                  R[:, 64 * h:64 * h + 64], start=True, stop=True)
                elif q == 3:
                    pe.wait_ge(seq_act, 3 * C + 2 + OPEN)
                    for h in range(2):
                        o = bank[rows(h), 5, 0:64]
                        mm(o, tok[:, s, cc, 0, 64 * h:64 * h + 64], Uu[:, 64 * h:64 * h + 64], start=True, stop=False)
                        last = mm(o, tok[:, s, cc, 1, 64 * h:64 * h + 64], vv(h), start=False, stop=True)
                else:
                    for h in range(2):
                        o = bank[0:TT, 6 + h, 128:192]
                        if t > 0:
                            mm(o, kr[rows(h), 1, ch], S[rows(h), t % 2, :], start=True, stop=False)
                        mm(o, M4[:, s, 2 * cc + h, 1, :], Uu[:, 64 * h:64 * h + 64], start=(t == 0), stop=False)
                        last = mm(o, M4[:, s, 2 * cc + h, 3, :], vv(h), start=False, stop=True)
                last.then_inc(seq_pe, 1)

            def wide(lhsT, rhs):
                for lo_ in range(0, T, 512):
                    hi = min(lo_ + 512, T)
                    last = nc.tensor.matmul(region[:, lo_:hi], lhsT, rhs[:, lo_:hi], start=True, stop=True)
                last.then_inc(prep_pe, 1)

            pe.wait_ge(consts, 13 * 16 + OPEN)
            nc.tensor.transpose(bank[:, 5, 0:NR], rows_[:], c.ident[0:NR, 0:NR]).then_inc(par_turned, 1)
            pe.wait_ge(lora, 2 + OPEN)
            with pe.Fori(0, NF) as i:
                pe.wait_ge(x_in, 96 * i + 96 + OPEN)
                pe.wait_ge(gn_act, 4 * i + OPEN)
                wide(wa[0:64, :], lo[0:64, 0, :])
                pe.wait_ge(prep_act, ac(i, "sw") + OPEN)
                wide(wa[64:128, :], lo[64:128, 0, :])
                pe.wait_ge(prep_act, ac(i, "a") + OPEN)
                wide(g2[:], lo[:, 1, :])
                pe.wait_ge(prep_act, ac(i, "kk2") + OPEN)
                wide(ones[:], kk2[:])
                pe.wait_ge(prep_act, ac(i, "kn") + OPEN)
                pe.wait_ge(prep_dve, dv(i, "rk") + OPEN)
                wide(ones[:], d3[:, 0, :])
                for kind, b, q in ORDER:
                    if kind == "solve":
                        solve(i, b, q)
                    else:
                        seq(i, b, *q)
                pe.wait_ge(gn_dve, 8 * i + 6 + OPEN)
                for t in range(NT):
                    last = nc.tensor.transpose(bank[:, 2 + t // 4, (t % 4) * TT:(t % 4 + 1) * TT],
                                               Yq[:, 2 * t:2 * t + 2, :].rearrange("p h d -> p (h d)"),
                                               c.ident[0:TT, 0:TT])
                last.then_inc(gn_pe, 1)

        @block.scalar
        def _(act):
            act.wait_ge(pre, 3 + OPEN)
            nc.scalar.activation(lo[0:64, 0, :], lo[0:64, 0, :], ACT.Tanh).then_inc(lora, 1)
            nc.scalar.activation(lo[:, 1, :], lo[:, 1, :], ACT.Sigmoid).then_inc(lora, 1)

            def solve(i, b, n):
                B = NB * i + b
                s = b % 2
                pair = lambda lo_: bank[0:TT, lo_:lo_ + 2, 0:4 * TT].rearrange("p k (u t) -> p k u t", u=4)
                one = lambda lo_: bank[0:TT, lo_, 0:4 * TT].rearrange("p (u t) -> p u t", u=4)
                what = {3: lambda: (tok[:, s, 0].rearrange("p j d -> p (j d)"), bank[0:TT, 5, 0:384]),
                        5: lambda: (tok[:, s, 1].rearrange("p j d -> p (j d)"), bank[0:TT, 5, 0:384]),
                        6: lambda: (X2[:], pair(2)), 7: lambda: (X4[:], pair(2)), 8: lambda: (N8[:], one(3)),
                        10: lambda: (Y1[:], pair(2)), 11: lambda: (Y2[:], pair(2)), 12: lambda: (Y4[:], one(2)),
                        14: lambda: (MT[:, s], one(4))}
                if n in what:
                    act.wait_ge(solve_pe, NPE * B + n + OPEN)
                    nc.scalar.copy(*what[n]()).then_inc(solve_act, 1)

            both = lambda x: x.rearrange("p (h d) -> p h d", h=2)

            def seq(i, b, cc, q):
                C = NT * i + 2 * b + cc
                if q == 1:
                    act.wait_ge(seq_pe, 4 * C + 1 + OPEN)
                    nc.scalar.mul(both(R[:]), bank[0:TT, 6:8, 0:64], -1.0).then_inc(seq_act, 1)
                elif q == 2:
                    act.wait_ge(seq_pe, 4 * C + 2 + OPEN)
                    nc.scalar.copy(both(Uu[:]), bank[0:TT, 6:8, 64:128]).then_inc(seq_act, 1)
                elif q == 4:
                    act.wait_ge(seq_pe, 4 * C + 4 + OPEN)
                    t = 2 * b + cc
                    nc.scalar.copy(Y[:, 2 * t:2 * t + 2, :], bank[0:TT, 6:8, 128:192]).then_inc(seq_act, 1)

            with act.Fori(0, NF) as i:
                act.wait_ge(pfc, i + 1 + OPEN)
                for name, dst, bias in (("w", sw, W0), ("a", a, A0)):
                    act.wait_ge(prep_pe, pr(i, name) + OPEN)
                    nc.scalar.activation(dst[:], region[:, 0:T], ACT.Sigmoid, bias=pf[:, bias:bias + 1]).then_inc(prep_act, 1)
                act.wait_ge(prep_pe, pr(i, "g") + OPEN)
                nc.scalar.copy(g[:], region[:, 0:T]).then_inc(prep_act, 1)
                act.wait_ge(prep_dve, dv(i, "mk") + OPEN)
                nc.scalar.activation(kk2[:], m3[:, 1, :], ACT.Square, scale=pf[:, K_K:K_K + 1]).then_inc(prep_act, 1)
                act.wait_ge(prep_dve, dv(i, "lpr") + OPEN)
                nc.scalar.activation(P[:], run[:], ACT.Exp, scale=-DECAY).then_inc(prep_act, 1)
                nc.scalar.activation(Pi[:], run[:], ACT.Exp, scale=DECAY).then_inc(prep_act, 1)
                nc.scalar.activation(Pp[:], lpr[:], ACT.Exp, scale=-DECAY).then_inc(prep_act, 1)
                act.wait_ge(prep_pe, pr(i, "ss") + OPEN)
                nc.scalar.activation(kn[:], region[:, 0:T], ACT.Sqrt).then_inc(prep_act, 1)
                for kind, b, q in ORDER:
                    if kind == "solve":
                        solve(i, b, q)
                    else:
                        seq(i, b, *q)
                act.wait_ge(gn_dve, 8 * i + 3 + OPEN)
                nc.scalar.activation(Yq[:], Y[:], ACT.Square).then_inc(gn_act, 1)
                act.wait_ge(gn_dve, 8 * i + 4 + OPEN)
                nc.scalar.activation(gs[:, 2, :], gs[:, 1, :], ACT.Sqrt, bias=geps[0:TT, :], scale=1.0 / RD).then_inc(gn_act, 1)
                act.wait_ge(gn_pe, i + 1 + OPEN)
                act.wait_ge(y_out, 16 * i + OPEN)
                for lo_, n, b in ((0, 8, 2), (8, 2, 1)):
                    nc.scalar.activation(yw[:, lo_ * TT:(lo_ + n) * TT].rearrange("p (b t) -> p b t", b=b),
                                         bank[:, 2 + lo_ // 4:2 + lo_ // 4 + b, 0:n // b * TT], ACT.Identity,
                                         scale=pf[:, LN_W:LN_W + 1], bias=pf[:, LN_B:LN_B + 1]).then_inc(gn_act, 1)

        @block.vector
        def _(dve):
            tt, ts, stt = nc.vector.tensor_tensor, nc.vector.tensor_scalar, nc.vector.scalar_tensor_tensor
            nc.vector.memset(geps[:], GN_EPS)
            nc.vector.memset(ones[:], 0.0).then_inc(made, 1)
            nc.vector.memset(reset[:], 1.0).then_inc(made, 1)
            dve.wait_ge(made, 2 + OPEN)
            for h in range(2):
                nc.vector.memset(ones[64 * h:64 * h + 64, 64 * h:64 * h + 64], 1.0).then_inc(made, 1)
            nc.vector.memset(reset[:, 0::TT], 0.0).then_inc(made, 1)
            dve.wait_ge(made, 5 + OPEN)
            nc.vector.memset(x3[:, :, 0:1], 0.0).then_inc(pre, 1)
            dve.wait_ge(consts, 13 * 16 + OPEN)
            dve.wait_ge(lora_in, 32 + OPEN)
            dve.wait_ge(pre, 1 + OPEN)
            dve.wait_ge(par_turned, 1 + OPEN)
            nc.vector.tensor_copy(par_[:], bank[:, 5, 0:NR]).then_inc(made, 1)
            tt(d3[:, 0:2, :], x3[:, 0:2, 0:T], x3[:, 0:2, 1:T + 1], ALU.subtract).then_inc(made, 1)
            dve.wait_ge(made, 7 + OPEN)
            for j in range(2):
                stt(out=lo[:, j, :], in0=d3[:, j, :], scalar=lmu[:, j:j + 1], in1=x3[:, j, 1:T + 1],
                    op0=ALU.mult, op1=ALU.add).then_inc(pre, 1)
            dve.wait_ge(pre, 3 + OPEN)

            def solve(i, b, n):
                B = NB * i + b
                s = b % 2
                bq = bank[0:TT, 4, 0:4 * TT].rearrange("p (u t) -> p u t", u=4)
                if n in (2, 1, 4, 7, 8, 9, 10, 11, 12, 13):
                    dve.wait_ge(solve_pe, NPE * B + n + OPEN)
                if n in (1, 4):
                    cc = n // 4
                    tt(M4[:, s, 2 * cc:2 * cc + 2], bank[0:TT, 0:2, 0:4 * TT].rearrange("p h (k t) -> p h k t", k=4),
                       mask4[:].unsqueeze(1).to_broadcast([TT, 2, 4, TT]), ALU.mult).then_inc(solve_dve, 1)
                    if n == 4:
                        dve.wait_ge(solve_dve, ND * B + 3 + OPEN)
                        tt(Q[:, 0], M4[:, s, :, 0, :], c.ident[0:TT, 0:TT].unsqueeze(1).to_broadcast([TT, 4, TT]),
                           ALU.add).then_inc(solve_dve, 1)
                elif n == 2:
                    for j in range(2):
                        last = tt(Nn[:, j].rearrange("p (cc h) t -> p h cc t", h=2),
                                  bank[0:TT, 3:5, 0:2 * TT].rearrange("p h (cc t) -> p h cc t", cc=2),
                                  maskn[:, j, :].unsqueeze(1).unsqueeze(1).to_broadcast([TT, 2, 2, TT]), ALU.mult)
                    last.then_inc(solve_dve, 1)
                elif n in (7, 8, 9):
                    o = n % 2
                    dve.wait_ge(solve_dve, ND * B + n - 3 + OPEN)
                    tt(Q[:, o], bq, Q[:, 1 - o], ALU.add).then_inc(solve_dve, 1)
                elif n == 10:
                    nc.vector.tensor_copy(G[:, 0], bq).then_inc(solve_dve, 1)
                elif n in (11, 12, 13):
                    o = n % 2
                    dve.wait_ge(solve_dve, ND * B + n - 3 + OPEN)
                    tt(G[:, o], bq, G[:, 1 - o], ALU.add).then_inc(solve_dve, 1)

            def seq(i, b, cc, q):
                t = 2 * b + cc
                C = NT * i + t
                if q == 3 and t < NT - 1:
                    dve.wait_ge(seq_pe, 4 * C + 3 + OPEN)
                    nxt, end = S[:, (t + 1) % 2, :], P[:, (t + 1) * TT - 1:(t + 1) * TT]
                    if t == 0:
                        dve.wait_ge(seq_dve, (NT - 1) * i + OPEN)
                        ts(nxt, bank[:, 5, 0:64], end, None, ALU.mult).then_inc(seq_dve, 1)
                    else:
                        dve.wait_ge(seq_dve, (NT - 1) * i + t + OPEN)
                        tt(St[:], bank[:, 5, 0:64], S[:, t % 2, :], ALU.add).then_inc(seq_add, 1)
                        dve.wait_ge(seq_add, (NT - 2) * i + t + OPEN)
                        dve.wait_ge(seq_pe, 4 * C + OPEN)
                        ts(nxt, St[:], end, None, ALU.mult).then_inc(seq_dve, 1)

            with dve.Fori(0, NF) as i:
                def w(*names):
                    for name in names:
                        dve.wait_ge(prep_dve, dv(i, name) + OPEN)

                def v(name, ins):
                    assert v.n == DV.index(name)
                    v.n += 1
                    ins.then_inc(prep_dve, 1)
                v.n = 0
                dve.wait_ge(gn_act, 4 * i + OPEN)
                nc.vector.tensor_copy(pf[:], par[:, :, bass.ds(i, 1)].rearrange("p n o -> p (n o)")).then_inc(pfc, 1)
                dve.wait_ge(pfc, i + 1 + OPEN)
                dve.wait_ge(x_in, 96 * i + 96 + OPEN)
                p = lambda n: pf[:, n:n + 1]
                v("diff", tt(d3[:], x3[:, :, 0:T], x3[:, :, 1:T + 1], ALU.subtract))
                w("diff")
                for j, name in enumerate(("mr", "mk", "mv")):
                    v(name, stt(out=m3[:, j, :], in0=d3[:, j, :], scalar=p(MU_R + j), in1=x3[:, j, 1:T + 1],
                                op0=ALU.mult, op1=ALU.add))
                w("mv")
                v("kk", ts(kk[:], m3[:, 1, :], p(K_K), None, ALU.mult))
                dve.wait_ge(prep_act, ac(i, "sw") + OPEN)
                v("run", nc.vector.tensor_tensor_scan(run[:], reset[:], sw[:], 0.0, ALU.mult, ALU.add))
                w("run")
                v("lpr", tt(lpr[:], run[:], sw[:], ALU.subtract))
                dve.wait_ge(prep_act, ac(i, "kn") + OPEN)
                v("kmax", ts(kn[:], kn[:], 1e-12, None, ALU.max))
                w("kmax")
                v("krec", nc.vector.reciprocal(kn[:], kn[:]))
                w("krec")
                v("kkn", tt(kk[:], kk[:], kn[:], ALU.mult))
                w("kkn")
                v("kap", tt(kr[:, 0, :], kk[:], Pp[:], ALU.mult))
                v("ta", ts(d3[:, 1, :], a[:], -1.0, p(K_A), ALU.add, ALU.mult))
                w("ta")
                v("kp", stt(out=d3[:, 1, :], in0=d3[:, 1, :], scalar=1.0, in1=m3[:, 1, :], op0=ALU.add, op1=ALU.mult))
                v("b", tt(kk[:], kk[:], a[:], ALU.mult))
                w("b")
                v("bh", tt(bk[:, 0, :], kk[:], Pi[:], ALU.mult))
                v("kh", tt(bk[:, 1, :], d3[:, 1, :], Pi[:], ALU.mult))
                v("rh", tt(kr[:, 1, :], m3[:, 0, :], P[:], ALU.mult))
                v("rk", stt(out=d3[:, 0, :], in0=m3[:, 0, :], scalar=p(R_K), in1=d3[:, 1, :], op0=ALU.mult, op1=ALU.mult))
                dve.wait_ge(prep_pe, pr(i, "bs") + OPEN)
                v("bon", tt(bon[:], region[:, 0:T], m3[:, 2, :], ALU.mult))
                for kind, b, q in ORDER:
                    if kind == "solve":
                        solve(i, b, q)
                    else:
                        seq(i, b, *q)
                ch = Chain(dve, gn_dve, 8 * i)
                wide = lambda j: gs[:, j, :].unsqueeze(2).to_broadcast([TT, 2 * NT, RD])
                dve.wait_ge(seq_act, 3 * NT * i + 3 * NT + OPEN)
                ch(nc.vector.tensor_reduce(gs[:, 0, :], Y[:], AX.X, ALU.add))
                ch(ts(gs[:, 0, :], gs[:, 0, :], 1.0 / RD, None, ALU.mult))
                ch(tt(Y[:], Y[:], wide(0), ALU.subtract))
                dve.wait_ge(gn_act, 4 * i + 1 + OPEN)
                ch(nc.vector.tensor_reduce(gs[:, 1, :], Yq[:], AX.X, ALU.add))
                dve.wait_ge(gn_act, 4 * i + 2 + OPEN)
                ch(nc.vector.reciprocal(gs[:, 3, :], gs[:, 2, :]))
                ch(tt(Yq[:], Y[:], wide(3), ALU.mult))
                dve.wait_ge(gn_act, 4 * i + 4 + OPEN)
                ch(tt(yw[:], yw[:], bon[:], ALU.add))
                ch(tt(yw[:], yw[:], g[:], ALU.mult))


NG, EG = 4, 8
NE = NG * EG
FF = 512
SLOTS = 128
OVER = 2 * T // (SLOTS + 1)
NBLK = NE + OVER
BIG = 1.0e30


def merge_branches(nc, c):
    with ExitStack() as st:
        sb, ps, sem, begin = scope(nc, st)
        yT = sb("mb_yT", [128, KD, T])
        oT = sb("mb_oT", [128, KD, T])
        o = sb("mb_o", [TT, 2, D])
        rs = sb("mb_rs", [TT, NT * DH])
        ri = sb("mb_ri", [TT, NT * DH])
        sw = sb("mb_sw", [TT, 128])
        w = sb("mb_w", [128, 2, KD, 128])
        gt = sb("mb_gt", [128, 2, T])
        part = sb("mb_part", [128, 2, T])
        bank = ps("mb_bank", [128, 8, 512])
        sw_in = sem("mb_sw_in")
        o_in = [sem(f"mb_o_in{s}") for s in range(2)]
        y_in = sem("mb_y_in")
        w_in = [sem(f"mb_w_in{s}") for s in range(2)]
        g_in = [sem(f"mb_g_in{s}") for s in range(2)]
        rs_done = sem("mb_rs_done")
        vec = sem("mb_vec")
        turned = sem("mb_turned")
        moved = sem("mb_moved")
        product = [sem(f"mb_product{s}") for s in range(2)]
        opened = [sem(f"mb_opened{s}") for s in range(2)]
        gated = [sem(f"mb_gated{s}") for s in range(2)]
        summed = sem("mb_summed")
        block = begin()
        LAMBDA0 = 0.8 - 0.6

        @block.sync
        def _(sp):
            sp.dma_start(sw[:], c.diff_subln_w.to_broadcast([TT, 128])).then_inc(sw_in, 16)
            for t in range(2):
                sp.dma_start(o[:, t, :], c.oD[t]).then_inc(o_in[t], 16)
            sp.dma_start(yT[:], c.yrT.rearrange("f p t -> p f t")).then_inc(y_in, 16)
            with sp.Fori(1, NT // 2) as i:
                for s in range(2):
                    sp.wait_ge(turned, 2 * i + s - 1 + OPEN)
                    sp.dma_start(o[:, s, :], c.oD[bass.ds(2 * i + s, 1)].rearrange("o p d -> (o p) d")).then_inc(o_in[s], 16)
            with sp.Fori(0, KD) as i:
                for s, src in enumerate((c.w_branch_rwkv, c.w_branch_diff)):
                    sp.wait_ge(product[s], i + OPEN)
                    sp.dma_start(w[:, s], src.rearrange("o (k p) f -> p (o k) f", p=128)[:, :, bass.ds(i * 128, 128)]).then_inc(w_in[s], 16)
                    sp.wait_ge(gated[s], i + OPEN)
                    sp.dma_start(gt[:, s, :], c.pT[bass.ds(i + RT + 8 * s, 1)].rearrange("o p t -> (o p) t")).then_inc(g_in[s], 16)

        @block.scalar
        def _(act):
            nc.scalar.activation(rs[:], c.o_ms[:].rearrange("p t h -> p (t h)"), ACT.Sqrt, bias=c.eps[0:TT, :],
                                 scale=1.0 / 128).then_inc(rs_done, 1)
            with act.Fori(0, NT) as i:
                act.wait_ge(turned, i + 1 + OPEN)
                nc.scalar.copy(oT[:, :, bass.ds(i * TT, TT)].rearrange("p (b k) t -> p b k t", b=2),
                               bank[:, 0:2, 0:4 * TT].rearrange("p b (k t) -> p b k t", k=4)).then_inc(moved, 1)
            with act.Fori(0, KD) as i:
                for s in range(2):
                    act.wait_ge(g_in[s], 16 * i + 16 + OPEN)
                    nc.scalar.activation(gt[:, s, :], gt[:, s, :], ACT.Sigmoid).then_inc(opened[s], 1)

        @block.vector
        def _(dve):
            dve.wait_ge(sw_in, 16 + OPEN)
            dve.wait_ge(rs_done, 1 + OPEN)
            ch = Chain(dve, vec)
            ch(nc.vector.tensor_scalar(sw[:], sw[:], 1.0 - LAMBDA0, None, ALU.mult))
            ch(nc.vector.reciprocal(ri[:], rs[:]))
            with dve.Fori(0, NT // 2) as i:
                ch = Chain(dve, vec, 4 * i + 2)
                for s in range(2):
                    dve.wait_ge(o_in[s], 16 * i + 16 + OPEN)
                    o3 = o[:, s, :].rearrange("p (h d) -> p h d", h=DH)
                    ch(nc.vector.tensor_tensor(o3, o3, ri[:, bass.ds((2 * i + s) * DH, DH)].unsqueeze(2).to_broadcast([TT, DH, 128]), ALU.mult))
                    ch(nc.vector.tensor_tensor(o3, o3, sw[:].unsqueeze(1).to_broadcast([TT, DH, 128]), ALU.mult))
            split = lambda x: x.rearrange("p (n t) -> p n t", n=NCOL)
            with dve.Fori(0, KD) as i:
                for s in range(2):
                    dve.wait_ge(product[s], i + 1 + OPEN)
                    dve.wait_ge(opened[s], i + 1 + OPEN)
                    nc.vector.tensor_tensor(split(part[:, s, :]), bank[:, 4 * s:4 * s + 4, 0:CW], split(gt[:, s, :]),
                                            ALU.mult).then_inc(gated[s], 1)
                dve.wait_ge(gated[0], i + 1 + OPEN)
                dve.wait_ge(gated[1], i + 1 + OPEN)
                nc.vector.tensor_tensor(c.mT[:, bass.ds(i, 1), :].rearrange("p o t -> p (o t)"), part[:, 0, :], part[:, 1, :],
                                        ALU.add).then_inc(summed, 1)
                dve.wait_ge(summed, i + 1 + OPEN)

        @block.tensor
        def _(pe):
            with pe.Fori(0, NT // 2) as i:
                for s in range(2):
                    pe.wait_ge(vec, 4 * i + 2 * s + 4 + OPEN)
                    pe.wait_ge(moved, 2 * i + s + OPEN)
                    for k in range(KD):
                        last = nc.tensor.transpose(bank[:, k // 4, (k % 4) * TT:(k % 4 + 1) * TT],
                                                   o[:, s, k * 128:(k + 1) * 128], c.ident[0:TT, 0:TT])
                    last.then_inc(turned, 1)
            pe.wait_ge(moved, NT + OPEN)
            pe.wait_ge(y_in, 16 + OPEN)
            with pe.Fori(0, KD) as i:
                for s, src in enumerate((yT, oT)):
                    pe.wait_ge(w_in[s], 16 * i + 16 + OPEN)
                    pe.wait_ge(gated[s], i + OPEN)
                    for k in range(KD):
                        for n in range(NCOL):
                            last = nc.tensor.matmul(bank[:, 4 * s + n, 0:CW], w[:, s, k, :], src[:, k, n * CW:(n + 1) * CW],
                                                    start=(k == 0), stop=(k == KD - 1))
                    last.then_inc(product[s], 1)


def output_and_route(nc, c):
    NR = NG + NE
    with ExitStack() as st:
        sb, ps, sem, begin = scope(nc, st)
        wo = sb("or_wo", [128, KD, D])
        wr = sb("or_wr", [128, KD, NR])
        n2 = sb("or_n2", [TT, D])
        h = sb("or_h", [TT, 2, D])
        sq = sb("or_sq", [TT, D])
        ms = sb("or_ms", [TT, 2])
        rs = sb("or_rs", [TT, 2])
        ri = sb("or_ri", [TT, 2])
        u = sb("or_u", [TT, 2, D])
        uT = sb("or_uT", [128, 2, KD * TT])
        bank = ps("or_bank", [128, 8, 512])
        w_in = sem("or_w_in")
        h_in = [sem(f"or_h_in{s}") for s in range(2)]
        product = sem("or_product")
        added = sem("or_added")
        squared = sem("or_squared")
        rs_done = sem("or_rs_done")
        vec = sem("or_vec")
        normed = sem("or_normed")
        turned = sem("or_turned")
        moved = sem("or_moved")
        logits = sem("or_logits")
        kept = sem("or_kept")
        h_out = [sem(f"or_h_out{s}") for s in range(2)]
        u_out = [sem(f"or_u_out{s}") for s in range(2)]
        block = begin()

        @block.sync
        def _(sp):
            sp.dma_start(wo[:], c.w_out.rearrange("o (k p) f -> p (o k) f", p=128)).then_inc(w_in, 16)
            sp.dma_start(h[0:META, 0, :], c.meta_tokens).then_inc(h_in[0], 16)
            sp.dma_start(h[META:TT, 0, :], c.x[0, 0:TT - META, :]).then_inc(h_in[0], 16)
            sp.dma_start(h[:, 1, :], c.x[0, TT - META:2 * TT - META, :]).then_inc(h_in[1], 16)
            sp.dma_start(wr[:, :, 0:NG], c.router_group_w.rearrange("o (k p) e -> p (o k) e", p=128)).then_inc(w_in, 16)
            sp.dma_start(wr[:, :, NG:NR], c.router_expert_w.rearrange("o (k p) e -> p (o k) e", p=128)).then_inc(w_in, 16)
            sp.dma_start(n2[:], c.norm2_w.to_broadcast([TT, D])).then_inc(w_in, 16)
            for t in range(NT):
                s, m = t % 2, t // 2
                if t >= 2:
                    sp.wait_ge(normed, t - 1 + OPEN)
                    sp.wait_ge(h_out[s], 16 * m + OPEN)
                    sp.dma_start(h[:, s, :], c.x[0, t * TT - META:(t + 1) * TT - META, :]).then_inc(h_in[s], 16)
                sp.wait_ge(added, t + 1 + OPEN)
                sp.dma_start(c.h2D[t], h[:, s, :]).then_inc(h_out[s], 16)
                sp.wait_ge(normed, t + 1 + OPEN)
                sp.dma_start(c.u2D[t * TT:(t + 1) * TT, :], u[:, s, :]).then_inc(u_out[s], 16)
            for s in range(2):
                sp.wait_ge(h_out[s], 16 * NT // 2 + OPEN)
                sp.wait_ge(u_out[s], 16 * NT // 2 + OPEN)

        @block.tensor
        def _(pe):
            def route(t):
                s = t % 2
                pe.wait_ge(normed, t + 1 + OPEN)
                if t >= 1:
                    pe.wait_ge(moved, t + OPEN)
                for k in range(KD):
                    last = nc.tensor.transpose(bank[:, 4 + k // 4, (k % 4) * TT:(k % 4 + 1) * TT],
                                               u[:, s, k * 128:(k + 1) * 128], c.ident[0:TT, 0:TT])
                last.then_inc(turned, 1)
                pe.wait_ge(moved, t + 1 + OPEN)
                if t >= 1:
                    pe.wait_ge(kept, t + OPEN)
                for k in range(KD):
                    last = nc.tensor.matmul(bank[0:TT, 6, 0:NR], uT[:, s, k * TT:(k + 1) * TT], wr[:, k, :],
                                            start=(k == 0), stop=(k == KD - 1))
                last.then_inc(logits, 1)

            pe.wait_ge(w_in, 64 + OPEN)
            for t in range(NT):
                if t >= 2:
                    pe.wait_ge(added, t - 1 + OPEN)
                for n in range(2):
                    for k in range(KD):
                        last = nc.tensor.matmul(bank[0:TT, 2 * (t % 2) + n, :], c.mT[:, k, t * TT:(t + 1) * TT],
                                                wo[:, k, n * 512:(n + 1) * 512], start=(k == 0), stop=(k == KD - 1))
                last.then_inc(product, 1)
                if t >= 1:
                    route(t - 1)
            route(NT - 1)

        @block.vector
        def _(dve):
            dve.wait_ge(w_in, 64 + OPEN)
            ch = Chain(dve, vec)
            for t in range(NT):
                s = t % 2
                dve.wait_ge(product, t + 1 + OPEN)
                dve.wait_ge(h_in[s], 16 * (t // 2) + (32 if s == 0 else 16) + OPEN)
                nc.vector.tensor_tensor(h[:, s, :].rearrange("p (b n) -> p b n", b=2), bank[0:TT, 2 * s:2 * s + 2, :],
                                        h[:, s, :].rearrange("p (b n) -> p b n", b=2), ALU.add).then_inc(added, 1)
                dve.wait_ge(rs_done, t + 1 + OPEN)
                ch(nc.vector.reciprocal(ri[:, s:s + 1], rs[:, s:s + 1]))
                if t >= 2:
                    dve.wait_ge(turned, t - 1 + OPEN)
                    dve.wait_ge(u_out[s], 16 * (t // 2) + OPEN)
                nc.vector.scalar_tensor_tensor(out=u[:, s, :], in0=h[:, s, :], scalar=ri[:, s:s + 1], in1=n2[:],
                                               op0=ALU.mult, op1=ALU.mult).then_inc(normed, 1)

        @block.scalar
        def _(act):
            def move(t):
                s = t % 2
                act.wait_ge(turned, t + 1 + OPEN)
                nc.scalar.copy(uT[:, s, :].rearrange("p (b n) -> p b n", b=2), bank[:, 4:6, 0:4 * TT]).then_inc(moved, 1)
                act.wait_ge(logits, t + 1 + OPEN)
                nc.scalar.copy(c.logits[:, t, :], bank[0:TT, 6, 0:NR]).then_inc(kept, 1)

            for t in range(NT):
                s = t % 2
                act.wait_ge(added, t + 1 + OPEN)
                nc.scalar.activation(sq[:], h[:, s, :], ACT.Square, accum_out=ms[:, s:s + 1]).then_inc(squared, 1)
                act.wait_ge(squared, t + 1 + OPEN)
                nc.scalar.activation(rs[:, s:s + 1], ms[:, s:s + 1], ACT.Sqrt, bias=c.eps[0:TT, :],
                                     scale=1.0 / D).then_inc(rs_done, 1)
                if t >= 1:
                    move(t - 1)
            move(NT - 1)


def dispatch(nc, c):
    with ExitStack() as st:
        sb, ps, sem, begin = scope(nc, st)
        bias = sb("di_bias", [TT, NG + NE])
        iota = sb("di_iota", [128, NE])
        big = lambda name: sb(name, [TT, NT, NE])
        el, eq, oh1, oh2, O, pre, slot, t1, t2 = (big("di_" + n) for n in ("el", "eq", "oh1", "oh2", "O", "pre", "slot", "t1", "t2"))
        ge, goh = sb("di_ge", [TT, NT, NG]), sb("di_goh", [TT, NT, NG])
        sm = sb("di_small", [TT, 12, NT])
        M_, GSUM, GI, M1, I1, M2, I2, DF, E2, DEN = range(10)
        lt = sb("di_lt", [TT, TT])
        ones = sb("di_ones", [TT, 128])
        thr = sb("di_thr", [128, NE, 8])
        nov = sb("di_nov", [128, 6, NE])
        onesr = sb("di_onesr", [128, NE])
        ob = sb("di_ob", [128, OVER, NE])
        obi = sb("di_obi", [128, 1, OVER])
        of = sb("di_of", [128, 2, OVER])
        tid = sb("di_tid", [TT, NT], I32)
        zero = sb("di_zero", [NBLK, SLOTS], I32)
        sf = sb("di_sf", [TT, 2, NT])
        pR = ps("di_pR", [TT, 512])
        pC = ps("di_pC", [128, 512])
        made = sem("di_made")
        b_in = sem("di_b_in")
        vec = sem("di_vec")
        o_ready = sem("di_o_ready")
        g_exp = sem("di_g_exp")
        shifted = sem("di_shifted")
        e2_exp = sem("di_e2_exp")
        ranked = sem("di_ranked")
        slots_done = sem("di_slots_done")
        cleared = sem("di_cleared", 0)
        scattered = [sem(f"di_scattered{j}", 0) for j in range(2)]
        block = begin()

        @block.sync
        def _(sp):
            sp.dma_start(bias[:, 0:NG], c.router_group_b.to_broadcast([TT, NG])).then_inc(b_in, 16)
            sp.dma_start(bias[:, NG:], c.router_expert_b.to_broadcast([TT, NE])).then_inc(b_in, 16)

        @block.gpsimd
        def _(pool):
            nc.gpsimd.iota(iota[:], pattern=[[1, NE]], base=0, channel_multiplier=0,
                           allow_small_or_imprecise_dtypes=True).then_inc(made, 1)
            nc.gpsimd.iota(thr[:], pattern=[[0, NE], [SLOTS, 8]], base=SLOTS, channel_multiplier=0,
                           allow_small_or_imprecise_dtypes=True).then_inc(made, 1)
            nc.gpsimd.iota(obi[:], pattern=[[0, 1], [1, OVER]], base=0, channel_multiplier=0,
                           allow_small_or_imprecise_dtypes=True).then_inc(made, 1)
            nc.gpsimd.iota(tid[:], pattern=[[TT, NT]], base=0, channel_multiplier=1).then_inc(made, 1)
            nc.gpsimd.memset(ones[:], 1.0).then_inc(made, 1)
            nc.gpsimd.memset(onesr[:], 1.0).then_inc(made, 1)
            nc.gpsimd.memset(zero[:], 0).then_inc(made, 1)
            nc.gpsimd.memset(lt[:], 1.0).then_inc(made, 1)
            pool.wait_ge(made, 8 + OPEN)
            nc.gpsimd.affine_select(out=lt[:], in_=lt[:], compare_op=ALU.is_gt, fill=0.0, base=0,
                                    pattern=[[1, TT]], channel_multiplier=-1).then_inc(made, 1)
            pool.dma_start(c.slotD.rearrange("(b s) o -> b (s o)", s=SLOTS), zero[:]).then_inc(cleared, 16)
            pool.wait_ge(cleared, 16)
            pool.wait_ge(slots_done, 2 + OPEN)
            for t in range(NT):
                for j in range(2):
                    if t >= 1:
                        pool.wait_ge(scattered[j], 16 * t)
                    pool.indirect_dma_start(c.slotD, bass.IndirectOffsetOnAxis(ap=c.sidx[:, j, t:t + 1], axis=0),
                                            tid[:, t:t + 1], None).then_inc(scattered[j], 16)
            for j in range(2):
                pool.wait_ge(scattered[j], 16 * NT)

        @block.scalar
        def _(act):
            act.wait_ge(shifted, 1 + OPEN)
            nc.scalar.activation(ge[:], ge[:], ACT.Exp).then_inc(g_exp, 1)
            act.wait_ge(shifted, 2 + OPEN)
            nc.scalar.activation(sm[:, E2, :], sm[:, DF, :], ACT.Exp).then_inc(e2_exp, 1)

        @block.tensor
        def _(pe):
            pe.wait_ge(o_ready, 1 + OPEN)
            pe.wait_ge(made, 9 + OPEN)
            flat = lambda x: x.rearrange("p t e -> p (t e)")
            nc.tensor.matmul(pR[:, 0:NT * NE], lt[:], flat(O[:]), start=True, stop=False)
            nc.tensor.matmul(pR[:, 0:NT * NE], ones[:, 0:TT], flat(pre[:]), start=False, stop=True)
            nc.tensor.matmul(pC[:, 0:NE], ones[:], O[:, NT - 1, :], start=True, stop=False)
            nc.tensor.matmul(pC[:, 0:NE], ones[:], pre[:, NT - 1, :], start=False, stop=True).then_inc(ranked, 1)

        @block.vector
        def _(dve):
            tt, ts, red = nc.vector.tensor_tensor, nc.vector.tensor_scalar, nc.vector.tensor_reduce
            ch = Chain(dve, vec)
            over_g = lambda x: x.unsqueeze(2).to_broadcast([TT, NT, NG])
            over_e = lambda x: x.unsqueeze(2).to_broadcast([TT, NT, NE])
            iot = lambda n: iota[0:TT, 0:n].unsqueeze(1).to_broadcast([TT, NT, n])
            r = lambda k: sm[:, k, :]
            dve.wait_ge(made, 9 + OPEN)
            dve.wait_ge(b_in, 32 + OPEN)

            def first_max(vals, n, m, idx, oh, over):
                ch(red(r(m), vals, AX.X, ALU.max))
                ch(tt(oh, vals, over(r(m)), ALU.is_lt))
                ch(nc.vector.scalar_tensor_tensor(out=oh, in0=oh, scalar=1000.0, in1=iot(n), op0=ALU.mult, op1=ALU.add))
                ch(red(r(idx), oh, AX.X, ALU.min))
                ch(tt(oh, iot(n), over(r(idx)), ALU.is_equal))

            ch(tt(c.logits[:], c.logits[:], bias[:].unsqueeze(1).to_broadcast([TT, NT, NG + NE]), ALU.add))
            gl = c.logits[:, :, 0:NG]
            first_max(gl, NG, M_, GI, goh[:], over_g)
            tt(ge[:], gl, over_g(r(M_)), ALU.subtract).then_inc(shifted, 1)
            ch(ts(goh[:], goh[:], -1.0, BIG, ALU.add, ALU.mult))
            ch(tt(el[:].rearrange("p t (g e) -> p t g e", g=NG), c.logits[:, :, NG:].rearrange("p t (g e) -> p t g e", g=NG),
                  goh[:].unsqueeze(3).to_broadcast([TT, NT, NG, EG]), ALU.add))
            first_max(el[:], NE, M1, I1, oh1[:], over_e)
            ch(nc.vector.scalar_tensor_tensor(out=eq[:], in0=oh1[:], scalar=-3 * BIG, in1=el[:], op0=ALU.mult, op1=ALU.add))
            first_max(eq[:], NE, M2, I2, oh2[:], over_e)
            tt(r(DF), r(M2), r(M1), ALU.subtract).then_inc(shifted, 1)
            ch(tt(O[:], oh1[:], oh2[:], ALU.add))
            ch(nc.vector.memset(pre[:, 0, :], 0.0))
            for t in range(1, NT):
                ch(tt(pre[:, t, :], pre[:, t - 1, :], O[:, t - 1, :], ALU.add))
            dve.sem_inc(o_ready, 1)
            dve.wait_ge(g_exp, 1 + OPEN)
            ch(red(r(GSUM), ge[:], AX.X, ALU.add))
            dve.wait_ge(e2_exp, 1 + OPEN)
            ch(ts(r(DEN), r(E2), 1.0, None, ALU.add))
            ch(tt(r(DEN), r(DEN), r(GSUM), ALU.mult))
            ch(nc.vector.reciprocal(c.gate[:, 0, :], r(DEN)))
            ch(tt(c.gate[:, 1, :], c.gate[:, 0, :], r(E2), ALU.mult))
            dve.wait_ge(ranked, 1 + OPEN)
            CNT, N_, INC, B1, B2, DB = range(6)
            v = lambda k: nov[:, k, :]
            ch(nc.vector.tensor_copy(v(CNT), pC[:, 0:NE]))
            ch(tt(thr[:], thr[:], v(CNT).unsqueeze(2).to_broadcast([128, NE, 8]), ALU.is_lt))
            ch(red(v(N_), thr[:], AX.X, ALU.add))
            ch(nc.vector.tensor_tensor_scan(v(INC), onesr[:], v(N_), 0.0, ALU.mult, ALU.add))
            ch(ts(v(B1), iota[:], float(SLOTS), None, ALU.mult))
            ch(tt(v(B2), v(INC), v(N_), ALU.subtract))
            ch(ts(v(B2), v(B2), float(SLOTS), float((NE - 1) * SLOTS), ALU.mult, ALU.add))
            ch(tt(v(DB), v(B2), v(B1), ALU.subtract))
            bc = lambda k: nov[0:TT, k, :].unsqueeze(1).to_broadcast([TT, NT, NE])
            ch(nc.vector.tensor_copy(slot[:].rearrange("p t e -> p (t e)"), pR[:, 0:NT * NE]))
            ch(ts(t1[:], slot[:], float(SLOTS), None, ALU.is_ge))
            ch(tt(t1[:], t1[:], bc(DB), ALU.mult))
            ch(tt(slot[:], slot[:], bc(B1), ALU.add))
            ch(tt(slot[:], slot[:], t1[:], ALU.add))
            for j, oh in enumerate((oh1, oh2)):
                ch(tt(t2[:], slot[:], oh[:], ALU.mult))
                ch(red(sf[:, j, :], t2[:], AX.X, ALU.add))
                nc.vector.tensor_copy(c.sidx[:, j, :], sf[:, j, :]).then_inc(slots_done, 1)
            ch(tt(ob[:], nov[:, INC, :].unsqueeze(1).to_broadcast([128, OVER, NE]),
                  obi[:, 0, :].unsqueeze(2).to_broadcast([128, OVER, NE]), ALU.is_le))
            ch(red(of[:, 0, :], ob[:], AX.X, ALU.add))
            ch(ts(of[:, 1, :], of[:, 0, :], float(NE), None, ALU.is_lt))
            ch(ts(of[:, 0, :], of[:, 0, :], float(NE - 1), None, ALU.min))
            ch(nc.vector.tensor_copy(c.over[:], of[0:1, :, :]))


def experts(nc, c):
    with ExitStack() as st:
        sb, ps, sem, begin = scope(nc, st)
        wgu = sb("ex_wgu", [128, 2, 2, KD, FF])
        wd = sb("ex_wd", [128, 2, FF // 128, D])
        idx = sb("ex_idx", [SLOTS, 2], U32)
        x = sb("ex_x", [SLOTS, 2, D])
        xT = sb("ex_xT", [128, 2, KD, SLOTS])
        sg = sb("ex_sg", [SLOTS, FF])
        hid = sb("ex_hid", [SLOTS, FF])
        hT = sb("ex_hT", [128, FF // 128, SLOTS])
        y = sb("ex_y", [SLOTS, 2, D])
        bank = ps("ex_bank", [128, 8, 512])
        idx_in = [sem(f"ex_idx_in{s}", 0) for s in range(2)]
        gathered = [sem(f"ex_gathered{s}", 0) for s in range(2)]
        wgu_in = [sem(f"ex_wgu_in{s}") for s in range(2)]
        wd_in = [sem(f"ex_wd_in{s}") for s in range(2)]
        asked, over_stored = sem("ex_asked"), sem("ex_over_stored")
        x_turned, x_moved = sem("ex_x_turned"), sem("ex_x_moved")
        gu_done, opened, silu, mixed = sem("ex_gu_done"), sem("ex_opened"), sem("ex_silu"), sem("ex_mixed")
        h_turned, h_moved = sem("ex_h_turned"), sem("ex_h_moved")
        down = sem("ex_down")
        y_moved = [sem(f"ex_y_moved{s}") for s in range(2)]
        y_out = [sem(f"ex_y_out{s}") for s in range(2)]
        block = begin()
        FK = FF // 128
        wg_v = c.expert_w_gate.rearrange("o e (p k) f -> (o e) p k f", k=KD)
        wu_v = c.expert_w_up.rearrange("o e (p k) f -> (o e) p k f", k=KD)
        wd_v = c.expert_w_down.rearrange("o e (p k) f -> (o e) p k f", k=FK)
        pick = lambda ap, e: ap[bass.ds(e, 1)].rearrange("o p k f -> (o p) k f")

        def load_weights(sp, s, e):
            sp.dma_start(wgu[:, s, 0], pick(wg_v, e)).then_inc(wgu_in[s], 16)
            sp.dma_start(wgu[:, s, 1], pick(wu_v, e)).then_inc(wgu_in[s], 16)
            sp.dma_start(wd[:, s], pick(wd_v, e)).then_inc(wd_in[s], 16)

        @block.sync
        def _(sp):
            for s in range(2):
                load_weights(sp, s, s)
            with sp.Fori(1, NE // 2) as i:
                for s in range(2):
                    sp.wait_ge(down, 2 * i + s - 1 + OPEN)
                    load_weights(sp, s, 2 * i + s)
            expert = sp.alloc_register("ex_sp_expert")
            used = sp.alloc_register("ex_sp_used")
            with sp.Fori(0, OVER) as n:
                sp.reg_load(used, c.over[0:1, 1, bass.ds(n, 1)])
                with sp.If_ne(used, 0):
                    sp.reg_load(expert, c.over[0:1, 0, bass.ds(n, 1)])
                    sp.wait_ge(down, n + NE + OPEN)
                    load_weights(sp, 0, sp.snap(expert, min_val=0, max_val=NE - 1))

        @block.gpsimd
        def _(pool):
            def gather(s, n, times):
                pool.dma_start(idx[:, s:s + 1], c.slotD[bass.ds(n * SLOTS, SLOTS), :].bitcast(U32)).then_inc(idx_in[s], 16)
                pool.wait_ge(idx_in[s], 16 * times + 16)
                pool.sem_inc(asked, 1)
                pool.indirect_dma_start(x[:, s, :], None, c.u2D, bass.IndirectOffsetOnAxis(ap=idx[:, s:s + 1], axis=0)).then_inc(gathered[s], 16)

            with pool.Fori(0, NE // 2) as i:
                for s in range(2):
                    pool.wait_ge(x_turned, 2 * i + OPEN)
                    gather(s, 2 * i + s, i)
            used = pool.alloc_register("ex_pool_used")
            with pool.Fori(0, OVER) as n:
                pool.reg_load(used, c.over[0:1, 1, bass.ds(n, 1)])
                with pool.If_ne(used, 0):
                    pool.wait_ge(x_turned, n + NE + OPEN)
                    gather(0, n + NE, n + NE // 2)

        def turn_x(pe, s, n, times):
            pe.wait_ge(gathered[s], 16 * times + 16)
            pe.wait_ge(x_moved, n + OPEN)
            for k in range(KD):
                last = nc.tensor.transpose(bank[:, k // 4, (k % 4) * 128:(k % 4 + 1) * 128], x[:, s, k::KD], c.ident[:])
            last.then_inc(x_turned, 1)

        def gate_up(pe, s, n, times):
            pe.wait_ge(x_moved, n + 1 + OPEN)
            pe.wait_ge(wgu_in[s], 32 * times + 32 + OPEN)
            pe.wait_ge(mixed, n + OPEN)
            for j in range(2):
                for k in range(KD):
                    last = nc.tensor.matmul(bank[:, 2 + j, :], xT[:, s, k, :], wgu[:, s, j, k, :],
                                            start=(k == 0), stop=(k == KD - 1))
            last.then_inc(gu_done, 1)

        def turn_h(pe, s, n, times):
            pe.wait_ge(mixed, n + 1 + OPEN)
            for k in range(FK):
                last = nc.tensor.transpose(bank[:, 4, k * 128:(k + 1) * 128], hid[:, k::FK], c.ident[:])
            last.then_inc(h_turned, 1)

        def project(pe, s, n, times):
            pe.wait_ge(h_moved, n + 1 + OPEN)
            pe.wait_ge(wd_in[s], 16 * times + 16 + OPEN)
            for o in range(2):
                pe.wait_ge(y_moved[o], n + OPEN)
                for k in range(FK):
                    last = nc.tensor.matmul(bank[:, 5 + o, :], hT[:, k, :], wd[:, s, k, o * 512:(o + 1) * 512],
                                            start=(k == 0), stop=(k == FK - 1))
            last.then_inc(down, 1)

        @block.tensor
        def _(pe):
            turn_x(pe, 0, 0, 0)
            with pe.Fori(0, NE // 2 - 1) as i:
                for s in range(2):
                    gate_up(pe, s, 2 * i + s, i)
                    turn_x(pe, 1 - s, 2 * i + s + 1, i + s)
                    turn_h(pe, s, 2 * i + s, i)
                    project(pe, s, 2 * i + s, i)
            i = NE // 2 - 1
            for s in range(2):
                gate_up(pe, s, 2 * i + s, i)
                if s == 0:
                    turn_x(pe, 1, 2 * i + 1, i)
                turn_h(pe, s, 2 * i + s, i)
                project(pe, s, 2 * i + s, i)
            used = pe.alloc_register("ex_pe_used")
            with pe.Fori(0, OVER) as n:
                pe.reg_load(used, c.over[0:1, 1, bass.ds(n, 1)])
                with pe.If_ne(used, 0):
                    for step in (turn_x, gate_up, turn_h, project):
                        step(pe, 0, n + NE, n + NE // 2)

        def move_x(act, s, n):
            act.wait_ge(x_turned, n + 1 + OPEN)
            nc.scalar.copy(xT[:, s].rearrange("p (b k) t -> p b (k t)", b=2), bank[:, 0:2, :]).then_inc(x_moved, 1)

        def open_gate(act, n):
            act.wait_ge(gu_done, n + 1 + OPEN)
            nc.scalar.activation(sg[:], bank[:, 2, :], ACT.Sigmoid).then_inc(opened, 1)

        def move_h(act, n):
            act.wait_ge(h_turned, n + 1 + OPEN)
            nc.scalar.copy(hT[:].rearrange("p k t -> p (k t)"), bank[:, 4, :]).then_inc(h_moved, 1)

        def move_y(eng, s, n, times, o):
            eng.wait_ge(down, n + 1 + OPEN)
            eng.wait_ge(y_out[s], 16 * times + OPEN)
            copy = nc.scalar.copy if o == 0 else nc.vector.tensor_copy
            copy(y[:, s, o * 512:(o + 1) * 512], bank[:, 5 + o, :]).then_inc(y_moved[o], 1)

        def store_y(act, s, n):
            for o in range(2):
                act.wait_ge(y_moved[o], n + 1 + OPEN)
            act.dma_start(c.yD[bass.ds(n * SLOTS, SLOTS), :], y[:, s, :]).then_inc(y_out[s], 16)

        @block.scalar
        def _(act):
            move_x(act, 0, 0)
            with act.Fori(0, NE // 2 - 1) as i:
                for s in range(2):
                    n = 2 * i + s
                    open_gate(act, n)
                    move_x(act, 1 - s, n + 1)
                    move_h(act, n)
                    move_y(act, s, n, i, 0)
                    store_y(act, s, n)
            i = NE // 2 - 1
            for s in range(2):
                n = 2 * i + s
                open_gate(act, n)
                if s == 0:
                    move_x(act, 1, n + 1)
                move_h(act, n)
                move_y(act, s, n, i, 0)
                store_y(act, s, n)
            used = act.alloc_register("ex_act_used")
            with act.Fori(0, OVER) as n:
                act.reg_load(used, c.over[0:1, 1, bass.ds(n, 1)])
                with act.If_ne(used, 0):
                    move_x(act, 0, n + NE)
                    open_gate(act, n + NE)
                    move_h(act, n + NE)
                    move_y(act, 0, n + NE, n + NE // 2, 0)
                    store_y(act, 0, n + NE)
                    act.wait_ge(y_out[0], 16 * (n + NE // 2 + 1) + OPEN)
                    act.sem_inc(over_stored, 1)
            for s in range(2):
                act.wait_ge(y_out[s], 16 * NE // 2 + OPEN)

        def mix(dve, n):
            dve.wait_ge(opened, n + 1 + OPEN)
            dve.wait_ge(h_turned, n + OPEN)
            nc.vector.tensor_tensor(hid[:], bank[:, 2, :], sg[:], ALU.mult).then_inc(silu, 1)
            dve.wait_ge(silu, n + 1 + OPEN)
            nc.vector.tensor_tensor(hid[:], bank[:, 3, :], hid[:], ALU.mult).then_inc(mixed, 1)

        @block.vector
        def _(dve):
            with dve.Fori(0, NE // 2) as i:
                for s in range(2):
                    mix(dve, 2 * i + s)
                    move_y(dve, s, 2 * i + s, i, 1)
            used = dve.alloc_register("ex_dve_used")
            with dve.Fori(0, OVER) as n:
                dve.reg_load(used, c.over[0:1, 1, bass.ds(n, 1)])
                with dve.If_ne(used, 0):
                    mix(dve, n + NE)
                    move_y(dve, 0, n + NE, n + NE // 2, 1)


def combine(nc, c):
    with ExitStack() as st:
        sb, ps, sem, begin = scope(nc, st)
        h = sb("co_h", [TT, 2, D])
        y = sb("co_y", [TT, 2, 2, D])
        h_in = [sem(f"co_h_in{s}") for s in range(2)]
        y_in = [[sem(f"co_y_in{s}{j}", 0) for j in range(2)] for s in range(2)]
        half = sem("co_half")
        summed = sem("co_summed")
        out = [sem(f"co_out{s}") for s in range(2)]
        block = begin()

        @block.sync
        def _(sp):
            for t in range(NT):
                if t >= 2:
                    sp.wait_ge(out[t % 2], 16 * (t // 2) + OPEN)
                sp.dma_start(h[:, t % 2, :], c.h2D[t]).then_inc(h_in[t % 2], 16)

        @block.gpsimd
        def _(pool):
            for t in range(NT):
                if t >= 2:
                    pool.wait_ge(summed, t - 1 + OPEN)
                for j in range(2):
                    pool.indirect_dma_start(y[:, t % 2, j, :], None, c.yD,
                                            bass.IndirectOffsetOnAxis(ap=c.sidx[:, j, t:t + 1], axis=0)).then_inc(y_in[t % 2][j], 16)

        @block.vector
        def _(dve):
            for t in range(NT):
                s = t % 2
                dve.wait_ge(h_in[s], 16 * (t // 2) + 16 + OPEN)
                dve.wait_ge(y_in[s][0], 16 * (t // 2) + 16)
                nc.vector.scalar_tensor_tensor(out=h[:, s, :], in0=y[:, s, 0, :], scalar=c.gate[:, 0, t:t + 1], in1=h[:, s, :],
                                               op0=ALU.mult, op1=ALU.add).then_inc(half, 1)
                dve.wait_ge(half, t + 1 + OPEN)
                dve.wait_ge(y_in[s][1], 16 * (t // 2) + 16)
                nc.vector.scalar_tensor_tensor(out=h[:, s, :], in0=y[:, s, 1, :], scalar=c.gate[:, 1, t:t + 1], in1=h[:, s, :],
                                               op0=ALU.mult, op1=ALU.add).then_inc(summed, 1)

        @block.scalar
        def _(act):
            for t in range(NT):
                act.wait_ge(summed, t + 1 + OPEN)
                if t == 0:
                    act.dma_start(c.out[0, 0:TT - META, :], h[META:TT, 0, :]).then_inc(out[0], 16)
                else:
                    act.dma_start(c.out[0, t * TT - META:(t + 1) * TT - META, :], h[:, t % 2, :]).then_inc(out[t % 2], 16)
            for s in range(2):
                act.wait_ge(out[s], 16 * NT // 2 + OPEN)


def build(nc, ins, out, cst, upto=99, skip_at=False):
    c = Shared()
    c.x = ins["x"]
    c.meta_tokens = ins["meta_tokens"]
    c.norm1_w = ins["norm1_w"]
    c.w_in = ins["w_in"]
    c.rwkv_mu = ins["rwkv_mu"]
    c.rwkv_w0 = ins["rwkv_w0"]
    c.rwkv_w2 = ins["rwkv_w2"]
    c.rwkv_a0 = ins["rwkv_a0"]
    c.rwkv_a2 = ins["rwkv_a2"]
    c.rwkv_g2 = ins["rwkv_g2"]
    c.rwkv_k_k = ins["rwkv_k_k"]
    c.rwkv_k_a = ins["rwkv_k_a"]
    c.rwkv_r_k = ins["rwkv_r_k"]
    c.rwkv_ln_w = ins["rwkv_ln_w"]
    c.rwkv_ln_b = ins["rwkv_ln_b"]
    c.q_norm_w = ins["q_norm_w"]
    c.k_norm_w = ins["k_norm_w"]
    c.lambda_q1 = ins["lambda_q1"]
    c.lambda_k1 = ins["lambda_k1"]
    c.lambda_q2 = ins["lambda_q2"]
    c.lambda_k2 = ins["lambda_k2"]
    c.diff_subln_w = ins["diff_subln_w"]
    c.w_branch_rwkv = ins["w_branch_rwkv"]
    c.w_branch_diff = ins["w_branch_diff"]
    c.w_out = ins["w_out"]
    c.norm2_w = ins["norm2_w"]
    c.router_group_w = ins["router_group_w"]
    c.router_group_b = ins["router_group_b"]
    c.router_expert_w = ins["router_expert_w"]
    c.router_expert_b = ins["router_expert_b"]
    c.expert_w_gate = ins["expert_w_gate"]
    c.expert_w_up = ins["expert_w_up"]
    c.expert_w_down = ins["expert_w_down"]
    c.rope_cos = cst["rope_cos"]
    c.rope_sin = cst["rope_sin"]
    c.mask4 = cst["mask4"]
    c.maskn = cst["maskn"]
    c.out = out
    dram = lambda name, shape, dt=F32: nc.dram_tensor(name, shape, dt, kind="Internal").ap()
    c.qkT = dram("s_qkT", [2 * DH, 128, T])
    c.vD = dram("s_v", [NT, TT, D])
    c.yrT = dram("s_yrT", [KD, 128, T])
    c.h2D = dram("s_h2", [NT, TT, D])
    c.u2D = dram("s_u2", [T, D])
    c.slotD = dram("s_slot", [NBLK * SLOTS, 1], I32)
    c.yD = dram("s_y", [NBLK * SLOTS, D])
    c.oD = dram("s_o", [NT, TT, D])
    c.pT = dram("s_pT", [RT + GT, 128, T])
    with ExitStack() as st:
        sb = lambda name, shape, dt=F32: st.enter_context(nc.sbuf_tensor(name, shape, dt))
        c.ident = sb("ident", [128, 128])
        c.eps = sb("eps", [128, 1])
        c.logits = sb("logits", [TT, NT, NG + NE])
        c.gate = sb("gate", [TT, 2, NT])
        c.sidx = sb("sidx", [TT, 2, NT], U32)
        c.over = sb("over", [1, 2, OVER], I32)
        c.o_ms = sb("o_ms", [TT, NT, DH])
        constants(nc, c)
        with ExitStack() as st2:
            c.uT = st2.enter_context(nc.sbuf_tensor("uT", [128, KD, T], F32))
            norm1(nc, c)
            if upto >= 2:
                project_features(nc, c)
            project_heads(nc, c)
        if upto >= 3 and not skip_at:
            attention(nc, c)
        if upto >= 4:
            rwkv(nc, c)
        if upto >= 5:
            with ExitStack() as st2:
                c.mT = st2.enter_context(nc.sbuf_tensor("mT", [128, KD, T], F32))
                merge_branches(nc, c)
                output_and_route(nc, c)
            dispatch(nc, c)
            experts(nc, c)
            combine(nc, c)


def rope_tables():
    half = ROPE // 2
    freq = np.exp(np.float32(-math.log(THETA)) * np.arange(half, dtype=np.float32) * np.float32(2.0) / np.float32(ROPE))
    ang = np.arange(T, dtype=np.float32)[:, None] * freq[None, :].astype(np.float32)
    cos, sin = np.cos(ang), np.sin(ang)
    tiles = lambda a: np.ascontiguousarray(a.reshape(NT, TT, ROPE).transpose(1, 0, 2).astype(np.float32))
    return tiles(np.concatenate([cos, cos], 1)), tiles(np.concatenate([-sin, sin], 1))


def chunk_masks():
    p, f = np.arange(TT)[:, None], np.arange(TT)[None, :]
    same = p // SUB == f // SUB
    mask4 = np.stack([-1.0 * (same & (p < f)), 1.0 * (p <= f), 1.0 * (p < f), 1.0 * (p <= f)], 1)
    maskn = np.stack([-1.0 * (same & (p > f)), -1.0 * (~same & (p > f))], 1)
    return mask4.astype(np.float32), maskn.astype(np.float32)


_CONST = dict(zip(("rope_cos", "rope_sin", "mask4", "maskn"), rope_tables() + chunk_masks()))


def kernel(**inputs):
    import concourse.bacc as bacc
    from concourse.bass_utils import run_bass_kernel_spmd
    nc = bacc.Bacc("TRN2", target_bir_lowering=False, num_devices=1)
    arrays, ins = {}, {}
    for name, a in inputs.items():
        a = np.ascontiguousarray(a)
        arrays["in_" + name] = a
        ins[name] = nc.dram_tensor("in_" + name, a.shape, mybir.dt.from_np(a.dtype), kind="ExternalInput").ap()
    cst = {}
    for name, a in _CONST.items():
        arrays["const_" + name] = a
        cst[name] = nc.dram_tensor("const_" + name, a.shape, mybir.dt.from_np(a.dtype), kind="ExternalInput").ap()
    out = nc.dram_tensor("out_0", [1, SEQ, D], F32, kind="ExternalOutput").ap()
    build(nc, ins, out, cst)
    r = run_bass_kernel_spmd(nc, [arrays], core_ids=[0])
    return r.results[0]["out_0"]
```

```python
import math
from contextlib import ExitStack

import numpy as np
import concourse.bass as bass
from concourse import mybir

F32 = mybir.dt.float32
F32R = mybir.dt.float32r
I32 = mybir.dt.int32
U32 = mybir.dt.uint32
ALU = mybir.AluOpType
ACT = mybir.ActivationFunctionType
AX = mybir.AxisListType

META, SEQ, D = 16, 1024, 1024
T = META + SEQ
TT = 104
NT = T // TT
KD = D // 128
EPS = 1e-6
RH, RD = 16, 64
LW, LA, LG = 64, 64, 128
RWKV_COLS = 3 * D + LW + LA + LG
RT = RWKV_COLS // 128
GT = 2 * D // 128
DH, DD = 8, 64
DIFF_COL = RWKV_COLS
GATE_COL = RWKV_COLS + 3 * D
ROPE, THETA = DD // 4, 500000.0
OPEN = 16
NCOL = 4
CW = T // NCOL


class Shared:
    pass


class Chain:

    def __init__(self, eng, sem, start=0):
        self.eng, self.sem, self.n = eng, sem, start

    def __call__(self, ins):
        self.n += 1
        ins.then_inc(self.sem, 1)
        self.eng.wait_ge(self.sem, self.n + OPEN)


def scope(nc, st):
    def sb(name, shape, dt=F32):
        return st.enter_context(nc.sbuf_tensor(name, shape, dt))

    def ps(name, shape):
        return st.enter_context(nc.psum_tensor(name, shape, F32))

    sems = []

    def sem(name, first=OPEN):
        sems.append((nc.alloc_semaphore(name), first))
        return sems[-1][0]

    def begin():
        for x, first in sems:
            if first:
                nc.gpsimd.sem_inc(x, first)
        nc.all_engine_barrier()
        return st.enter_context(nc.Block())

    st.callback(lambda: nc.clear_and_free_semaphores([x for x, _ in sems]))
    return sb, ps, sem, begin


def constants(nc, c):
    with ExitStack() as st:
        sb, ps, sem, begin = scope(nc, st)
        zeroed = sem("ident_zeroed")
        block = begin()

        @block.gpsimd
        def _(pool):
            nc.gpsimd.memset(c.eps[:], EPS).then_inc(zeroed, 1)
            nc.gpsimd.memset(c.ident[:], 0.0).then_inc(zeroed, 1)
            pool.wait_ge(zeroed, 2 + OPEN)
            nc.gpsimd.affine_select(out=c.ident[:], in_=c.ident[:], compare_op=ALU.not_equal, fill=1.0,
                                    base=0, pattern=[[-1, 128]], channel_multiplier=1).then_inc(zeroed, 1)
            pool.wait_ge(zeroed, 3 + OPEN)


def norm1(nc, c):
    with ExitStack() as st:
        sb, ps, sem, begin = scope(nc, st)
        h = sb("n1_h", [TT, 2, D])
        sq = sb("n1_sq", [TT, D])
        ms = sb("n1_ms", [TT, 2])
        rs = sb("n1_rs", [TT, 2])
        ri = sb("n1_ri", [TT, 2])
        u = sb("n1_u", [TT, 2, D])
        w = sb("n1_w", [128, KD])
        v = sb("n1_v", [128, 2, KD, TT])
        pt = ps("n1_pt", [128, 2, 2, 512])
        w_in = sem("n1_w_in")
        h_in = [sem(f"n1_h_in{s}") for s in range(2)]
        h_used = sem("n1_h_used")
        sq_done = sem("n1_sq_done")
        u_done = sem("n1_u_done")
        t_done = sem("n1_t_done")
        scaled = sem("n1_scaled")
        high = sem("n1_high")
        low = sem("n1_low")
        rs_done = sem("n1_rs_done")
        vec = sem("n1_vec")
        block = begin()

        @block.sync
        def _(sp):
            sp.dma_start(w[:], c.norm1_w.rearrange("o (p k) -> p (o k)", k=KD)).then_inc(w_in, 16)
            sp.dma_start(h[0:META, 0, :], c.meta_tokens).then_inc(h_in[0], 16)
            sp.dma_start(h[META:TT, 0, :], c.x[0, 0:TT - META, :]).then_inc(h_in[0], 16)
            sp.dma_start(h[:, 1, :], c.x[0, TT - META:2 * TT - META, :]).then_inc(h_in[1], 16)
            with sp.Fori(1, NT // 2) as i:
                for s in range(2):
                    sp.wait_ge(h_used, 2 * i + s - 1 + OPEN)
                    sp.dma_start(h[:, s, :], c.x[0, bass.ds((2 * i + s) * TT - META, TT), :]).then_inc(h_in[s], 16)

        @block.scalar
        def _(act):
            with act.Fori(0, NT // 2) as i:
                for s in range(2):
                    act.wait_ge(h_in[s], 16 * i + (32 if s == 0 else 16) + OPEN)
                    nc.scalar.activation(sq[:], h[:, s, :], ACT.Square,
                                         accum_out=ms[:, s:s + 1]).then_inc(sq_done, 1)
                    act.wait_ge(sq_done, 2 * i + s + 1 + OPEN)
                    nc.scalar.activation(rs[:, s:s + 1], ms[:, s:s + 1], ACT.Sqrt, bias=c.eps[0:TT, :],
                                         scale=1.0 / D).then_inc(rs_done, 1)
                    act.wait_ge(scaled, 4 * i + 2 * s + 2 + OPEN)
                    nc.scalar.copy(c.uH[:, :, bass.ds((2 * i + s) * TT, TT)], v[:, s]).then_inc(high, 1)

        @block.vector
        def _(dve):
            dve.wait_ge(w_in, 16 + OPEN)
            with dve.Fori(0, NT // 2) as i:
                for s in range(2):
                    dve.wait_ge(rs_done, 2 * i + s + 1 + OPEN)
                    nc.vector.reciprocal(ri[:, s:s + 1], rs[:, s:s + 1]).then_inc(vec, 1)
                    dve.wait_ge(vec, 2 * i + s + 1 + OPEN)
                    dve.wait_ge(t_done, 2 * i + s + OPEN)
                    nc.vector.tensor_scalar(u[:, s, :], h[:, s, :], ri[:, s:s + 1], None, ALU.mult).then_inc(u_done, 1)
                    dve.wait_ge(u_done, 2 * i + s + 1 + OPEN)
                    dve.sem_inc(h_used, 1)
                    dve.wait_ge(t_done, 2 * i + s + 1 + OPEN)
                    for b in range(2):
                        nc.vector.tensor_tensor(
                            v[:, s, 4 * b:4 * b + 4, :], pt[:, s, b, 0:4 * TT].rearrange("p (k t) -> p k t", k=4),
                            w[:, 4 * b:4 * b + 4].unsqueeze(2).to_broadcast([128, 4, TT]), ALU.mult).then_inc(scaled, 1)
                    dve.wait_ge(high, 2 * i + s + 1 + OPEN)
                    here = bass.ds((2 * i + s) * TT, TT)
                    nc.vector.tensor_tensor(c.uL[:, :, here], v[:, s], c.uH[:, :, here], ALU.subtract).then_inc(low, 1)
            dve.wait_ge(low, NT + OPEN)

        @block.tensor
        def _(pe):
            with pe.Fori(0, NT // 2) as i:
                for s in range(2):
                    pe.wait_ge(u_done, 2 * i + s + 1 + OPEN)
                    pe.wait_ge(scaled, 4 * i + OPEN)
                    for k in range(KD):
                        last = nc.tensor.transpose(pt[:, s, k // 4, (k % 4) * TT:(k % 4 + 1) * TT],
                                                   u[:, s, k::KD], c.ident[0:TT, 0:TT])
                    last.then_inc(t_done, 1)


def project_features(nc, c):
    with ExitStack() as st:
        sb, ps, sem, begin = scope(nc, st)
        w = sb("pf_w", [128, 2, KD, 128])
        wH = sb("pf_wH", [128, 2, KD, 128], F32R)
        wL = sb("pf_wL", [128, 2, KD, 128], F32R)
        ev = sb("pf_ev", [128, 2, T])
        acc = ps("pf_acc", [128, 2, NCOL, 512])
        w_ready = [sem(f"pf_w_ready{s}") for s in range(2)]
        high = [sem(f"pf_high{s}") for s in range(2)]
        low = [sem(f"pf_low{s}") for s in range(2)]
        product = [sem(f"pf_product{s}") for s in range(2)]
        copied = [sem(f"pf_copied{s}") for s in range(2)]
        stored = [sem(f"pf_stored{s}") for s in range(2)]
        zero = sb("pf_zero", [SLOTS, D])
        zeroed = sem("pf_zeroed")
        cleared = sem("pf_cleared")
        w_v = c.w_in.rearrange("o (p k) f -> p (o k) f", k=KD)
        block = begin()
        RI, GI = RT // 2, GT // 2

        @block.gpsimd
        def _(pool):
            nc.gpsimd.memset(zero[:], 0.0).then_inc(zeroed, 1)

        @block.sync
        def _(sp):
            for s in range(2):
                sp.dma_start(w[:, s], w_v[:, :, s * 128:s * 128 + 128]).then_inc(w_ready[s], 16)
            sp.wait_ge(zeroed, 1 + OPEN)
            with sp.Fori(NE, NBLK) as n:
                sp.dma_start(c.yD[bass.ds(n * SLOTS, SLOTS), :], zero[:]).then_inc(cleared, 16)
            for lo, hi, shift in ((1, RI, 0), (RI, RI + GI, GATE_COL - RWKV_COLS)):
                with sp.Fori(lo, hi) as i:
                    for s in range(2):
                        sp.wait_ge(low[s], i + OPEN)
                        sp.dma_start(w[:, s], w_v[:, :, bass.ds((2 * i + s) * 128 + shift, 128)]).then_inc(w_ready[s], 16)
            for s in range(2):
                sp.wait_ge(low[s], RI + GI + OPEN)
                sp.dma_start(w[:, s], w_v[:, :, s * 128:s * 128 + 128]).then_inc(w_ready[s], 16)
            sp.wait_ge(cleared, 16 * OVER + OPEN)

        @block.tensor
        def _(pe):
            with pe.Fori(0, RI + GI) as i:
                for s in range(2):
                    pe.wait_ge(low[s], i + 1 + OPEN)
                    pe.wait_ge(copied[s], i + OPEN)
                    for k in range(KD):
                        for j, (ww, uu) in enumerate(((wH, c.uH), (wH, c.uL), (wL, c.uH))):
                            for n in range(NCOL):
                                last = nc.tensor.matmul(acc[:, s, n, 0:CW], ww[:, s, k, :],
                                                        uu[:, k, n * CW:(n + 1) * CW],
                                                        start=(k == 0 and j == 0), stop=(k == KD - 1 and j == 2))
                    last.then_inc(product[s], 1)

        def read_out(eng, s, i):
            eng.wait_ge(product[s], i + 1 + OPEN)
            eng.wait_ge(stored[s], 16 * i + OPEN)

        def split_high(act, s, i):
            act.wait_ge(w_ready[s], 16 * i + 16 + OPEN)
            act.wait_ge(product[s], i + OPEN)
            nc.scalar.copy(wH[:, s], w[:, s]).then_inc(high[s], 1)

        def split_low(dve, s, i):
            dve.wait_ge(high[s], i + 1 + OPEN)
            nc.vector.tensor_tensor(wL[:, s], w[:, s], wH[:, s], ALU.subtract).then_inc(low[s], 1)

        @block.scalar
        def _(act):
            split_high(act, 0, 0)
            split_high(act, 1, 0)
            with act.Fori(0, RI + GI) as i:
                read_out(act, 0, i)
                nc.scalar.copy(ev[:, 0, :].rearrange("p (n t) -> p n t", n=NCOL),
                               acc[:, 0, :, 0:CW]).then_inc(copied[0], 1)
                for s in range(2):
                    act.wait_ge(copied[s], i + 1 + OPEN)
                    split_high(act, s, i + 1)
                    act.dma_start(c.pT[bass.ds(2 * i + s, 1)].rearrange("o p t -> (o p) t"),
                                  ev[:, s, :]).then_inc(stored[s], 16)
            for s in range(2):
                act.wait_ge(stored[s], 16 * (RI + GI) + OPEN)

        @block.vector
        def _(dve):
            split_low(dve, 0, 0)
            split_low(dve, 1, 0)
            with dve.Fori(0, RI + GI) as i:
                split_low(dve, 0, i + 1)
                read_out(dve, 1, i)
                nc.vector.tensor_copy(ev[:, 1, :].rearrange("p (n t) -> p n t", n=NCOL),
                                      acc[:, 1, :, 0:CW]).then_inc(copied[1], 1)
                split_low(dve, 1, i + 1)


def project_heads(nc, c):
    NB = 2 * D // 512
    G = 512 // DD
    with ExitStack() as st:
        sb, ps, sem, begin = scope(nc, st)
        w = sb("ph_w", [128, KD, 512])
        wH = sb("ph_wH", [128, 2, KD, 512], F32R)
        wL = sb("ph_wL", [128, 2, KD, 512], F32R)
        nw = sb("ph_norm_w", [TT, 2, DD])
        cos = sb("ph_cos", [TT, NT, ROPE])
        sin = sb("ph_sin", [TT, NT, ROPE])
        sq = sb("ph_sq", [TT, 2, 512])
        ms = sb("ph_ms", [TT, 2, G])
        rs = sb("ph_rs", [TT, 2, G])
        ri = sb("ph_ri", [TT, 2, G])
        qn = sb("ph_qn", [TT, 2, 512])
        ra = sb("ph_ra", [TT, G, ROPE])
        rb = sb("ph_rb", [TT, G, ROPE])
        stg = sb("ph_stg", [128, 2, 4, T])
        vst = sb("ph_vst", [TT, 2, 512])
        acc = ps("ph_acc", [TT, 2, 512])
        tp = ps("ph_tp", [128, 2, 512])
        tables = sem("ph_tables")
        scaled = sem("ph_scaled")
        w_ready = sem("ph_w_ready")
        high = sem("ph_high")
        low = sem("ph_low")
        product = sem("ph_product")
        sq_done = sem("ph_sq_done")
        ms_done = sem("ph_ms_done")
        rs_done = sem("ph_rs_done")
        vec = sem("ph_vec")
        normed = sem("ph_normed")
        roped = sem("ph_roped")
        rope_step = sem("ph_rope_step")
        turned = sem("ph_turned")
        staged = sem("ph_staged")
        stored = [sem(f"ph_stored{s}") for s in range(2)]
        v_copied = sem("ph_v_copied")
        v_stored = [sem(f"ph_v_stored{s}") for s in range(2)]
        block = begin()
        w_v = c.w_in.rearrange("o (p k) f -> p (o k) f", k=KD)
        U = 2 * NT
        NI = NB // 2
        QK = NI * U

        @block.sync
        def _(sp):
            for j, src in enumerate((c.q_norm_w, c.k_norm_w)):
                sp.dma_start(nw[:, j, :], src.to_broadcast([TT, DD])).then_inc(tables, 16)
            sp.dma_start(cos[:], c.rope_cos).then_inc(tables, 16)
            sp.dma_start(sin[:], c.rope_sin).then_inc(tables, 16)
            with sp.Fori(0, NB + 2) as i:
                sp.wait_ge(low, i + OPEN)
                sp.dma_start(w[:], w_v[:, :, bass.ds(i * 512 + DIFF_COL, 512)]).then_inc(w_ready, 16)

        def multiply(pe, b, t, slot):
            for k in range(KD):
                for j, (uu, ww) in enumerate(((c.uH, wH), (c.uH, wL), (c.uL, wH))):
                    last = nc.tensor.matmul(acc[:, slot, :], uu[:, k, t * TT:(t + 1) * TT], ww[:, b, k, :],
                                            start=(k == 0 and j == 0), stop=(k == KD - 1 and j == 2))
            last.then_inc(product, 1)

        def split_high(act, b, blk):
            act.wait_ge(w_ready, 16 * blk + 16 + OPEN)
            nc.scalar.copy(wH[:, b], w[:]).then_inc(high, 1)

        def split_low(dve, b, blk):
            dve.wait_ge(high, blk + 1 + OPEN)
            nc.vector.tensor_tensor(wL[:, b], w[:], wH[:, b], ALU.subtract).then_inc(low, 1)

        @block.tensor
        def _(pe):
            def turn(i, u):
                pe.wait_ge(roped, U * i + u + 1 + OPEN)
                pe.wait_ge(staged, U * i + u - 1 + OPEN) if u >= 2 else pe.wait_ge(staged, U * i + OPEN)
                for k in range(4):
                    last = nc.tensor.transpose(tp[:, u % 2, k * TT:(k + 1) * TT],
                                               qn[:, u % 2, k * 128:(k + 1) * 128], c.ident[0:TT, 0:TT])
                last.then_inc(turned, 1)

            with pe.Fori(0, NI) as i:
                for u in range(U):
                    b, t = divmod(u, NT)
                    if t == 0:
                        pe.wait_ge(low, 2 * i + b + 1 + OPEN)
                    pe.wait_ge(normed, U * i + u - 1 + OPEN) if u >= 2 else pe.wait_ge(normed, U * i + OPEN)
                    multiply(pe, b, t, u % 2)
                    if u >= 1:
                        turn(i, u - 1)
                turn(i, U - 1)
            pe.wait_ge(normed, QK + OPEN)
            for u in range(U):
                b, t = divmod(u, NT)
                if t == 0:
                    pe.wait_ge(low, 2 * NI + b + 1 + OPEN)
                if u >= 2:
                    pe.wait_ge(v_copied, u - 1 + OPEN)
                multiply(pe, b, t, u % 2)

        @block.scalar
        def _(act):
            def stage(i, u):
                b, t = divmod(u, NT)
                act.wait_ge(turned, U * i + u + 1 + OPEN)
                if t == 0:
                    act.wait_ge(stored[b], 16 * i + OPEN)
                nc.scalar.copy(stg[:, b, :, t * TT:(t + 1) * TT],
                               tp[:, u % 2, 0:4 * TT].rearrange("p (k t) -> p k t", k=4)).then_inc(staged, 1)
                if t == NT - 1:
                    act.wait_ge(staged, U * i + u + 1 + OPEN)
                    act.dma_start(c.qkT[bass.ds(8 * i + 4 * b, 4)].rearrange("k p t -> p k t"),
                                  stg[:, b]).then_inc(stored[b], 16)

            for b in range(2):
                split_high(act, b, b)
            with act.Fori(0, NI) as i:
                for u in range(U):
                    s = u % 2
                    act.wait_ge(product, U * i + u + 1 + OPEN)
                    nc.scalar.activation(sq[:, s, :], acc[:, s, :], ACT.Square).then_inc(sq_done, 1)
                    if u % NT == NT - 1:
                        split_high(act, u // NT, 2 * i + 2 + u // NT)
                    act.wait_ge(ms_done, U * i + u + 1 + OPEN)
                    nc.scalar.activation(rs[:, s, :], ms[:, s, :], ACT.Sqrt, bias=c.eps[0:TT, :],
                                         scale=1.0 / DD).then_inc(rs_done, 1)
                    if u >= 1:
                        stage(i, u - 1)
                stage(i, U - 1)
            for s in range(2):
                act.wait_ge(stored[s], 16 * NI + OPEN)
            for u in range(U):
                b, t = divmod(u, NT)
                act.wait_ge(product, QK + u + 1 + OPEN)
                if u >= 2:
                    act.wait_ge(v_stored[u % 2], 16 * (u // 2) + OPEN)
                nc.scalar.copy(vst[:, u % 2, :], acc[:, u % 2, :]).then_inc(v_copied, 1)
                act.wait_ge(v_copied, u + 1 + OPEN)
                act.dma_start(c.vD[t, :, b * 512:(b + 1) * 512], vst[:, u % 2, :]).then_inc(v_stored[u % 2], 16)
            for s in range(2):
                act.wait_ge(v_stored[s], 16 * (U // 2) + OPEN)

        @block.vector
        def _(dve):
            dve.wait_ge(tables, 64 + OPEN)
            nc.vector.tensor_scalar(nw[:, 0, :], nw[:, 0, :], DD ** -0.5, None, ALU.mult).then_inc(scaled, 1)
            dve.wait_ge(scaled, 1 + OPEN)
            for b in range(2):
                split_low(dve, b, b)
            for part in range(2):
                with dve.Fori(part * (NI // 2), (part + 1) * (NI // 2)) as i:
                    ch = Chain(dve, vec, 2 * U * i)
                    for u in range(U):
                        s = u % 2
                        dve.wait_ge(sq_done, U * i + u + 1 + OPEN)
                        nc.vector.tensor_reduce(ms[:, s, :], sq[:, s, :].rearrange("p (g d) -> p g d", g=G),
                                                AX.X, ALU.add).then_inc(ms_done, 1)
                        dve.wait_ge(rs_done, U * i + u + 1 + OPEN)
                        ch(nc.vector.reciprocal(ri[:, s, :], rs[:, s, :]))
                        if u >= 2:
                            dve.wait_ge(turned, U * i + u - 1 + OPEN)
                        else:
                            dve.wait_ge(turned, U * i + OPEN)
                        q3 = qn[:, s, :].rearrange("p (g d) -> p g d", g=G)
                        ch(nc.vector.tensor_tensor(q3, acc[:, s, :].rearrange("p (g d) -> p g d", g=G),
                                                   ri[:, s, :].unsqueeze(2).to_broadcast([TT, G, DD]), ALU.mult))
                        nc.vector.tensor_tensor(q3, q3, nw[:, part, :].unsqueeze(1).to_broadcast([TT, G, DD]),
                                                ALU.mult).then_inc(normed, 1)
                        if u % NT == NT - 1:
                            split_low(dve, u // NT, 2 * i + 2 + u // NT)

        @block.gpsimd
        def _(pool):
            pool.wait_ge(tables, 64 + OPEN)
            with pool.Fori(0, NI) as i:
                ch = Chain(pool, rope_step, 3 * U * i)
                for u in range(U):
                    b, t = divmod(u, NT)
                    pool.wait_ge(normed, U * i + u + 1 + OPEN)
                    q3 = qn[:, u % 2, :].rearrange("p (g d) -> p g d", g=G)
                    h = ROPE // 2
                    cs = cos[:, t, :].unsqueeze(1).to_broadcast([TT, G, ROPE])
                    sn = sin[:, t, :].unsqueeze(1).to_broadcast([TT, G, ROPE])
                    ch(nc.gpsimd.tensor_tensor(ra[:], q3[:, :, 0:ROPE], cs, ALU.mult))
                    ch(nc.gpsimd.tensor_tensor(rb[:, :, 0:h], q3[:, :, h:ROPE], sn[:, :, 0:h], ALU.mult))
                    ch(nc.gpsimd.tensor_tensor(rb[:, :, h:ROPE], q3[:, :, 0:h], sn[:, :, h:ROPE], ALU.mult))
                    nc.gpsimd.tensor_tensor(q3[:, :, 0:ROPE], ra[:], rb[:], ALU.add).then_inc(roped, 1)
                    pool.wait_ge(roped, U * i + u + 1 + OPEN)


def attention(nc, c):
    with ExitStack() as st:
        sb, ps, sem, begin = scope(nc, st)
        q = sb("at_q", [128, 2, 2, T])
        k = sb("at_k", [128, 2, T])
        v = sb("at_v", [TT, 2, NT, 128])
        mask = sb("at_mask", [TT, TT])
        lams = sb("at_lams", [TT, 4, DD])
        lj = sb("at_lj", [TT, 2, DD])
        ls = sb("at_ls", [TT, 2])
        le = sb("at_le", [TT, 2])
        nlam = sb("at_nlam", [TT, 1])
        nmx = sb("at_nmx", [TT, 2, 2])
        den = sb("at_den", [TT, 2, 2])
        rden = sb("at_rden", [TT, 2, 2])
        rel = sb("at_rel", [TT, 2])
        e = sb("at_e", [TT, 2, 2, T])
        a = sb("at_a", [TT, 2, T])
        aT = sb("at_aT", [TT, 2, 4 * TT])
        o = sb("at_o", [TT, 2, 128])
        osq = sb("at_osq", [TT, 128])
        S = [ps(f"at_S{n}", [TT, 1536]) for n in range(2)]
        tp = ps("at_tp", [TT, 512])
        pv = ps("at_pv", [TT, 512])
        tables = sem("at_tables")
        lam_sum = sem("at_lam_sum")
        lam_exp = sem("at_lam_exp")
        vec = sem("at_vec")
        mask_made = sem("at_mask_made")
        zeroed = sem("at_zeroed")
        loaded = [sem(f"at_loaded{s}") for s in range(2)]
        head_done = [sem(f"at_head_done{s}") for s in range(2)]
        scored = [sem(f"at_scored{n}") for n in range(2)]
        maxed = [sem(f"at_maxed{n}") for n in range(2)]
        exped = [sem(f"at_exped{n}") for n in range(2)]
        mixed = sem("at_mixed")
        turned = sem("at_turned")
        moved = sem("at_moved")
        pv_done = sem("at_pv_done")
        o_done = sem("at_o_done")
        squared = sem("at_squared")
        stored = [sem(f"at_stored{s}") for s in range(2)]
        block = begin()
        NI = DH // 2
        U = 2 * NT
        GR = [-(-(t + 1) // 4) for t in range(NT)]
        BEFORE = [sum(GR[u2 % NT] for u2 in range(u)) for u in range(U + 1)]
        NG = BEFORE[U]

        @block.sync
        def _(sp):
            for j, src in enumerate((c.lambda_q1, c.lambda_k1, c.lambda_q2, c.lambda_k2)):
                sp.dma_start(lams[:, j, :], src.to_broadcast([TT, DD])).then_inc(tables, 16)
            with sp.Fori(0, NI) as i:
                for s in range(2):
                    sp.wait_ge(head_done[s], i + OPEN)
                    for n in range(2):
                        half = slice(64 * n, 64 * n + 64)
                        sp.dma_start(q[half, s, n, :], c.qkT[bass.ds(2 * i + s, 1), half].rearrange("o p t -> (o p) t")).then_inc(loaded[s], 16)
                    sp.dma_start(k[:, s, :], c.qkT[bass.ds(2 * i + s + DH, 1)].rearrange("o p t -> (o p) t")).then_inc(loaded[s], 16)
                    sp.dma_start(v[:, s], c.vD[:, :, bass.ds((2 * i + s) * 128, 128)].rearrange("n p d -> p n d")).then_inc(loaded[s], 16)

        @block.gpsimd
        def _(pool):
            nc.gpsimd.memset(mask[:], 0.0).then_inc(mask_made, 1)
            pool.wait_ge(mask_made, 1 + OPEN)
            nc.gpsimd.affine_select(out=mask[:], in_=mask[:], compare_op=ALU.is_ge, fill=-3.0e38,
                                    base=0, pattern=[[-1, TT]], channel_multiplier=1).then_inc(mask_made, 1)
            pool.wait_ge(mask_made, 2 + OPEN)
            for n in range(2):
                nc.gpsimd.memset(q[64 - 64 * n:128 - 64 * n, :, n, :], 0.0).then_inc(zeroed, 1)
                pool.wait_ge(zeroed, n + 1 + OPEN)

        @block.tensor
        def _(pe):
            def scores(i, u, n):
                s, t = divmod(u, NT)
                if t == 0 and n == 0:
                    pe.wait_ge(loaded[s], 64 * i + 64 + OPEN)
                pe.wait_ge(exped[n], U * i + u + OPEN)
                keys = (t + 1) * TT
                for lo in range(0, keys, 512):
                    hi = min(lo + 512, keys)
                    last = nc.tensor.matmul(S[n][:, lo:hi], q[:, s, n, t * TT:(t + 1) * TT], k[:, s, lo:hi],
                                            start=True, stop=True)
                last.then_inc(scored[n], 1)

            def turn(i, u, g):
                t = u % NT
                if g == 0:
                    pe.wait_ge(mixed, U * i + u + 1 + OPEN)
                pe.wait_ge(moved, NG * i + BEFORE[u] + g + OPEN)
                for j in range(4 * g, min(4 * g + 4, t + 1)):
                    last = nc.tensor.transpose(tp[:, (j % 4) * TT:(j % 4 + 1) * TT],
                                               a[:, u % 2, j * TT:(j + 1) * TT], c.ident[0:TT, 0:TT])
                last.then_inc(turned, 1)

            def times(i, u, g):
                s, t = divmod(u, NT)
                pe.wait_ge(moved, NG * i + BEFORE[u] + g + 1 + OPEN)
                if g == 0:
                    pe.wait_ge(o_done, U * i + u + OPEN)
                for j in range(4 * g, min(4 * g + 4, t + 1)):
                    last = nc.tensor.matmul(pv[:, 0:128], aT[:, (BEFORE[u] + g) % 2, (j % 4) * TT:(j % 4 + 1) * TT],
                                            v[:, s, j, :], start=(j == 0), stop=(j == t))
                if g == GR[t] - 1:
                    last.then_inc(pv_done, 1)

            def values(i, u):
                s, t = divmod(u, NT)
                for g in range(1, GR[t] + 1):
                    if g < GR[t]:
                        turn(i, u, g)
                    times(i, u, g - 1)
                if t == NT - 1:
                    pe.wait_ge(pv_done, U * i + u + 1 + OPEN)
                    pe.sem_inc(head_done[s], 1)

            pe.wait_ge(zeroed, 2 + OPEN)
            with pe.Fori(0, NI) as i:
                for u in range(U + 2):
                    if u < U:
                        scores(i, u, 0)
                    if u >= 2:
                        turn(i, u - 2, 0)
                    if u < U:
                        scores(i, u, 1)
                    if u >= 2:
                        values(i, u - 2)

        @block.vector
        def _(dve):
            dve.wait_ge(tables, 64 + OPEN)
            for j in range(2):
                nc.vector.tensor_tensor_reduce(out=lj[:, j, :], in0=lams[:, 2 * j, :], in1=lams[:, 2 * j + 1, :],
                                               scale=1.0, scalar=0.0, op0=ALU.mult, op1=ALU.add,
                                               accum_out=ls[:, j:j + 1]).then_inc(lam_sum, 1)
            dve.wait_ge(lam_exp, 1 + OPEN)
            LAMBDA0 = 0.8 - 0.6
            ch = Chain(dve, vec)
            ch(nc.vector.tensor_tensor(nlam[:], le[:, 1:2], le[:, 0:1], ALU.subtract))
            ch(nc.vector.tensor_scalar(nlam[:], nlam[:], -LAMBDA0, None, ALU.add))
            dve.wait_ge(mask_made, 2 + OPEN)

            def maxima(i, u, ch):
                t = u % NT
                for n in range(2):
                    dve.wait_ge(scored[n], U * i + u + 1 + OPEN)
                    ch(nc.vector.tensor_tensor(S[n][:, t * TT:(t + 1) * TT], S[n][:, t * TT:(t + 1) * TT],
                                               mask[:], ALU.add))
                    nc.vector.tensor_reduce(nmx[:, u % 2, n:n + 1], S[n][:, 0:(t + 1) * TT], AX.X, ALU.max,
                                            negate=True).then_inc(maxed[n], 1)

            def mix(i, u, ch):
                t, s = u % NT, u % 2
                for n in range(2):
                    dve.wait_ge(exped[n], U * i + u + 1 + OPEN)
                dve.wait_ge(o_done, U * i + u - 1 + OPEN)
                ch(nc.vector.reciprocal(rden[:, s, :], den[:, s, :]))
                ch(nc.vector.tensor_scalar(rel[:, s:s + 1], rden[:, s, 1:2], den[:, s, 0:1], nlam[:], ALU.mult, ALU.mult))
                nc.vector.scalar_tensor_tensor(out=a[:, s, 0:(t + 1) * TT], in0=e[:, s, 1, 0:(t + 1) * TT],
                                               scalar=rel[:, s:s + 1], in1=e[:, s, 0, 0:(t + 1) * TT],
                                               op0=ALU.mult, op1=ALU.add).then_inc(mixed, 1)

            def outs(i, u):
                s = u % 2
                dve.wait_ge(pv_done, U * i + u + 1 + OPEN)
                dve.wait_ge(stored[s], 16 * (U // 2 * i + u // 2) + OPEN)
                nc.vector.tensor_scalar(o[:, s, :], pv[:, 0:128], rden[:, s, 0:1], None, ALU.mult).then_inc(o_done, 1)

            with dve.Fori(0, NI) as i:
                ch = Chain(dve, vec, 4 * U * i + 2)
                for u in range(U + 2):
                    if u < U:
                        maxima(i, u, ch)
                    if 1 <= u <= U:
                        mix(i, u - 1, ch)
                    if u >= 2:
                        outs(i, u - 2)

        @block.scalar
        def _(act):
            act.wait_ge(lam_sum, 2 + OPEN)
            nc.scalar.activation(le[:], ls[:], ACT.Exp).then_inc(lam_exp, 1)

            def exps(i, u, n):
                t, s = u % NT, u % 2
                act.wait_ge(maxed[n], U * i + u + 1 + OPEN)
                act.wait_ge(mixed, U * i + u - 1 + OPEN)
                nc.scalar.activation(e[:, s, n, 0:(t + 1) * TT], S[n][:, 0:(t + 1) * TT], ACT.Exp,
                                     bias=nmx[:, s, n:n + 1], accum_out=den[:, s, n:n + 1]).then_inc(exped[n], 1)

            def move(i, u, g):
                n = min(4, u % NT + 1 - 4 * g) * TT
                act.wait_ge(turned, NG * i + BEFORE[u] + g + 1 + OPEN)
                nc.scalar.copy(aT[:, (BEFORE[u] + g) % 2, 0:n], tp[:, 0:n]).then_inc(moved, 1)

            def square(i, u):
                t = u % NT
                act.wait_ge(o_done, U * i + u + 1 + OPEN)
                act.dma_start(c.oD[t, :, bass.ds((2 * i + u // NT) * 128, 128)], o[:, u % 2, :]).then_inc(stored[u % 2], 16)
                nc.scalar.activation(osq[:], o[:, u % 2, :], ACT.Square,
                                     accum_out=c.o_ms[:, t, bass.ds(2 * i + u // NT, 1)]).then_inc(squared, 1)

            with act.Fori(0, NI) as i:
                for u in range(U + 2):
                    if u < U:
                        exps(i, u, 0)
                    if u >= 2:
                        move(i, u - 2, 0)
                    if u < U:
                        exps(i, u, 1)
                    if u >= 2:
                        for g in range(1, GR[(u - 2) % NT]):
                            move(i, u - 2, g)
                        square(i, u - 2)
            act.wait_ge(squared, NI * U + OPEN)
            for s in range(2):
                act.wait_ge(stored[s], 16 * NI * U // 2 + OPEN)


SUB = 13
DECAY = math.exp(-0.5)
GN_EPS = 64e-5


def rwkv(nc, c):
    with ExitStack() as st:
        sb, ps, sem, begin = scope(nc, st)
        x3 = sb("rw_x3", [128, 3, T + 1])
        d3 = sb("rw_d3", [128, 3, T])
        m2 = sb("rw_m2", [128, 2, T])
        v = sb("rw_v", [128, 2, T])
        lo = sb("rw_lo", [128, 2, T])
        NF = RH // 2
        NP = 10
        MU_R, MU_K, MU_V, W0, A0, K_K, K_A, R_K, LN_W, LN_B = range(NP)
        NR = NP * NF + 2
        rows_ = sb("rw_rows", [NR, 128])
        par = sb("rw_par", [128, NP, NF + 1])
        lmu = sb("rw_lmu", [128, 2])
        pf = sb("rw_pf", [128, 2, NP])
        wa = sb("rw_wa", [128, 128])
        g2 = sb("rw_g2", [128, 128])
        ones_row = sb("rw_ones_row", [128, TT])
        ones = sb("rw_ones", [128, 128])
        mask4 = sb("rw_mask4", [TT, 4, TT])
        maskn = sb("rw_maskn", [TT, 2, TT])
        geps = sb("rw_geps", [128, 1])
        sw = sb("rw_sw", [128, T])
        a = sb("rw_a", [128, T])
        g = sb("rw_g", [128, T])
        run = sb("rw_run", [128, T])
        P = sb("rw_P", [128, T])
        Pi = sb("rw_Pi", [128, T])
        Pp = sb("rw_Pp", [128, T])
        kk = sb("rw_kk", [128, T])
        b_ = sb("rw_b", [128, T])
        kn = Pi
        yw = Pp
        Pend = sb("rw_Pend", [128, 2, NT])
        kr = sb("rw_kr", [128, 2, 2, T])
        bkz = sb("rw_bkz", [128, 2, 2, 2, T])
        bon = sb("rw_bon", [128, T])
        M4 = sb("rw_M4", [TT, 4, 2, 4, TT])
        MT = sb("rw_MT", [TT, 4, 2, TT])
        tok = sb("rw_tok", [TT, 4, 3, 128])
        Nn = sb("rw_Nn", [TT, 2, 2, 2, TT])
        X2 = sb("rw_X2", [TT, 2, 2, 2, TT])
        X4 = sb("rw_X4", [TT, 2, 2, 2, TT])
        N8 = sb("rw_N8", [TT, 2, 2, TT])
        Q = sb("rw_Q", [TT, 2, 2, 2, TT])
        Y1 = sb("rw_Y1", [TT, 2, 2, 2, TT])
        Y2 = sb("rw_Y2", [TT, 2, 2, 2, TT])
        Y4 = sb("rw_Y4", [TT, 2, 2, TT])
        G = sb("rw_G", [TT, 2, 2, 2, TT])
        R = sb("rw_R", [TT, 128])
        Uu = sb("rw_U", [TT, 128])
        S = sb("rw_S", [128, 2, 128])
        St = sb("rw_St", [128, 128])
        Y = sb("rw_Y", [TT, 2, NT * 2, RD])
        Yq = d3[0:TT, 1:3, 0:NT * RD].rearrange("p a (n d) -> p a n d", d=RD)
        gs = sb("rw_gs", [TT, 4, NT * 2])
        bank = ps("rw_bank", [128, 8, 512])
        consts, made, par_turned, pre, lora = (sem("rw_" + n) for n in ("consts", "made", "par_turned", "pre", "lora"))
        x_in, wa_in, g2_in, lora_in = sem("rw_x_in"), sem("rw_wa_in"), sem("rw_g2_in"), sem("rw_lora_in")
        prep_dve, prep_act, prep_pool = sem("rw_prep_dve"), sem("rw_prep_act"), sem("rw_prep_pool")
        KINDS = ("w", "a", "ss", "g", "bs", "gn")
        wide_done = [sem(f"rw_wide_{k}") for k in KINDS]
        wide_read = [sem(f"rw_wide_read_{k}") for k in KINDS]
        sdve, sact, spe = ([sem(f"rw_solve_{e}{j}") for j in range(2)] for e in ("dve", "act", "pe"))
        made_pool = sem("rw_made_pool")
        seq_dve, seq_act, seq_pe, seq_add = sem("rw_seq_dve"), sem("rw_seq_act"), sem("rw_seq_pe"), sem("rw_seq_add")
        gn_dve, gn_act, y_out = sem("rw_gn_dve"), sem("rw_gn_act"), sem("rw_y_out")
        block = begin()

        PIECES = ((0, 352), (352, 704), (704, T))
        ZEROS = (kr[:, 1], M4[:, 2:4], MT[:, 2:4], tok[:, 2:4], S[:], Pend[:, 1], Y[:, 1], pf[:, 1], g[:], bon[:])
        ZEROED = 4 + len(ZEROS)
        RC = 4
        PREP_SHARE = 0.95
        AC = ["kk2", "P", "Pp", "Pi"]
        PO = ["b", "bh0", "bh1", "kh0", "kh1"]
        PE_STEPS = (1, 2, 3, 6, 7, 8, 9, 10, 11, 12, 13, 14)
        SD, SA, PEN = 10, 8, len(PE_STEPS)

        def dv(p, name):
            return len(DV) * p + DV.index(name) + 1 + OPEN

        def ac(p, name):
            return len(AC) * p + AC.index(name) + 1 + OPEN

        def po(p, name):
            return len(PO) * p + PO.index(name) + 1 + OPEN

        wide = lambda kind: [("wide", (kind, j)) for j in range(3)]
        PREP = ([("dve", n) for n in ("pf", "d0", "d1", "d2", "mk", "mr", "mv", "kk")] + [("act", "kk2")] + wide("w") + wide("a")
                + [("dve", f"run{t}") for t in range(NT)] + wide("ss") + [("dve", "lpr"), ("dve", "kmax"), ("act", "P"), ("act", "Pp")]
                + [("dve", f"rec{t}") for t in range(RC)] + [("dve", "kkn"), ("act", "Pi"), ("pool", "b"), ("dve", "kap"), ("pool", "bh0"),
                   ("pool", "bh1"), ("dve", "ta"), ("dve", "kp"), ("pool", "kh0"), ("pool", "kh1"), ("dve", "rk"), ("dve", "rh"), ("dve", "pend")])
        DV = [n for e, n in PREP if e == "dve"]
        GN = [("gn", k) for k in ("mean", "sum", "norm")] + wide("gn") + [("gn", "gate")]
        REST = wide("bs") + wide("g")

        def weave(main, side, share=1.0):
            out, k = [], 0
            for n, x in enumerate(main):
                out.append(x)
                while k < len(side) and k * share * len(main) < (n + 1) * len(side):
                    out.append(side[k])
                    k += 1
            return out + side[k:]

        def round_(d, r):
            before = [(d, 2 * r - 2 + j) if r > 0 else (d - 1, NT - 2 + j) for j in range(2)]
            pieces = [("seq", d_, (t, q)) for d_, t in before for q in (1, 2, 3, 4)]
            out = [("solve", d, (2 * r + j, n)) for j in range(2) for n in (1, 2, 3)]
            for k, n in enumerate((6, 7, 8, 9, 10, 11, 12, 13)):
                out += [("solve", d, (2 * r + j, n)) for j in range(2)]
                out.append(pieces[k])
            return out + [("solve", d, (2 * r + j, 14)) for j in range(2)]

        tag = lambda steps, d: [(e, d, n) for e, n in steps]

        ORDER = []
        for d in range(2):
            ORDER += round_(d, 0)
            ORDER += weave(round_(d, 1), tag(GN, d - 1) + tag(REST[:2], d))
            ORDER += weave(sum((round_(d, r) for r in range(2, NT // 2)), []), tag(REST[2:], d) + tag(PREP, d + 1), PREP_SHARE)
        PROLOGUE = tag(PREP, 0)
        EPILOGUE = [("seq", 1, (t, q)) for t in (NT - 2, NT - 1) for q in (1, 2, 3, 4)] + tag(GN, 1)

        def walk(i, order, parts):
            for e, d, n in order:
                if e in ("seq", "solve") and e in parts:
                    parts[e](2 * i + d, d % 2, *n)
                elif e in parts:
                    parts[e](2 * i + d, d % 2, n)

        @block.sync
        def _(sp):
            row = lambda ap: ap.rearrange("o (f p) -> (o f) p", p=128)
            mu = c.rwkv_mu
            for j, src in enumerate((mu[:, 0:D], mu[:, D:2 * D], mu[:, 2 * D:3 * D], c.rwkv_w0, c.rwkv_a0,
                                     c.rwkv_k_k, c.rwkv_k_a, c.rwkv_r_k.rearrange("o h d -> o (h d)"),
                                     c.rwkv_ln_w, c.rwkv_ln_b)):
                sp.dma_start(rows_[NF * j:NF * j + NF, :], row(src)).then_inc(consts, 16)
            sp.dma_start(rows_[NF * NP:NF * NP + 2, :], row(mu[:, 3 * D:RWKV_COLS])).then_inc(consts, 16)
            sp.dma_start(mask4[:], c.mask4).then_inc(consts, 16)
            sp.dma_start(maskn[:], c.maskn).then_inc(consts, 16)
            for j in range(2):
                sp.dma_start(x3[:, j, 1:T + 1], c.pT[24 + j]).then_inc(lora_in, 16)
            sp.wait_ge(pre, 3 + OPEN)

            def load(p, f):
                sp.wait_ge(prep_dve, len(DV) * p + OPEN)
                for j in range(3):
                    sp.dma_start(x3[:, j, 1:T + 1], c.pT[bass.ds(f + 8 * j, 1)].rearrange("o p t -> (o p) t")).then_inc(x_in, 16)
                fs = bass.ds(f * 128, 128)
                sp.wait_ge(wide_read[1], 3 * p + OPEN)
                sp.dma_start(wa[0:64, :], c.rwkv_w2[0, :, fs]).then_inc(wa_in, 16)
                sp.dma_start(wa[64:128, :], c.rwkv_a2[0, :, fs]).then_inc(wa_in, 16)

            def load_g(p, f):
                sp.wait_ge(wide_read[3], 3 * p + OPEN)
                sp.dma_start(g2[:], c.rwkv_g2[0, :, bass.ds(f * 128, 128)]).then_inc(g2_in, 16)

            def store(n):
                sp.wait_ge(gn_dve, 8 * (n + 1) + 8 + OPEN)
                sp.dma_start(c.yrT[bass.ds(n, 1)].rearrange("o p t -> (o p) t"), yw[:]).then_inc(y_out, 16)

            sp.sem_inc(y_out, 16)
            for p in range(2):
                load(p, p)
                load_g(p, p)
            with sp.Fori(0, NF // 2 - 1) as i:
                for p in range(1, 3):
                    load(2 * i + p + 1, 2 * i + p + 1)
                    store(2 * i + p - 1)
                    load_g(2 * i + p + 1, 2 * i + p + 1)
            load(NF, 0)
            store(NF - 2)
            load_g(NF, 0)
            store(NF - 1)
            sp.wait_ge(g2_in, 16 * (NF + 1) + OPEN)
            sp.wait_ge(y_out, 16 * NF + 16 + OPEN)

        mm, tr = nc.tensor.matmul, nc.tensor.transpose
        half = lambda h: slice(64 * h, 64 * h + 64)
        chunk = lambda t: slice(t * TT, (t + 1) * TT)

        @block.tensor
        def _(pe):
            last_wide = [None]

            def solve(p, z, t, n):
                ln, m = t % 2, (NT * z + t) % 4
                bx, bq = 2 + 2 * ln, 3 + 2 * ln
                at = lambda b, k, h: bank[0:TT, b, (2 * k + h) * TT:(2 * k + h + 1) * TT]
                dve_ge = lambda k: pe.wait_ge(sdve[ln], SD * (5 * p + t // 2) + k + OPEN)
                act_ge = lambda k: pe.wait_ge(sact[ln], SA * (5 * p + t // 2) + k + OPEN)
                if n == 1:
                    if ln == 1:
                        pe.wait_ge(sdve[0], SD * (5 * p + t // 2) + 1 + OPEN)
                    else:
                        pe.wait_ge(sdve[1], SD * (5 * p + t // 2 - 1) + 1 + OPEN) if t > 0 else pe.wait_ge(sdve[1], SD * 5 * p + OPEN)
                    if t == 0:
                        pe.wait_ge(prep_dve, dv(p, "pend"))
                        pe.wait_ge(prep_pool, po(p, "kh1"))
                    for h in range(2):
                        for j in range(2):
                            last = mm(bank[0:TT, h, 2 * j * TT:(2 * j + 2) * TT].rearrange("p (a t) -> p a t", a=2),
                                      bkz[:, z, h, j, chunk(t)], kr[:, z, :, chunk(t)], start=True, stop=True)
                elif n == 2:
                    act_ge(0)
                    dve_ge(0)
                    for h in range(2):
                        last = mm(at(bx, 0, h), kr[:, z, 0, chunk(t)], bkz[:, z, h, 0, chunk(t)], start=True, stop=True)
                elif n == 3:
                    for j in range(2):
                        for h in range(2):
                            mm(bank[0:TT, bq, j * 128 + 64 * h:j * 128 + 64 * h + 64], bkz[:, z, h, j, chunk(t)],
                               c.ident[:, half(h)], start=True, stop=True)
                    last = tr(bank[0:TT, bq, 256:384], v[:, z, chunk(t)], c.ident[:])
                elif n == 6:
                    dve_ge(2)
                    for h in range(2):
                        mm(at(bx, 0, h), Nn[:, ln, 0, h, :], M4[:, m, h, 0, :], start=True, stop=True)
                        last = mm(at(bx, 1, h), M4[:, m, h, 0, :], Nn[:, ln, 0, h, :], start=True, stop=True)
                elif n == 7:
                    act_ge(2)
                    dve_ge(3)
                    for h in range(2):
                        mm(at(bx, 0, h), X2[:, ln, 1, h, :], X2[:, ln, 0, h, :], start=True, stop=True)
                        mm(at(bx, 1, h), X2[:, ln, 0, h, :], X2[:, ln, 1, h, :], start=True, stop=True)
                        last = mm(at(bq, 0, h), X2[:, ln, 1, h, :], Q[:, ln, 0, h, :], start=True, stop=True)
                elif n == 8:
                    act_ge(3)
                    dve_ge(4)
                    for h in range(2):
                        mm(at(bx, 0, h), X4[:, ln, 0, h, :], X4[:, ln, 1, h, :], start=True, stop=True)
                        last = mm(at(bq, 0, h), X4[:, ln, 1, h, :], Q[:, ln, 1, h, :], start=True, stop=True)
                elif n == 9:
                    act_ge(4)
                    dve_ge(5)
                    for h in range(2):
                        last = mm(at(bq, 0, h), N8[:, ln, h, :], Q[:, ln, 0, h, :], start=True, stop=True)
                elif n == 10:
                    dve_ge(6)
                    for h in range(2):
                        mm(at(bx, 0, h), Nn[:, ln, 1, h, :], Q[:, ln, 1, h, :], start=True, stop=True)
                        mm(at(bx, 1, h), Q[:, ln, 1, h, :], Nn[:, ln, 1, h, :], start=True, stop=True)
                        last = tr(at(bq, 0, h), Q[:, ln, 1, h, :], c.ident[0:TT, 0:TT])
                elif n == 11:
                    act_ge(5)
                    for h in range(2):
                        mm(at(bx, 0, h), Y1[:, ln, 1, h, :], Y1[:, ln, 0, h, :], start=True, stop=True)
                        last = mm(at(bx, 1, h), Y1[:, ln, 0, h, :], Y1[:, ln, 1, h, :], start=True, stop=True)
                elif n == 12:
                    act_ge(6)
                    dve_ge(8)
                    for h in range(2):
                        mm(at(bx, 0, h), Y2[:, ln, 0, h, :], Y2[:, ln, 1, h, :], start=True, stop=True)
                        last = mm(at(bq, 0, h), Y2[:, ln, 1, h, :], G[:, ln, 1, h, :], start=True, stop=True)
                elif n == 13:
                    act_ge(7)
                    dve_ge(9)
                    for h in range(2):
                        last = mm(at(bq, 0, h), Y4[:, ln, h, :], G[:, ln, 1, h, :], start=True, stop=True)
                elif n == 14:
                    dve_ge(10)
                    for h in range(2):
                        last = mm(at(bq, 0, h), G[:, ln, 0, h, :], G[:, ln, 1, h, :], start=True, stop=True)
                last.then_inc(spe[ln], 1)

            def seq(p, z, t, q):
                C = NT * p + t + 2
                m, ln = (NT * z + t) % 4, t % 2
                vv = lambda h: tok[:, m, 2, half(h)]
                o = lambda k, h=None: bank[0:TT, 6, 128 * k:128 * (k + 1)] if h is None else bank[0:TT, 6, 128 * k + 64 * h:128 * k + 64 * h + 64]
                if q == 1:
                    if t > 0:
                        pe.wait_ge(seq_dve, (NT - 1) * p + t + 1 + OPEN)
                    pe.wait_ge(sact[ln], SA * (5 * p + t // 2) + 8 + OPEN)
                    pe.wait_ge(seq_act, 3 * C + OPEN)
                    for h in range(2):
                        last = mm(o(0, h), M4[:, m, h, 2, :], vv(h), start=(t == 0 or h == 0), stop=(t == 0), skip_group_check=t > 0)
                    if t > 0:
                        last = mm(o(0), kr[:, z, 0, chunk(t)], S[:, t % 2, :], start=False, stop=True, skip_group_check=True)
                elif q == 2:
                    pe.wait_ge(seq_act, 3 * C + 1 + OPEN)
                    for h in range(2):
                        last = mm(o(1, h), MT[:, m, h, :], R[:, half(h)], start=True, stop=True)
                elif q == 3:
                    pe.wait_ge(seq_act, 3 * C + 2 + OPEN)
                    if t == NT - 1:
                        return
                    mm(bank[:, 6, 384:512], tok[:, m, 0, :], Uu[:], start=True, stop=False)
                    last = mm(bank[:, 6, 384:512], tok[:, m, 1, :], tok[:, m, 2, :], start=False, stop=True)
                else:
                    if 0 < t < NT - 1:
                        pe.wait_ge(seq_add, (NT - 1) * p + t + 2 + OPEN)
                    elif t == 0:
                        pe.wait_ge(seq_add, (NT - 1) * p + 2 + OPEN)
                    for h in range(2):
                        mm(o(2, h), M4[:, m, h, 1, :], Uu[:, half(h)], start=(t == 0 or h == 0), stop=False, skip_group_check=t > 0)
                        last = mm(o(2, h), M4[:, m, h, 3, :], vv(h), start=False, stop=(t == 0), skip_group_check=t > 0)
                    if t > 0:
                        last = mm(o(2), kr[:, z, 1, chunk(t)], S[:, t % 2, :], start=False, stop=True, skip_group_check=True)
                last.then_inc(seq_pe, 1)

            def wide_piece(p, z, what):
                kind, j = what
                k = KINDS.index(kind)
                if last_wide[0] is not None:
                    kb, nb = last_wide[0]
                    pe.wait_ge(wide_read[kb], nb + OPEN)
                last_wide[0] = (k, 3 * (p + (kind == "gn")) + j + 1)
                lo_, hi = PIECES[j]
                out = bank[:, 7, 0:hi - lo_]
                if kind == "w":
                    pe.wait_ge(wa_in, 32 * p + 32 + OPEN)
                    last = mm(out, wa[0:64, :], lo[0:64, 0, lo_:hi], start=True, stop=True)
                elif kind == "a":
                    last = mm(out, wa[64:128, :], lo[64:128, 0, lo_:hi], start=True, stop=True)
                elif kind == "g":
                    pe.wait_ge(g2_in, 16 * p + 16 + OPEN)
                    last = mm(out, g2[:], lo[:, 1, lo_:hi], start=True, stop=True)
                elif kind == "ss":
                    pe.wait_ge(prep_act, ac(p, "kk2"))
                    last = mm(out, ones[:], kn[:, lo_:hi], start=True, stop=True)
                elif kind == "bs":
                    pe.wait_ge(prep_dve, dv(p, "rk"))
                    last = mm(out, ones[:], d3[:, 0, lo_:hi], start=True, stop=True)
                else:
                    pe.wait_ge(gn_dve, 8 * (p + 1) + 6 + OPEN)
                    for t in range(4 * j, min(4 * j + 4, NT)):
                        last = tr(bank[:, 7, (t % 4) * TT:(t % 4 + 1) * TT],
                                  Yq[:, t // 5, 2 * (t % 5):2 * (t % 5) + 2, :].rearrange("p h d -> p (h d)"), c.ident[0:TT, 0:TT])
                last.then_inc(wide_done[k], 1)

            pe.wait_ge(consts, 13 * 16 + OPEN)
            tr(bank[:, 5, 0:NR], rows_[:], c.ident[0:NR, 0:NR]).then_inc(par_turned, 1)
            pe.wait_ge(lora, 2 + OPEN)
            pe.wait_ge(made_pool, ZEROED + OPEN)
            walk(0, PROLOGUE, {"wide": wide_piece})
            parts = {"solve": solve, "seq": seq, "wide": wide_piece}
            with pe.Fori(0, NF // 2) as i:
                last_wide[0] = (KINDS.index("ss"), 6 * i + 3)
                walk(i, ORDER, parts)
            last_wide[0] = (KINDS.index("ss"), 3 * NF + 3)
            walk(NF // 2 - 1, EPILOGUE, parts)

        @block.scalar
        def _(act):
            act.wait_ge(pre, 3 + OPEN)
            nc.scalar.activation(lo[0:64, 0, :], lo[0:64, 0, :], ACT.Tanh).then_inc(lora, 1)
            nc.scalar.activation(lo[:, 1, :], lo[:, 1, :], ACT.Sigmoid).then_inc(lora, 1)

            def solve(p, z, t, n):
                ln, m = t % 2, (NT * z + t) % 4
                bx, bq = 2 + 2 * ln, 3 + 2 * ln
                four = bank[0:TT, bx, 0:4 * TT].rearrange("p (k h t) -> p k h t", k=2, h=2)
                two = lambda b: bank[0:TT, b, 0:2 * TT].rearrange("p (h t) -> p h t", h=2)
                what = {3: (tok[:, m].rearrange("p j d -> p (j d)"), bank[0:TT, bq, 0:384]),
                        6: (X2[:, ln], four), 7: (X4[:, ln], four), 8: (N8[:, ln], two(bx)),
                        10: (Y1[:, ln], four), 11: (Y2[:, ln], four), 12: (Y4[:, ln], two(bx)),
                        14: (MT[:, m], two(bq))}
                if n in what:
                    act.wait_ge(spe[ln], PEN * (5 * p + t // 2) + PE_STEPS.index(n) + 1 + OPEN)
                    nc.scalar.copy(*what[n]).then_inc(sact[ln], 1)

            def seq(p, z, t, q):
                k = (4 * NT - 1) * p + 4 * t + 7
                if q == 1:
                    act.wait_ge(seq_pe, k + 1 + OPEN)
                    nc.scalar.mul(R[:], bank[0:TT, 6, 0:128], -1.0).then_inc(seq_act, 1)
                elif q == 2:
                    act.wait_ge(seq_pe, k + 2 + OPEN)
                    nc.scalar.copy(Uu[:], bank[0:TT, 6, 128:256]).then_inc(seq_act, 1)
                elif q == 4:
                    act.wait_ge(seq_pe, k + (4 if t < NT - 1 else 3) + OPEN)
                    nc.scalar.copy(Y[:, z, 2 * t:2 * t + 2, :].rearrange("p h d -> p (h d)"),
                                   bank[0:TT, 6, 256:384]).then_inc(seq_act, 1)

            def wide_piece(p, z, what):
                kind, j = what
                k = KINDS.index(kind)
                if kind == "bs":
                    return
                lo_, hi = PIECES[j]
                src = bank[:, 7, 0:hi - lo_]
                act.wait_ge(wide_done[k], 3 * (p + (kind == "gn")) + j + 1 + OPEN)
                if kind in "wa":
                    if j == 0:
                        act.wait_ge(prep_dve, dv(p, "pf"))
                    dst, b = (sw, W0) if kind == "w" else (a, A0)
                    ins = nc.scalar.activation(dst[:, lo_:hi], src, ACT.Sigmoid, bias=pf[:, z, b:b + 1])
                elif kind == "g":
                    ins = nc.scalar.copy(g[:, lo_:hi], src)
                elif kind == "ss":
                    ins = nc.scalar.activation(kn[:, lo_:hi], src, ACT.Sqrt)
                else:
                    if j == 0:
                        act.wait_ge(y_out, 16 * (p + 1) + OPEN)
                        act.wait_ge(prep_dve, dv(p + 1, "kap"))
                    n = min(4, NT - 4 * j) * TT
                    ins = nc.scalar.activation(yw[:, 4 * j * TT:4 * j * TT + n], bank[:, 7, 0:n], ACT.Identity,
                                               scale=pf[:, z, LN_W:LN_W + 1], bias=pf[:, z, LN_B:LN_B + 1])
                ins.then_inc(wide_read[k], 1)

            def prep(p, z, name):
                if name == "kk2":
                    act.wait_ge(prep_dve, dv(p, "mk"))
                    act.wait_ge(prep_pool, po(p, "kh1") - len(PO))
                    nc.scalar.activation(kn[:], m2[:, 1, :], ACT.Square, scale=pf[:, z, K_K:K_K + 1]).then_inc(prep_act, 1)
                elif name == "P":
                    act.wait_ge(prep_dve, dv(p, "lpr"))
                    nc.scalar.activation(P[:], run[:], ACT.Exp, scale=-DECAY).then_inc(prep_act, 1)
                elif name == "Pp":
                    act.wait_ge(y_out, 16 * p + OPEN)
                    nc.scalar.activation(Pp[:], sw[:], ACT.Exp, scale=-DECAY).then_inc(prep_act, 1)
                elif name == "Pi":
                    act.wait_ge(prep_dve, dv(p, "kkn"))
                    nc.scalar.activation(Pi[:], run[:], ACT.Exp, scale=DECAY).then_inc(prep_act, 1)

            def gn(p, z, k):
                if k == "sum":
                    act.wait_ge(gn_dve, 8 * (p + 1) + 3 + OPEN)
                    act.wait_ge(prep_dve, dv(p + 1, "pend"))
                    act.wait_ge(prep_pool, po(p + 1, "kh1"))
                    nc.scalar.activation(Yq, Y[:, z].rearrange("p (a n) d -> p a n d", a=2), ACT.Square).then_inc(gn_act, 1)
                elif k == "norm":
                    act.wait_ge(gn_dve, 8 * (p + 1) + 4 + OPEN)
                    nc.scalar.activation(gs[:, 2, :], gs[:, 1, :], ACT.Sqrt, bias=geps[0:TT, :], scale=1.0 / RD).then_inc(gn_act, 1)

            parts = {"solve": solve, "seq": seq, "wide": wide_piece, "act": prep, "gn": gn}
            walk(0, PROLOGUE, parts)
            act.wait_ge(made_pool, ZEROED + OPEN)
            with act.Fori(0, NF // 2) as i:
                walk(i, ORDER, parts)
            walk(NF // 2 - 1, EPILOGUE, parts)

        @block.gpsimd
        def _(pool):
            tt = nc.gpsimd.tensor_tensor
            for z in range(2):
                for h in range(2):
                    nc.gpsimd.memset(bkz[half(1 - h), z, h], 0.0).then_inc(made_pool, 1)
                    pool.wait_ge(made_pool, 2 * z + h + 1 + OPEN)
            for n, zeros in enumerate(ZEROS):
                nc.gpsimd.memset(zeros, 0.0).then_inc(made_pool, 1)
                pool.wait_ge(made_pool, n + 5 + OPEN)

            def prep(p, z, name):
                if name == "b":
                    pool.wait_ge(prep_dve, dv(p, "kkn"))
                    pool.wait_ge(wide_read[KINDS.index("a")], 3 * p + 3 + OPEN)
                    tt(b_[:], kk[:], a[:], ALU.mult).then_inc(prep_pool, 1)
                else:
                    h = int(name[2])
                    if name == "bh0":
                        pool.wait_ge(prep_act, ac(p, "Pi"))
                        pool.wait_ge(prep_pool, po(p, "b"))
                    if name == "kh0":
                        pool.wait_ge(prep_dve, dv(p, "kp"))
                    src = b_ if name[0] == "b" else d3[:, 1, :]
                    tt(bkz[half(h), z, h, "bk".index(name[0]), :], src[half(h)], Pi[half(h)], ALU.mult).then_inc(prep_pool, 1)

            walk(0, PROLOGUE, {"pool": prep})
            with pool.Fori(0, NF // 2) as i:
                walk(i, ORDER, {"pool": prep})

        @block.vector
        def _(dve):
            tt, ts, stt = nc.vector.tensor_tensor, nc.vector.tensor_scalar, nc.vector.scalar_tensor_tensor
            nc.vector.memset(geps[:], GN_EPS)
            nc.vector.memset(par[:], 0.0)
            nc.vector.memset(ones[:], 0.0).then_inc(made, 1)
            nc.vector.memset(ones_row[:], 1.0).then_inc(made, 1)
            dve.wait_ge(made, 2 + OPEN)
            for h in range(2):
                nc.vector.memset(ones[half(h), half(h)], 1.0).then_inc(made, 1)
            nc.vector.memset(x3[:, :, 0:1], 0.0).then_inc(pre, 1)
            dve.wait_ge(consts, 13 * 16 + OPEN)
            dve.wait_ge(lora_in, 32 + OPEN)
            dve.wait_ge(pre, 1 + OPEN)
            dve.wait_ge(par_turned, 1 + OPEN)
            nc.vector.tensor_copy(par[:, :, 0:NF], bank[:, 5, 0:NP * NF].rearrange("p (n f) -> p n f", n=NP)).then_inc(made, 1)
            nc.vector.tensor_copy(lmu[:], bank[:, 5, NP * NF:NR]).then_inc(made, 1)
            tt(d3[:, 0:2, :], x3[:, 0:2, 0:T], x3[:, 0:2, 1:T + 1], ALU.subtract).then_inc(made, 1)
            dve.wait_ge(made, 7 + OPEN)
            for j in range(2):
                stt(out=lo[:, j, :], in0=d3[:, j, :], scalar=lmu[:, j:j + 1], in1=x3[:, j, 1:T + 1],
                    op0=ALU.mult, op1=ALU.add).then_inc(pre, 1)
            dve.wait_ge(pre, 3 + OPEN)

            def solve(p, z, t, n):
                ln, m = t % 2, (NT * z + t) % 4
                bx, bq = 2 + 2 * ln, 3 + 2 * ln
                base = 5 * p + t // 2
                two = bank[0:TT, bq, 0:2 * TT].rearrange("p (h t) -> p h t", h=2)
                wait_pe = lambda: dve.wait_ge(spe[ln], PEN * base + PE_STEPS.index(n) + 1 + OPEN)
                own = lambda k: dve.wait_ge(sdve[ln], SD * base + k + OPEN)
                if n == 1:
                    wait_pe()
                    tt(M4[:, m], bank[0:TT, 0:2, 0:4 * TT].rearrange("p h (k t) -> p h k t", k=4),
                       mask4[:].unsqueeze(1).to_broadcast([TT, 2, 4, TT]), ALU.mult).then_inc(sdve[ln], 1)
                elif n == 2:
                    wait_pe()
                    src = bank[0:TT, bx, 0:2 * TT].rearrange("p (h t) -> p h t", h=2)
                    for j in range(2):
                        last = tt(Nn[:, ln, j], src, maskn[:, j, :].unsqueeze(1).to_broadcast([TT, 2, TT]), ALU.mult)
                    last.then_inc(sdve[ln], 1)
                elif n == 6:
                    own(1)
                    tt(Q[:, ln, 0], M4[:, m, :, 0, :], c.ident[0:TT, 0:TT].unsqueeze(1).to_broadcast([TT, 2, TT]),
                       ALU.add).then_inc(sdve[ln], 1)
                elif n in (7, 8, 9):
                    wait_pe()
                    own(n - 4)
                    tt(Q[:, ln, n % 2], two, Q[:, ln, 1 - n % 2], ALU.add).then_inc(sdve[ln], 1)
                elif n == 10:
                    wait_pe()
                    nc.vector.tensor_copy(G[:, ln, 0], two).then_inc(sdve[ln], 1)
                elif n == 11:
                    dve.wait_ge(sact[ln], SA * base + 5 + OPEN)
                    tt(G[:, ln, 1], Y1[:, ln, 0], c.ident[0:TT, 0:TT].unsqueeze(1).to_broadcast([TT, 2, TT]),
                       ALU.add).then_inc(sdve[ln], 1)
                elif n in (12, 13):
                    wait_pe()
                    own(n - 4)
                    tt(G[:, ln, 1], two, G[:, ln, 1], ALU.add).then_inc(sdve[ln], 1)

            def seq(p, z, t, q):
                if q == 3 and t < NT - 1:
                    k = (4 * NT - 1) * p + 4 * t + 7
                    dve.wait_ge(seq_pe, k + 3 + OPEN)
                    end = Pend[:, z, t:t + 1]
                    if t == 0:
                        nc.vector.tensor_copy(St[:], bank[:, 6, 384:512]).then_inc(seq_add, 1)
                    else:
                        dve.wait_ge(seq_dve, (NT - 1) * p + t + 1 + OPEN)
                        tt(St[:], bank[:, 6, 384:512], S[:, t % 2, :], ALU.add).then_inc(seq_add, 1)
                    dve.wait_ge(seq_add, (NT - 1) * p + t + 2 + OPEN)
                    stt(out=S[:, (t + 1) % 2, :], in0=St[:], scalar=end, in1=ones[:], op0=ALU.mult,
                        op1=ALU.mult).then_inc(seq_dve, 1)

            def wide_piece(p, z, what):
                kind, j = what
                if kind == "bs":
                    k = KINDS.index(kind)
                    lo_, hi = PIECES[j]
                    dve.wait_ge(wide_done[k], 3 * p + j + 1 + OPEN)
                    tt(bon[:, lo_:hi], bank[:, 7, 0:hi - lo_], v[:, z, lo_:hi], ALU.mult).then_inc(wide_read[k], 1)

            def prep(p, z, name):
                q = lambda n: pf[:, z, n:n + 1]
                w = lambda *names: [dve.wait_ge(prep_dve, dv(p, x)) for x in names]
                if name == "pf":
                    ins = nc.vector.tensor_copy(pf[:, z], par[:, :, bass.ds(p, 1)].rearrange("p n o -> p (n o)"))
                elif name[0] == "d":
                    j = int(name[1])
                    if j == 0:
                        dve.wait_ge(x_in, 48 * p + 48 + OPEN)
                    elif j == 1:
                        dve.wait_ge(prep_pool, len(PO) * p + OPEN)
                    ins = tt(d3[:, j, :], x3[:, j, 0:T], x3[:, j, 1:T + 1], ALU.subtract)
                elif name in ("mr", "mk", "mv"):
                    j = "rkv".index(name[1])
                    w("pf", f"d{j}")
                    dst = v[:, z] if j == 2 else m2[:, j, :]
                    ins = stt(out=dst, in0=d3[:, j, :], scalar=q(MU_R + j), in1=x3[:, j, 1:T + 1], op0=ALU.mult, op1=ALU.add)
                elif name == "kk":
                    w("mk")
                    dve.wait_ge(prep_pool, len(PO) * p + OPEN)
                    ins = ts(kk[:], m2[:, 1, :], q(K_K), None, ALU.mult)
                elif name[:3] == "run":
                    t = int(name[3:])
                    if t == 0:
                        dve.wait_ge(wide_read[KINDS.index("w")], 3 * p + 3 + OPEN)
                    ins = nc.vector.tensor_tensor_scan(run[:, chunk(t)], ones_row[:], sw[:, chunk(t)], 0.0, ALU.mult, ALU.add)
                elif name == "lpr":
                    w(f"run{NT - 1}")
                    ins = tt(sw[:], run[:], sw[:], ALU.subtract)
                elif name == "kmax":
                    dve.wait_ge(wide_read[KINDS.index("ss")], 3 * p + 3 + OPEN)
                    ins = ts(kn[:], kn[:], 1e-12, None, ALU.max)
                elif name[:3] == "rec":
                    t = int(name[3:])
                    w("kmax")
                    part = slice(t * T // RC, (t + 1) * T // RC)
                    ins = nc.vector.reciprocal(kn[:, part], kn[:, part])
                elif name == "kkn":
                    w("kk", f"rec{RC - 1}")
                    ins = tt(kk[:], kk[:], kn[:], ALU.mult)
                elif name == "kap":
                    w("kkn")
                    dve.wait_ge(prep_act, ac(p, "Pp"))
                    ins = tt(kr[:, z, 0, :], kk[:], Pp[:], ALU.mult)
                elif name == "ta":
                    dve.wait_ge(wide_read[KINDS.index("a")], 3 * p + 3 + OPEN)
                    ins = ts(d3[:, 1, :], a[:], -1.0, q(K_A), ALU.add, ALU.mult)
                elif name == "kp":
                    w("ta")
                    ins = stt(out=d3[:, 1, :], in0=d3[:, 1, :], scalar=1.0, in1=m2[:, 1, :], op0=ALU.add, op1=ALU.mult)
                elif name == "rk":
                    w("kp", "mr")
                    ins = stt(out=d3[:, 0, :], in0=m2[:, 0, :], scalar=q(R_K), in1=d3[:, 1, :], op0=ALU.mult, op1=ALU.mult)
                elif name == "rh":
                    dve.wait_ge(prep_act, ac(p, "P"))
                    ins = tt(kr[:, z, 1, :], m2[:, 0, :], P[:], ALU.mult)
                elif name == "pend":
                    ins = nc.vector.tensor_copy(Pend[:, z], P[:, TT - 1::TT])
                ins.then_inc(prep_dve, 1)

            def gn(p, z, k):
                gn_at = {"mean": 0, "sum": 3, "norm": 4, "gate": 6}[k]
                ch = Chain(dve, gn_dve, 8 * (p + 1) + gn_at)
                wide = lambda j: gs[:, j, :].unsqueeze(2).to_broadcast([TT, 2 * NT, RD])
                Yz = Y[:, z]
                if k == "mean":
                    dve.wait_ge(seq_act, 3 * NT * (p + 1) + 6 + OPEN)
                    ch(nc.vector.tensor_reduce(gs[:, 0, :], Yz, AX.X, ALU.add))
                    ch(ts(gs[:, 0, :], gs[:, 0, :], 1.0 / RD, None, ALU.mult))
                    ch(tt(Yz, Yz, wide(0), ALU.subtract))
                elif k == "sum":
                    dve.wait_ge(gn_act, 2 * (p + 1) + 1 + OPEN)
                    ch(nc.vector.tensor_reduce(gs[:, 1, :].rearrange("p (a n) -> p a n", a=2), Yq, AX.X, ALU.add))
                elif k == "norm":
                    dve.wait_ge(gn_act, 2 * (p + 1) + 2 + OPEN)
                    ch(nc.vector.reciprocal(gs[:, 3, :], gs[:, 2, :]))
                    for j in range(2):
                        part = slice(NT * j, NT * (j + 1))
                        last = tt(Yq[:, j], Y[:, z, part], gs[:, 3, part].unsqueeze(2).to_broadcast([TT, NT, RD]), ALU.mult)
                    ch(last)
                else:
                    dve.wait_ge(wide_read[KINDS.index("gn")], 3 * (p + 1) + 3 + OPEN)
                    dve.wait_ge(wide_read[KINDS.index("bs")], 3 * p + 3 + OPEN)
                    dve.wait_ge(wide_read[KINDS.index("g")], 3 * p + 3 + OPEN)
                    ch(tt(yw[:], yw[:], bon[:], ALU.add))
                    ch(tt(yw[:], yw[:], g[:], ALU.mult))

            parts = {"solve": solve, "seq": seq, "wide": wide_piece, "dve": prep, "gn": gn}
            dve.wait_ge(made_pool, ZEROED + OPEN)
            walk(0, PROLOGUE, parts)
            with dve.Fori(0, NF // 2) as i:
                walk(i, ORDER, parts)
            walk(NF // 2 - 1, EPILOGUE, parts)


NG, EG = 4, 8
NE = NG * EG
FF = 512
SLOTS = 128
OVER = 2 * T // (SLOTS + 1)
NBLK = NE + OVER
BIG = 1.0e30


def merge_branches(nc, c):
    with ExitStack() as st:
        sb, ps, sem, begin = scope(nc, st)
        yT = sb("mb_yT", [128, KD, T])
        oT = sb("mb_oT", [128, KD, T])
        o = sb("mb_o", [TT, 2, D])
        rs = sb("mb_rs", [TT, NT * DH])
        ri = sb("mb_ri", [TT, NT * DH])
        sw = sb("mb_sw", [TT, 128])
        w = sb("mb_w", [128, 2, KD, 128])
        gt = sb("mb_gt", [128, 2, T])
        part = sb("mb_part", [128, 2, T])
        bank = ps("mb_bank", [128, 8, 512])
        sw_in = sem("mb_sw_in")
        o_in = [sem(f"mb_o_in{s}") for s in range(2)]
        y_in = sem("mb_y_in")
        w_in = [sem(f"mb_w_in{s}") for s in range(2)]
        g_in = [sem(f"mb_g_in{s}") for s in range(2)]
        rs_done = sem("mb_rs_done")
        vec = sem("mb_vec")
        turned = sem("mb_turned")
        moved = sem("mb_moved")
        product = [sem(f"mb_product{s}") for s in range(2)]
        opened = [sem(f"mb_opened{s}") for s in range(2)]
        gated = [sem(f"mb_gated{s}") for s in range(2)]
        summed = sem("mb_summed")
        block = begin()
        LAMBDA0 = 0.8 - 0.6

        @block.sync
        def _(sp):
            sp.dma_start(sw[:], c.diff_subln_w.to_broadcast([TT, 128])).then_inc(sw_in, 16)
            for t in range(2):
                sp.dma_start(o[:, t, :], c.oD[t]).then_inc(o_in[t], 16)
            sp.dma_start(yT[:], c.yrT.rearrange("f p t -> p f t")).then_inc(y_in, 16)
            with sp.Fori(1, NT // 2) as i:
                for s in range(2):
                    sp.wait_ge(turned, 2 * i + s - 1 + OPEN)
                    sp.dma_start(o[:, s, :], c.oD[bass.ds(2 * i + s, 1)].rearrange("o p d -> (o p) d")).then_inc(o_in[s], 16)
            with sp.Fori(0, KD) as i:
                for s, src in enumerate((c.w_branch_rwkv, c.w_branch_diff)):
                    sp.wait_ge(product[s], i + OPEN)
                    sp.dma_start(w[:, s], src.rearrange("o (k p) f -> p (o k) f", p=128)[:, :, bass.ds(i * 128, 128)]).then_inc(w_in[s], 16)
                    sp.wait_ge(gated[s], i + OPEN)
                    sp.dma_start(gt[:, s, :], c.pT[bass.ds(i + RT + 8 * s, 1)].rearrange("o p t -> (o p) t")).then_inc(g_in[s], 16)

        @block.scalar
        def _(act):
            nc.scalar.activation(rs[:], c.o_ms[:].rearrange("p t h -> p (t h)"), ACT.Sqrt, bias=c.eps[0:TT, :],
                                 scale=1.0 / 128).then_inc(rs_done, 1)
            with act.Fori(0, NT) as i:
                act.wait_ge(turned, i + 1 + OPEN)
                nc.scalar.copy(oT[:, :, bass.ds(i * TT, TT)].rearrange("p (b k) t -> p b k t", b=2),
                               bank[:, 0:2, 0:4 * TT].rearrange("p b (k t) -> p b k t", k=4)).then_inc(moved, 1)
            with act.Fori(0, KD) as i:
                for s in range(2):
                    act.wait_ge(g_in[s], 16 * i + 16 + OPEN)
                    nc.scalar.activation(gt[:, s, :], gt[:, s, :], ACT.Sigmoid).then_inc(opened[s], 1)

        @block.vector
        def _(dve):
            dve.wait_ge(sw_in, 16 + OPEN)
            dve.wait_ge(rs_done, 1 + OPEN)
            ch = Chain(dve, vec)
            ch(nc.vector.tensor_scalar(sw[:], sw[:], 1.0 - LAMBDA0, None, ALU.mult))
            ch(nc.vector.reciprocal(ri[:], rs[:]))
            with dve.Fori(0, NT // 2) as i:
                ch = Chain(dve, vec, 4 * i + 2)
                for s in range(2):
                    dve.wait_ge(o_in[s], 16 * i + 16 + OPEN)
                    o3 = o[:, s, :].rearrange("p (h d) -> p h d", h=DH)
                    ch(nc.vector.tensor_tensor(o3, o3, ri[:, bass.ds((2 * i + s) * DH, DH)].unsqueeze(2).to_broadcast([TT, DH, 128]), ALU.mult))
                    ch(nc.vector.tensor_tensor(o3, o3, sw[:].unsqueeze(1).to_broadcast([TT, DH, 128]), ALU.mult))
            split = lambda x: x.rearrange("p (n t) -> p n t", n=NCOL)
            with dve.Fori(0, KD) as i:
                for s in range(2):
                    dve.wait_ge(product[s], i + 1 + OPEN)
                    dve.wait_ge(opened[s], i + 1 + OPEN)
                    nc.vector.tensor_tensor(split(part[:, s, :]), bank[:, 4 * s:4 * s + 4, 0:CW], split(gt[:, s, :]),
                                            ALU.mult).then_inc(gated[s], 1)
                dve.wait_ge(gated[0], i + 1 + OPEN)
                dve.wait_ge(gated[1], i + 1 + OPEN)
                nc.vector.tensor_tensor(c.mT[:, bass.ds(i, 1), :].rearrange("p o t -> p (o t)"), part[:, 0, :], part[:, 1, :],
                                        ALU.add).then_inc(summed, 1)
                dve.wait_ge(summed, i + 1 + OPEN)

        @block.tensor
        def _(pe):
            with pe.Fori(0, NT // 2) as i:
                for s in range(2):
                    pe.wait_ge(vec, 4 * i + 2 * s + 4 + OPEN)
                    pe.wait_ge(moved, 2 * i + s + OPEN)
                    for k in range(KD):
                        last = nc.tensor.transpose(bank[:, k // 4, (k % 4) * TT:(k % 4 + 1) * TT],
                                                   o[:, s, k * 128:(k + 1) * 128], c.ident[0:TT, 0:TT])
                    last.then_inc(turned, 1)
            pe.wait_ge(moved, NT + OPEN)
            pe.wait_ge(y_in, 16 + OPEN)
            with pe.Fori(0, KD) as i:
                for s, src in enumerate((yT, oT)):
                    pe.wait_ge(w_in[s], 16 * i + 16 + OPEN)
                    pe.wait_ge(gated[s], i + OPEN)
                    for k in range(KD):
                        for n in range(NCOL):
                            last = nc.tensor.matmul(bank[:, 4 * s + n, 0:CW], w[:, s, k, :], src[:, k, n * CW:(n + 1) * CW],
                                                    start=(k == 0), stop=(k == KD - 1))
                    last.then_inc(product[s], 1)


def output_and_route(nc, c):
    NR = NG + NE
    with ExitStack() as st:
        sb, ps, sem, begin = scope(nc, st)
        wo = sb("or_wo", [128, KD, D])
        wr = sb("or_wr", [128, KD, NR])
        n2 = sb("or_n2", [TT, D])
        h = sb("or_h", [TT, 2, D])
        sq = sb("or_sq", [TT, D])
        ms = sb("or_ms", [TT, 2])
        rs = sb("or_rs", [TT, 2])
        ri = sb("or_ri", [TT, 2])
        u = sb("or_u", [TT, 2, D])
        uT = sb("or_uT", [128, 2, KD * TT])
        bank = ps("or_bank", [128, 8, 512])
        w_in = sem("or_w_in")
        h_in = [sem(f"or_h_in{s}") for s in range(2)]
        product = sem("or_product")
        added = sem("or_added")
        squared = sem("or_squared")
        rs_done = sem("or_rs_done")
        vec = sem("or_vec")
        normed = sem("or_normed")
        turned = sem("or_turned")
        moved = sem("or_moved")
        logits = sem("or_logits")
        kept = sem("or_kept")
        h_out = [sem(f"or_h_out{s}") for s in range(2)]
        u_out = [sem(f"or_u_out{s}") for s in range(2)]
        block = begin()

        @block.sync
        def _(sp):
            sp.dma_start(wo[:], c.w_out.rearrange("o (k p) f -> p (o k) f", p=128)).then_inc(w_in, 16)
            sp.dma_start(h[0:META, 0, :], c.meta_tokens).then_inc(h_in[0], 16)
            sp.dma_start(h[META:TT, 0, :], c.x[0, 0:TT - META, :]).then_inc(h_in[0], 16)
            sp.dma_start(h[:, 1, :], c.x[0, TT - META:2 * TT - META, :]).then_inc(h_in[1], 16)
            sp.dma_start(wr[:, :, 0:NG], c.router_group_w.rearrange("o (k p) e -> p (o k) e", p=128)).then_inc(w_in, 16)
            sp.dma_start(wr[:, :, NG:NR], c.router_expert_w.rearrange("o (k p) e -> p (o k) e", p=128)).then_inc(w_in, 16)
            sp.dma_start(n2[:], c.norm2_w.to_broadcast([TT, D])).then_inc(w_in, 16)
            for t in range(NT):
                s, m = t % 2, t // 2
                if t >= 2:
                    sp.wait_ge(normed, t - 1 + OPEN)
                    sp.wait_ge(h_out[s], 16 * m + OPEN)
                    sp.dma_start(h[:, s, :], c.x[0, t * TT - META:(t + 1) * TT - META, :]).then_inc(h_in[s], 16)
                sp.wait_ge(added, t + 1 + OPEN)
                sp.dma_start(c.h2D[t], h[:, s, :]).then_inc(h_out[s], 16)
                sp.wait_ge(normed, t + 1 + OPEN)
                sp.dma_start(c.u2D[t * TT:(t + 1) * TT, :], u[:, s, :]).then_inc(u_out[s], 16)
            for s in range(2):
                sp.wait_ge(h_out[s], 16 * NT // 2 + OPEN)
                sp.wait_ge(u_out[s], 16 * NT // 2 + OPEN)

        @block.tensor
        def _(pe):
            def route(t):
                s = t % 2
                pe.wait_ge(normed, t + 1 + OPEN)
                if t >= 1:
                    pe.wait_ge(moved, t + OPEN)
                for k in range(KD):
                    last = nc.tensor.transpose(bank[:, 4 + k // 4, (k % 4) * TT:(k % 4 + 1) * TT],
                                               u[:, s, k * 128:(k + 1) * 128], c.ident[0:TT, 0:TT])
                last.then_inc(turned, 1)
                pe.wait_ge(moved, t + 1 + OPEN)
                if t >= 1:
                    pe.wait_ge(kept, t + OPEN)
                for k in range(KD):
                    last = nc.tensor.matmul(bank[0:TT, 6, 0:NR], uT[:, s, k * TT:(k + 1) * TT], wr[:, k, :],
                                            start=(k == 0), stop=(k == KD - 1))
                last.then_inc(logits, 1)

            pe.wait_ge(w_in, 64 + OPEN)
            for t in range(NT):
                if t >= 2:
                    pe.wait_ge(added, t - 1 + OPEN)
                for n in range(2):
                    for k in range(KD):
                        last = nc.tensor.matmul(bank[0:TT, 2 * (t % 2) + n, :], c.mT[:, k, t * TT:(t + 1) * TT],
                                                wo[:, k, n * 512:(n + 1) * 512], start=(k == 0), stop=(k == KD - 1))
                last.then_inc(product, 1)
                if t >= 1:
                    route(t - 1)
            route(NT - 1)

        @block.vector
        def _(dve):
            dve.wait_ge(w_in, 64 + OPEN)
            ch = Chain(dve, vec)
            for t in range(NT):
                s = t % 2
                dve.wait_ge(product, t + 1 + OPEN)
                dve.wait_ge(h_in[s], 16 * (t // 2) + (32 if s == 0 else 16) + OPEN)
                nc.vector.tensor_tensor(h[:, s, :].rearrange("p (b n) -> p b n", b=2), bank[0:TT, 2 * s:2 * s + 2, :],
                                        h[:, s, :].rearrange("p (b n) -> p b n", b=2), ALU.add).then_inc(added, 1)
                dve.wait_ge(rs_done, t + 1 + OPEN)
                ch(nc.vector.reciprocal(ri[:, s:s + 1], rs[:, s:s + 1]))
                if t >= 2:
                    dve.wait_ge(turned, t - 1 + OPEN)
                    dve.wait_ge(u_out[s], 16 * (t // 2) + OPEN)
                nc.vector.scalar_tensor_tensor(out=u[:, s, :], in0=h[:, s, :], scalar=ri[:, s:s + 1], in1=n2[:],
                                               op0=ALU.mult, op1=ALU.mult).then_inc(normed, 1)

        @block.scalar
        def _(act):
            def move(t):
                s = t % 2
                act.wait_ge(turned, t + 1 + OPEN)
                nc.scalar.copy(uT[:, s, :].rearrange("p (b n) -> p b n", b=2), bank[:, 4:6, 0:4 * TT]).then_inc(moved, 1)
                act.wait_ge(logits, t + 1 + OPEN)
                nc.scalar.copy(c.logits[:, t, :], bank[0:TT, 6, 0:NR]).then_inc(kept, 1)

            for t in range(NT):
                s = t % 2
                act.wait_ge(added, t + 1 + OPEN)
                nc.scalar.activation(sq[:], h[:, s, :], ACT.Square, accum_out=ms[:, s:s + 1]).then_inc(squared, 1)
                act.wait_ge(squared, t + 1 + OPEN)
                nc.scalar.activation(rs[:, s:s + 1], ms[:, s:s + 1], ACT.Sqrt, bias=c.eps[0:TT, :],
                                     scale=1.0 / D).then_inc(rs_done, 1)
                if t >= 1:
                    move(t - 1)
            move(NT - 1)


def dispatch(nc, c):
    with ExitStack() as st:
        sb, ps, sem, begin = scope(nc, st)
        bias = sb("di_bias", [TT, NG + NE])
        iota = sb("di_iota", [128, NE])
        big = lambda name: sb(name, [TT, NT, NE])
        el, eq, oh1, oh2, O, pre, slot, t1, t2 = (big("di_" + n) for n in ("el", "eq", "oh1", "oh2", "O", "pre", "slot", "t1", "t2"))
        ge, goh = sb("di_ge", [TT, NT, NG]), sb("di_goh", [TT, NT, NG])
        sm = sb("di_small", [TT, 12, NT])
        M_, GSUM, GI, M1, I1, M2, I2, DF, E2, DEN = range(10)
        lt = sb("di_lt", [TT, TT])
        ones = sb("di_ones", [TT, 128])
        thr = sb("di_thr", [128, NE, 8])
        nov = sb("di_nov", [128, 6, NE])
        onesr = sb("di_onesr", [128, NE])
        ob = sb("di_ob", [128, OVER, NE])
        obi = sb("di_obi", [128, 1, OVER])
        of = sb("di_of", [128, 2, OVER])
        tid = sb("di_tid", [TT, NT], I32)
        zero = sb("di_zero", [NBLK, SLOTS], I32)
        sf = sb("di_sf", [TT, 2, NT])
        pR = ps("di_pR", [TT, 512])
        pC = ps("di_pC", [128, 512])
        made = sem("di_made")
        b_in = sem("di_b_in")
        first_in = sem("di_first_in")
        vec = sem("di_vec")
        o_ready = sem("di_o_ready")
        g_exp = sem("di_g_exp")
        shifted = sem("di_shifted")
        e2_exp = sem("di_e2_exp")
        ranked = sem("di_ranked")
        slots_done = sem("di_slots_done")
        cleared = sem("di_cleared", 0)
        scattered = [sem(f"di_scattered{j}", 0) for j in range(2)]
        block = begin()

        @block.sync
        def _(sp):
            sp.dma_start(bias[:, 0:NG], c.router_group_b.to_broadcast([TT, NG])).then_inc(b_in, 16)
            sp.dma_start(bias[:, NG:], c.router_expert_b.to_broadcast([TT, NE])).then_inc(b_in, 16)
            for s in range(2):
                for dst, src in zip((c.wgu[:, s, 0], c.wgu[:, s, 1], c.wd[:, s]), expert_weights(c, s)):
                    sp.dma_start(dst, src).then_inc(first_in, 16)
            sp.wait_ge(first_in, 96 + OPEN)

        @block.gpsimd
        def _(pool):
            nc.gpsimd.iota(iota[:], pattern=[[1, NE]], base=0, channel_multiplier=0,
                           allow_small_or_imprecise_dtypes=True).then_inc(made, 1)
            nc.gpsimd.iota(thr[:], pattern=[[0, NE], [SLOTS, 8]], base=SLOTS, channel_multiplier=0,
                           allow_small_or_imprecise_dtypes=True).then_inc(made, 1)
            nc.gpsimd.iota(obi[:], pattern=[[0, 1], [1, OVER]], base=0, channel_multiplier=0,
                           allow_small_or_imprecise_dtypes=True).then_inc(made, 1)
            nc.gpsimd.iota(tid[:], pattern=[[TT, NT]], base=0, channel_multiplier=1).then_inc(made, 1)
            nc.gpsimd.memset(ones[:], 1.0).then_inc(made, 1)
            nc.gpsimd.memset(onesr[:], 1.0).then_inc(made, 1)
            nc.gpsimd.memset(zero[:], 0).then_inc(made, 1)
            nc.gpsimd.memset(lt[:], 1.0).then_inc(made, 1)
            pool.wait_ge(made, 8 + OPEN)
            nc.gpsimd.affine_select(out=lt[:], in_=lt[:], compare_op=ALU.is_gt, fill=0.0, base=0,
                                    pattern=[[1, TT]], channel_multiplier=-1).then_inc(made, 1)
            pool.dma_start(c.slotD.rearrange("(b s) o -> b (s o)", s=SLOTS), zero[:]).then_inc(cleared, 16)
            pool.wait_ge(cleared, 16)
            pool.wait_ge(slots_done, 2 + OPEN)
            for t in range(NT):
                for j in range(2):
                    if t >= 1:
                        pool.wait_ge(scattered[j], 16 * t)
                    pool.indirect_dma_start(c.slotD, bass.IndirectOffsetOnAxis(ap=c.sidx[:, j, t:t + 1], axis=0),
                                            tid[:, t:t + 1], None).then_inc(scattered[j], 16)
            for j in range(2):
                pool.wait_ge(scattered[j], 16 * NT)

        @block.scalar
        def _(act):
            act.wait_ge(shifted, 1 + OPEN)
            nc.scalar.activation(ge[:], ge[:], ACT.Exp).then_inc(g_exp, 1)
            act.wait_ge(shifted, 2 + OPEN)
            nc.scalar.activation(sm[:, E2, :], sm[:, DF, :], ACT.Exp).then_inc(e2_exp, 1)

        @block.tensor
        def _(pe):
            pe.wait_ge(o_ready, 1 + OPEN)
            pe.wait_ge(made, 9 + OPEN)
            flat = lambda x: x.rearrange("p t e -> p (t e)")
            nc.tensor.matmul(pR[:, 0:NT * NE], lt[:], flat(O[:]), start=True, stop=False)
            nc.tensor.matmul(pR[:, 0:NT * NE], ones[:, 0:TT], flat(pre[:]), start=False, stop=True)
            nc.tensor.matmul(pC[:, 0:NE], ones[:], O[:, NT - 1, :], start=True, stop=False)
            nc.tensor.matmul(pC[:, 0:NE], ones[:], pre[:, NT - 1, :], start=False, stop=True).then_inc(ranked, 1)

        @block.vector
        def _(dve):
            tt, ts, red = nc.vector.tensor_tensor, nc.vector.tensor_scalar, nc.vector.tensor_reduce
            ch = Chain(dve, vec)
            over_g = lambda x: x.unsqueeze(2).to_broadcast([TT, NT, NG])
            over_e = lambda x: x.unsqueeze(2).to_broadcast([TT, NT, NE])
            iot = lambda n: iota[0:TT, 0:n].unsqueeze(1).to_broadcast([TT, NT, n])
            r = lambda k: sm[:, k, :]
            dve.wait_ge(made, 9 + OPEN)
            dve.wait_ge(b_in, 32 + OPEN)

            def first_max(vals, n, m, idx, oh, over):
                ch(red(r(m), vals, AX.X, ALU.max))
                ch(tt(oh, vals, over(r(m)), ALU.is_lt))
                ch(nc.vector.scalar_tensor_tensor(out=oh, in0=oh, scalar=1000.0, in1=iot(n), op0=ALU.mult, op1=ALU.add))
                ch(red(r(idx), oh, AX.X, ALU.min))
                ch(tt(oh, iot(n), over(r(idx)), ALU.is_equal))

            ch(tt(c.logits[:], c.logits[:], bias[:].unsqueeze(1).to_broadcast([TT, NT, NG + NE]), ALU.add))
            gl = c.logits[:, :, 0:NG]
            first_max(gl, NG, M_, GI, goh[:], over_g)
            tt(ge[:], gl, over_g(r(M_)), ALU.subtract).then_inc(shifted, 1)
            ch(ts(goh[:], goh[:], -1.0, BIG, ALU.add, ALU.mult))
            ch(tt(el[:].rearrange("p t (g e) -> p t g e", g=NG), c.logits[:, :, NG:].rearrange("p t (g e) -> p t g e", g=NG),
                  goh[:].unsqueeze(3).to_broadcast([TT, NT, NG, EG]), ALU.add))
            first_max(el[:], NE, M1, I1, oh1[:], over_e)
            ch(nc.vector.scalar_tensor_tensor(out=eq[:], in0=oh1[:], scalar=-3 * BIG, in1=el[:], op0=ALU.mult, op1=ALU.add))
            first_max(eq[:], NE, M2, I2, oh2[:], over_e)
            tt(r(DF), r(M2), r(M1), ALU.subtract).then_inc(shifted, 1)
            ch(tt(O[:], oh1[:], oh2[:], ALU.add))
            ch(nc.vector.memset(pre[:, 0, :], 0.0))
            for t in range(1, NT):
                ch(tt(pre[:, t, :], pre[:, t - 1, :], O[:, t - 1, :], ALU.add))
            dve.sem_inc(o_ready, 1)
            dve.wait_ge(g_exp, 1 + OPEN)
            ch(red(r(GSUM), ge[:], AX.X, ALU.add))
            dve.wait_ge(e2_exp, 1 + OPEN)
            ch(ts(r(DEN), r(E2), 1.0, None, ALU.add))
            ch(tt(r(DEN), r(DEN), r(GSUM), ALU.mult))
            ch(nc.vector.reciprocal(c.gate[:, 0, :], r(DEN)))
            ch(tt(c.gate[:, 1, :], c.gate[:, 0, :], r(E2), ALU.mult))
            dve.wait_ge(ranked, 1 + OPEN)
            CNT, N_, INC, B1, B2, DB = range(6)
            v = lambda k: nov[:, k, :]
            ch(nc.vector.tensor_copy(v(CNT), pC[:, 0:NE]))
            ch(tt(thr[:], thr[:], v(CNT).unsqueeze(2).to_broadcast([128, NE, 8]), ALU.is_lt))
            ch(red(v(N_), thr[:], AX.X, ALU.add))
            ch(nc.vector.tensor_tensor_scan(v(INC), onesr[:], v(N_), 0.0, ALU.mult, ALU.add))
            ch(ts(v(B1), iota[:], float(SLOTS), None, ALU.mult))
            ch(tt(v(B2), v(INC), v(N_), ALU.subtract))
            ch(ts(v(B2), v(B2), float(SLOTS), float((NE - 1) * SLOTS), ALU.mult, ALU.add))
            ch(tt(v(DB), v(B2), v(B1), ALU.subtract))
            bc = lambda k: nov[0:TT, k, :].unsqueeze(1).to_broadcast([TT, NT, NE])
            ch(nc.vector.tensor_copy(slot[:].rearrange("p t e -> p (t e)"), pR[:, 0:NT * NE]))
            ch(ts(t1[:], slot[:], float(SLOTS), None, ALU.is_ge))
            ch(tt(t1[:], t1[:], bc(DB), ALU.mult))
            ch(tt(slot[:], slot[:], bc(B1), ALU.add))
            ch(tt(slot[:], slot[:], t1[:], ALU.add))
            for j, oh in enumerate((oh1, oh2)):
                ch(tt(t2[:], slot[:], oh[:], ALU.mult))
                ch(red(sf[:, j, :], t2[:], AX.X, ALU.add))
                nc.vector.tensor_copy(c.sidx[:, j, :], sf[:, j, :]).then_inc(slots_done, 1)
            ch(tt(ob[:], nov[:, INC, :].unsqueeze(1).to_broadcast([128, OVER, NE]),
                  obi[:, 0, :].unsqueeze(2).to_broadcast([128, OVER, NE]), ALU.is_le))
            ch(red(of[:, 0, :], ob[:], AX.X, ALU.add))
            ch(ts(of[:, 1, :], of[:, 0, :], float(NE), None, ALU.is_lt))
            ch(ts(of[:, 0, :], of[:, 0, :], float(NE - 1), None, ALU.min))
            ch(nc.vector.tensor_copy(c.over[:], of[0:1, :, :]))


def expert_weights(c, e):
    return [w.rearrange("o e (p k) f -> (o e) p k f", k=k)[bass.ds(e, 1)].rearrange("o p k f -> (o p) k f")
            for w, k in ((c.expert_w_gate, KD), (c.expert_w_up, KD), (c.expert_w_down, FF // 128))]


def experts(nc, c):
    with ExitStack() as st:
        sb, ps, sem, begin = scope(nc, st)
        wgu, wd = c.wgu, c.wd
        idx = sb("ex_idx", [SLOTS, 2], U32)
        x = sb("ex_x", [SLOTS, 2, D])
        xT = sb("ex_xT", [128, 2, KD, SLOTS])
        sg = sb("ex_sg", [SLOTS, FF])
        hid = sb("ex_hid", [SLOTS, FF])
        hT = sb("ex_hT", [128, FF // 128, SLOTS])
        y = sb("ex_y", [SLOTS, 2, D])
        bank = ps("ex_bank", [128, 8, 512])
        idx_in = [sem(f"ex_idx_in{s}", 0) for s in range(2)]
        gathered = [sem(f"ex_gathered{s}", 0) for s in range(2)]
        wgu_in = [[sem(f"ex_w{j}_in{s}") for s in range(2)] for j in "gu"]
        wd_in = [sem(f"ex_wd_in{s}") for s in range(2)]
        asked, over_stored = sem("ex_asked"), sem("ex_over_stored")
        x_turned, x_moved = sem("ex_x_turned"), sem("ex_x_moved")
        gate_done, up_done, opened, silu, mixed = sem("ex_gate_done"), sem("ex_up_done"), sem("ex_opened"), sem("ex_silu"), sem("ex_mixed")
        h_turned, h_moved = sem("ex_h_turned"), sem("ex_h_moved")
        down = sem("ex_down")
        y_moved = [sem(f"ex_y_moved{s}") for s in range(2)]
        y_out = [sem(f"ex_y_out{s}") for s in range(2)]
        block = begin()
        FK = FF // 128

        GATE_BANK = (2, 7)
        UP_BANK = 3

        def load_in(sp, s, e, j):
            sp.dma_start(wgu[:, s, j], expert_weights(c, e)[j]).then_inc(wgu_in[j][s], 16)

        def load_down(sp, s, e):
            sp.dma_start(wd[:, s], expert_weights(c, e)[2]).then_inc(wd_in[s], 16)

        @block.sync
        def _(sp):
            with sp.Fori(0, NE // 2 - 1) as i:
                for s in range(2):
                    n = 2 * i + s
                    sp.wait_ge(gate_done, n + 1 + OPEN)
                    load_in(sp, s, n + 2, 0)
                    sp.wait_ge(up_done, n + 1 + OPEN)
                    load_in(sp, s, n + 2, 1)
                    sp.wait_ge(down, n + 1 + OPEN)
                    load_down(sp, s, n + 2)
            expert = sp.alloc_register("ex_sp_expert")
            used = sp.alloc_register("ex_sp_used")
            with sp.Fori(0, OVER) as n:
                sp.reg_load(used, c.over[0:1, 1, bass.ds(n, 1)])
                with sp.If_ne(used, 0):
                    sp.reg_load(expert, c.over[0:1, 0, bass.ds(n, 1)])
                    sp.wait_ge(down, n + NE + OPEN)
                    e = sp.snap(expert, min_val=0, max_val=NE - 1)
                    load_in(sp, 0, e, 0)
                    load_in(sp, 0, e, 1)
                    load_down(sp, 0, e)

        @block.gpsimd
        def _(pool):
            def gather(s, n, times):
                pool.dma_start(idx[:, s:s + 1], c.slotD[bass.ds(n * SLOTS, SLOTS), :].bitcast(U32)).then_inc(idx_in[s], 16)
                pool.wait_ge(idx_in[s], 16 * times + 16)
                pool.sem_inc(asked, 1)
                pool.indirect_dma_start(x[:, s, :], None, c.u2D, bass.IndirectOffsetOnAxis(ap=idx[:, s:s + 1], axis=0)).then_inc(gathered[s], 16)

            with pool.Fori(0, NE // 2) as i:
                for s in range(2):
                    pool.wait_ge(x_turned, 2 * i + OPEN)
                    gather(s, 2 * i + s, i)
            used = pool.alloc_register("ex_pool_used")
            with pool.Fori(0, OVER) as n:
                pool.reg_load(used, c.over[0:1, 1, bass.ds(n, 1)])
                with pool.If_ne(used, 0):
                    pool.wait_ge(x_turned, n + NE + OPEN)
                    gather(0, n + NE, n + NE // 2)

        def turn_x(pe, s, n, times):
            pe.wait_ge(gathered[s], 16 * times + 16)
            pe.wait_ge(x_moved, n + OPEN)
            for k in range(KD):
                last = nc.tensor.transpose(bank[:, k // 4, (k % 4) * 128:(k % 4 + 1) * 128], x[:, s, k::KD], c.ident[:])
            last.then_inc(x_turned, 1)

        def gate(pe, s, n, times):
            pe.wait_ge(x_moved, n + 1 + OPEN)
            pe.wait_ge(wgu_in[0][s], 16 * times + OPEN)
            pe.wait_ge(mixed, n - 1 + OPEN)
            for k in range(KD):
                last = nc.tensor.matmul(bank[:, GATE_BANK[s], :], xT[:, s, k, :], wgu[:, s, 0, k, :],
                                        start=(k == 0), stop=(k == KD - 1))
            last.then_inc(gate_done, 1)

        def up(pe, s, n, times):
            pe.wait_ge(wgu_in[1][s], 16 * times + OPEN)
            pe.wait_ge(mixed, n + OPEN)
            for k in range(KD):
                last = nc.tensor.matmul(bank[:, UP_BANK, :], xT[:, s, k, :], wgu[:, s, 1, k, :],
                                        start=(k == 0), stop=(k == KD - 1))
            last.then_inc(up_done, 1)

        def turn_h(pe, s, n, times):
            pe.wait_ge(mixed, n + 1 + OPEN)
            for k in range(FK):
                last = nc.tensor.transpose(bank[:, 4, k * 128:(k + 1) * 128], hid[:, k::FK], c.ident[:])
            last.then_inc(h_turned, 1)

        def project(pe, s, n, times):
            pe.wait_ge(h_moved, n + 1 + OPEN)
            pe.wait_ge(wd_in[s], 16 * times + OPEN)
            for o in range(2):
                pe.wait_ge(y_moved[o], n + OPEN)
                for k in range(FK):
                    last = nc.tensor.matmul(bank[:, 5 + o, :], hT[:, k, :], wd[:, s, k, o * 512:(o + 1) * 512],
                                            start=(k == 0), stop=(k == FK - 1))
            last.then_inc(down, 1)

        @block.tensor
        def _(pe):
            turn_x(pe, 0, 0, 0)
            turn_x(pe, 1, 1, 0)
            gate(pe, 0, 0, 0)
            up(pe, 0, 0, 0)
            with pe.Fori(0, NE // 2 - 1) as i:
                for s in range(2):
                    n = 2 * i + s
                    gate(pe, 1 - s, n + 1, i + s)
                    turn_h(pe, s, n, i)
                    turn_x(pe, s, n + 2, i + 1)
                    project(pe, s, n, i)
                    up(pe, 1 - s, n + 1, i + s)
            i = NE // 2 - 1
            gate(pe, 1, NE - 1, i)
            turn_h(pe, 0, NE - 2, i)
            project(pe, 0, NE - 2, i)
            up(pe, 1, NE - 1, i)
            turn_h(pe, 1, NE - 1, i)
            project(pe, 1, NE - 1, i)
            used = pe.alloc_register("ex_pe_used")
            with pe.Fori(0, OVER) as n:
                pe.reg_load(used, c.over[0:1, 1, bass.ds(n, 1)])
                with pe.If_ne(used, 0):
                    for step in (turn_x, gate, up, turn_h, project):
                        step(pe, 0, n + NE, n + NE // 2)

        def move_x(act, s, n):
            act.wait_ge(x_turned, n + 1 + OPEN)
            nc.scalar.copy(xT[:, s].rearrange("p (b k) t -> p b (k t)", b=2), bank[:, 0:2, :]).then_inc(x_moved, 1)

        def open_gate(act, s, n):
            act.wait_ge(gate_done, n + 1 + OPEN)
            act.wait_ge(mixed, n + OPEN)
            nc.scalar.activation(sg[:], bank[:, GATE_BANK[s], :], ACT.Sigmoid).then_inc(opened, 1)

        def move_h(act, n):
            act.wait_ge(h_turned, n + 1 + OPEN)
            nc.scalar.copy(hT[:].rearrange("p k t -> p (k t)"), bank[:, 4, :]).then_inc(h_moved, 1)

        def move_y(eng, s, n, times, o):
            eng.wait_ge(down, n + 1 + OPEN)
            eng.wait_ge(y_out[s], 16 * times + OPEN)
            copy = nc.scalar.copy if o == 0 else nc.vector.tensor_copy
            copy(y[:, s, o * 512:(o + 1) * 512], bank[:, 5 + o, :]).then_inc(y_moved[o], 1)

        def store_y(act, s, n):
            for o in range(2):
                act.wait_ge(y_moved[o], n + 1 + OPEN)
            act.dma_start(c.yD[bass.ds(n * SLOTS, SLOTS), :], y[:, s, :]).then_inc(y_out[s], 16)

        @block.scalar
        def _(act):
            move_x(act, 0, 0)
            move_x(act, 1, 1)
            open_gate(act, 0, 0)
            with act.Fori(0, NE // 2 - 1) as i:
                for s in range(2):
                    n = 2 * i + s
                    open_gate(act, 1 - s, n + 1)
                    move_h(act, n)
                    move_x(act, s, n + 2)
                    move_y(act, s, n, i, 0)
                    store_y(act, s, n)
            i = NE // 2 - 1
            open_gate(act, 1, NE - 1)
            for s in range(2):
                n = 2 * i + s
                move_h(act, n)
                move_y(act, s, n, i, 0)
                store_y(act, s, n)
            used = act.alloc_register("ex_act_used")
            with act.Fori(0, OVER) as n:
                act.reg_load(used, c.over[0:1, 1, bass.ds(n, 1)])
                with act.If_ne(used, 0):
                    move_x(act, 0, n + NE)
                    open_gate(act, 0, n + NE)
                    move_h(act, n + NE)
                    move_y(act, 0, n + NE, n + NE // 2, 0)
                    store_y(act, 0, n + NE)
                    act.wait_ge(y_out[0], 16 * (n + NE // 2 + 1) + OPEN)
                    act.sem_inc(over_stored, 1)
            for s in range(2):
                act.wait_ge(y_out[s], 16 * NE // 2 + OPEN)

        def mix(dve, s, n):
            dve.wait_ge(opened, n + 1 + OPEN)
            dve.wait_ge(h_turned, n + OPEN)
            nc.vector.tensor_tensor(hid[:], bank[:, GATE_BANK[s], :], sg[:], ALU.mult).then_inc(silu, 1)
            dve.wait_ge(silu, n + 1 + OPEN)
            dve.wait_ge(up_done, n + 1 + OPEN)
            nc.vector.tensor_tensor(hid[:], bank[:, UP_BANK, :], hid[:], ALU.mult).then_inc(mixed, 1)

        @block.vector
        def _(dve):
            mix(dve, 0, 0)
            with dve.Fori(0, NE // 2 - 1) as i:
                for s in range(2):
                    n = 2 * i + s
                    move_y(dve, s, n, i, 1)
                    mix(dve, 1 - s, n + 1)
            i = NE // 2 - 1
            move_y(dve, 0, NE - 2, i, 1)
            mix(dve, 1, NE - 1)
            move_y(dve, 1, NE - 1, i, 1)
            used = dve.alloc_register("ex_dve_used")
            with dve.Fori(0, OVER) as n:
                dve.reg_load(used, c.over[0:1, 1, bass.ds(n, 1)])
                with dve.If_ne(used, 0):
                    mix(dve, 0, n + NE)
                    move_y(dve, 0, n + NE, n + NE // 2, 1)


def combine(nc, c):
    with ExitStack() as st:
        sb, ps, sem, begin = scope(nc, st)
        h = sb("co_h", [TT, 2, D])
        y = sb("co_y", [TT, 2, 2, D])
        h_in = [sem(f"co_h_in{s}") for s in range(2)]
        y_in = [[sem(f"co_y_in{s}{j}", 0) for j in range(2)] for s in range(2)]
        half = sem("co_half")
        summed = sem("co_summed")
        out = [sem(f"co_out{s}") for s in range(2)]
        block = begin()

        @block.sync
        def _(sp):
            for t in range(NT):
                if t >= 2:
                    sp.wait_ge(out[t % 2], 16 * (t // 2) + OPEN)
                sp.dma_start(h[:, t % 2, :], c.h2D[t]).then_inc(h_in[t % 2], 16)

        @block.gpsimd
        def _(pool):
            for t in range(NT):
                if t >= 2:
                    pool.wait_ge(summed, t - 1 + OPEN)
                for j in range(2):
                    pool.indirect_dma_start(y[:, t % 2, j, :], None, c.yD,
                                            bass.IndirectOffsetOnAxis(ap=c.sidx[:, j, t:t + 1], axis=0)).then_inc(y_in[t % 2][j], 16)

        @block.vector
        def _(dve):
            for t in range(NT):
                s = t % 2
                dve.wait_ge(h_in[s], 16 * (t // 2) + 16 + OPEN)
                dve.wait_ge(y_in[s][0], 16 * (t // 2) + 16)
                nc.vector.scalar_tensor_tensor(out=h[:, s, :], in0=y[:, s, 0, :], scalar=c.gate[:, 0, t:t + 1], in1=h[:, s, :],
                                               op0=ALU.mult, op1=ALU.add).then_inc(half, 1)
                dve.wait_ge(half, t + 1 + OPEN)
                dve.wait_ge(y_in[s][1], 16 * (t // 2) + 16)
                nc.vector.scalar_tensor_tensor(out=h[:, s, :], in0=y[:, s, 1, :], scalar=c.gate[:, 1, t:t + 1], in1=h[:, s, :],
                                               op0=ALU.mult, op1=ALU.add).then_inc(summed, 1)

        @block.scalar
        def _(act):
            for t in range(NT):
                act.wait_ge(summed, t + 1 + OPEN)
                if t == 0:
                    act.dma_start(c.out[0, 0:TT - META, :], h[META:TT, 0, :]).then_inc(out[0], 16)
                else:
                    act.dma_start(c.out[0, t * TT - META:(t + 1) * TT - META, :], h[:, t % 2, :]).then_inc(out[t % 2], 16)
            for s in range(2):
                act.wait_ge(out[s], 16 * NT // 2 + OPEN)


def build(nc, ins, out, cst, upto=99, skip_at=False):
    c = Shared()
    c.x = ins["x"]
    c.meta_tokens = ins["meta_tokens"]
    c.norm1_w = ins["norm1_w"]
    c.w_in = ins["w_in"]
    c.rwkv_mu = ins["rwkv_mu"]
    c.rwkv_w0 = ins["rwkv_w0"]
    c.rwkv_w2 = ins["rwkv_w2"]
    c.rwkv_a0 = ins["rwkv_a0"]
    c.rwkv_a2 = ins["rwkv_a2"]
    c.rwkv_g2 = ins["rwkv_g2"]
    c.rwkv_k_k = ins["rwkv_k_k"]
    c.rwkv_k_a = ins["rwkv_k_a"]
    c.rwkv_r_k = ins["rwkv_r_k"]
    c.rwkv_ln_w = ins["rwkv_ln_w"]
    c.rwkv_ln_b = ins["rwkv_ln_b"]
    c.q_norm_w = ins["q_norm_w"]
    c.k_norm_w = ins["k_norm_w"]
    c.lambda_q1 = ins["lambda_q1"]
    c.lambda_k1 = ins["lambda_k1"]
    c.lambda_q2 = ins["lambda_q2"]
    c.lambda_k2 = ins["lambda_k2"]
    c.diff_subln_w = ins["diff_subln_w"]
    c.w_branch_rwkv = ins["w_branch_rwkv"]
    c.w_branch_diff = ins["w_branch_diff"]
    c.w_out = ins["w_out"]
    c.norm2_w = ins["norm2_w"]
    c.router_group_w = ins["router_group_w"]
    c.router_group_b = ins["router_group_b"]
    c.router_expert_w = ins["router_expert_w"]
    c.router_expert_b = ins["router_expert_b"]
    c.expert_w_gate = ins["expert_w_gate"]
    c.expert_w_up = ins["expert_w_up"]
    c.expert_w_down = ins["expert_w_down"]
    c.rope_cos = cst["rope_cos"]
    c.rope_sin = cst["rope_sin"]
    c.mask4 = cst["mask4"]
    c.maskn = cst["maskn"]
    c.out = out
    dram = lambda name, shape, dt=F32: nc.dram_tensor(name, shape, dt, kind="Internal").ap()
    c.qkT = dram("s_qkT", [2 * DH, 128, T])
    c.vD = dram("s_v", [NT, TT, D])
    c.yrT = dram("s_yrT", [KD, 128, T])
    c.h2D = dram("s_h2", [NT, TT, D])
    c.u2D = dram("s_u2", [T, D])
    c.slotD = dram("s_slot", [NBLK * SLOTS, 1], I32)
    c.yD = dram("s_y", [NBLK * SLOTS, D])
    c.oD = dram("s_o", [NT, TT, D])
    c.pT = dram("s_pT", [RT + GT, 128, T])
    with ExitStack() as st:
        sb = lambda name, shape, dt=F32: st.enter_context(nc.sbuf_tensor(name, shape, dt))
        c.ident = sb("ident", [128, 128])
        c.eps = sb("eps", [128, 1])
        c.logits = sb("logits", [TT, NT, NG + NE])
        c.gate = sb("gate", [TT, 2, NT])
        c.sidx = sb("sidx", [TT, 2, NT], U32)
        c.over = sb("over", [1, 2, OVER], I32)
        c.o_ms = sb("o_ms", [TT, NT, DH])
        constants(nc, c)
        with ExitStack() as st2:
            c.uH = st2.enter_context(nc.sbuf_tensor("uH", [128, KD, T], F32R))
            c.uL = st2.enter_context(nc.sbuf_tensor("uL", [128, KD, T], F32R))
            norm1(nc, c)
            if upto >= 2:
                project_features(nc, c)
            project_heads(nc, c)
        if upto >= 3 and not skip_at:
            attention(nc, c)
        if upto >= 4:
            rwkv(nc, c)
        if upto >= 5:
            with ExitStack() as st2:
                c.mT = st2.enter_context(nc.sbuf_tensor("mT", [128, KD, T], F32))
                merge_branches(nc, c)
                if upto >= 6:
                    output_and_route(nc, c)
            with ExitStack() as st2:
                c.wgu = st2.enter_context(nc.sbuf_tensor("wgu", [128, 2, 2, KD, FF], F32))
                c.wd = st2.enter_context(nc.sbuf_tensor("wd", [128, 2, FF // 128, D], F32))
                if upto >= 7:
                    dispatch(nc, c)
                if upto >= 8:
                    experts(nc, c)
            if upto >= 9:
                combine(nc, c)


def rope_tables():
    half = ROPE // 2
    freq = np.exp(np.float32(-math.log(THETA)) * np.arange(half, dtype=np.float32) * np.float32(2.0) / np.float32(ROPE))
    ang = np.arange(T, dtype=np.float32)[:, None] * freq[None, :].astype(np.float32)
    cos, sin = np.cos(ang), np.sin(ang)
    tiles = lambda a: np.ascontiguousarray(a.reshape(NT, TT, ROPE).transpose(1, 0, 2).astype(np.float32))
    return tiles(np.concatenate([cos, cos], 1)), tiles(np.concatenate([-sin, sin], 1))


def chunk_masks():
    p, f = np.arange(TT)[:, None], np.arange(TT)[None, :]
    same = p // SUB == f // SUB
    mask4 = np.stack([-1.0 * (same & (p < f)), 1.0 * (p <= f), 1.0 * (p < f), 1.0 * (p <= f)], 1)
    maskn = np.stack([-1.0 * (same & (p > f)), -1.0 * (~same & (p > f))], 1)
    return mask4.astype(np.float32), maskn.astype(np.float32)


_CONST = dict(zip(("rope_cos", "rope_sin", "mask4", "maskn"), rope_tables() + chunk_masks()))


def kernel(**inputs):
    import concourse.bacc as bacc
    from concourse.bass_utils import run_bass_kernel_spmd
    nc = bacc.Bacc("TRN2", target_bir_lowering=False, num_devices=1)
    arrays, ins = {}, {}
    for name, a in inputs.items():
        a = np.ascontiguousarray(a)
        arrays["in_" + name] = a
        ins[name] = nc.dram_tensor("in_" + name, a.shape, mybir.dt.from_np(a.dtype), kind="ExternalInput").ap()
    cst = {}
    for name, a in _CONST.items():
        arrays["const_" + name] = a
        cst[name] = nc.dram_tensor("const_" + name, a.shape, mybir.dt.from_np(a.dtype), kind="ExternalInput").ap()
    out = nc.dram_tensor("out_0", [1, SEQ, D], F32, kind="ExternalOutput").ap()
    build(nc, ins, out, cst)
    r = run_bass_kernel_spmd(nc, [arrays], core_ids=[0])
    return r.results[0]["out_0"]
```
